# Optimizing a Trainium2 kernel written in Bass

```python
import jax, jax.numpy as jnp
from jax import lax
import numpy as np

D_MODEL = 1024
BATCH = 1
SEQ = 128
DEPTH = 2
DEC_BATCH = 1
DEC_SEQ = 256
PAST_LEN = 128

GRID_W = 64
HEAD_DIM = 64
NA_HEADS = 8
NA_WIN_R = 8
NA_WIN_C = 16
NA_QC = 16
NA_KC = NA_QC + NA_WIN_C
GQA_HEADS = 8
GQA_KV_HEADS = 2
QKV_WIDTH = 3 * NA_HEADS * HEAD_DIM + (GQA_HEADS + 2 * GQA_KV_HEADS) * HEAD_DIM
ATTN_OUT_WIDTH = (NA_HEADS + GQA_HEADS) * HEAD_DIM
ROPE_BASE = 10000.0
Q_BLOCK = 128
SGU_CHUNK = 128
SGU_GROUPS = 8
SGU_WIDTH = 2 * D_MODEL
FFN_HIDDEN = 2816
N_MOD = 9
N_ATTN_LAYERS = (DEPTH + 1) // 2
N_SGU_LAYERS = DEPTH // 2
EPS = 1e-6
NEG_INF = -1e30

kernel_name = 'hybrid_na_gqa_gmlp_diffusion_step'

def rms_norm(x, g):
    xf = x.astype(jnp.float32)
    y = xf * lax.rsqrt(jnp.mean(xf * xf, axis=-1, keepdims=True) + EPS)
    return (y * g.astype(jnp.float32)).astype(x.dtype)

def modulation(cond, w, b):
    m = jax.nn.silu(cond) @ w + b
    return m.reshape(cond.shape[0], 1, N_MOD, D_MODEL)

def adaln_input(h, mod, j, g):
    return rms_norm(h, g) * (1 + mod[:, :, 3 * j + 1]) + mod[:, :, 3 * j]

def adaln_gate(mod, j):
    return mod[:, :, 3 * j + 2]

def swiglu(x, w_gu, w_down):
    gate, up = jnp.split(x @ w_gu, 2, axis=-1)
    return (jax.nn.silu(gate) * up) @ w_down

def axial_rope(x):
    T, D = x.shape[1], x.shape[3]
    t = jnp.arange(T)
    half = D // 2
    freqs = ROPE_BASE ** (-jnp.arange(0, half, 2, dtype=jnp.float32) / half)

    def rotate(xa, pos):
        ang = pos.astype(jnp.float32)[:, None] * freqs[None, :]
        cos = jnp.cos(ang)[None, :, None, :]
        sin = jnp.sin(ang)[None, :, None, :]
        x1, x2 = jnp.split(xa.astype(jnp.float32), 2, axis=-1)
        return jnp.concatenate([x1 * cos - x2 * sin, x1 * sin + x2 * cos], axis=-1)

    out = jnp.concatenate([rotate(x[..., :half], t // GRID_W), rotate(x[..., half:], t % GRID_W)], axis=-1)
    return out.astype(x.dtype)

def attn_project(xn, w_in, na_q_g, na_k_g, gqa_q_g, gqa_k_g):
    B, S, _ = xn.shape
    na_w = NA_HEADS * HEAD_DIM
    q_w = GQA_HEADS * HEAD_DIM
    kv_w = GQA_KV_HEADS * HEAD_DIM
    splits = [na_w, 2 * na_w, 3 * na_w, 3 * na_w + q_w, 3 * na_w + q_w + kv_w]
    qa, ka, va, qb, kb, vb = jnp.split(xn @ w_in, splits, axis=-1)
    heads = lambda t: t.reshape(B, S, -1, HEAD_DIM)
    return (rms_norm(heads(qa), na_q_g), rms_norm(heads(ka), na_k_g), heads(va),
            rms_norm(heads(qb), gqa_q_g), rms_norm(heads(kb), gqa_k_g), heads(vb))

def dense_attention(q, k, v):
    B, S, Hq, D = q.shape
    Hk = k.shape[2]
    G = Hq // Hk
    nb = S // Q_BLOCK
    qb = (q * D ** -0.5).reshape(B, nb, Q_BLOCK, Hk, G, D).transpose(1, 0, 2, 3, 4, 5)

    def block(qblk):
        s = jnp.einsum('bqkgd,bskd->bkgqs', qblk, k).astype(jnp.float32)
        p = jax.nn.softmax(s, axis=-1).astype(v.dtype)
        return jnp.einsum('bkgqs,bskd->bqkgd', p, v)

    o = lax.map(block, qb)
    return o.transpose(1, 0, 2, 3, 4, 5).reshape(B, S, Hq, D)

def neighbourhood_attention(q, k, v, ctx_k, ctx_v, rpb):
    B, T, H, D = q.shape
    rows = T // GRID_W
    wr = min(NA_WIN_R, rows)
    ncb = GRID_W // NA_QC
    r = jnp.arange(rows)
    row_idx = jnp.clip(r - wr // 2, 0, rows - wr)[:, None] + jnp.arange(wr)[None, :]
    cb = jnp.arange(ncb)
    col_idx = jnp.clip(cb * NA_QC - NA_WIN_C // 2, 0, GRID_W - NA_KC)[:, None] + jnp.arange(NA_KC)[None, :]
    q_col = cb[:, None] * NA_QC + jnp.arange(NA_QC)[None, :]
    win_start = jnp.clip(q_col - NA_WIN_C // 2, 0, GRID_W - NA_WIN_C)
    kc = col_idx[:, None, :]
    ws = win_start[:, :, None]
    col_ok = (kc >= ws) & (kc < ws + NA_WIN_C)
    dr = row_idx - r[:, None] + NA_WIN_R - 1
    dc = jnp.clip(kc - q_col[:, :, None] + NA_WIN_C - 1, 0, 2 * NA_WIN_C - 2)
    bias = rpb[:, dr[:, None, None, :, None], dc[None, :, :, None, :]]
    bias = jnp.where(col_ok[None, None, :, :, None, :], bias.astype(jnp.float32), NEG_INF)
    n_loc = wr * NA_KC
    bias = bias.reshape(H, rows, ncb, NA_QC, n_loc).transpose(1, 2, 0, 3, 4)

    qg = (q * D ** -0.5).reshape(B, rows, ncb, NA_QC, H, D)
    kg = k.reshape(B, rows, GRID_W, H, D)
    vg = v.reshape(B, rows, GRID_W, H, D)
    ri = row_idx[:, None, :, None]
    ci = col_idx[None, :, None, :]
    kb = kg[:, ri, ci].reshape(B, rows, ncb, n_loc, H, D)
    vb = vg[:, ri, ci].reshape(B, rows, ncb, n_loc, H, D)
    s_loc = jnp.einsum('brnqhd,brnkhd->brnhqk', qg, kb).astype(jnp.float32) + bias[None]
    s_ctx = jnp.einsum('brnqhd,blhd->brnhql', qg, ctx_k).astype(jnp.float32)
    p = jax.nn.softmax(jnp.concatenate([s_loc, s_ctx], axis=-1), axis=-1).astype(v.dtype)
    o = (jnp.einsum('brnhqk,brnkhd->brnqhd', p[..., :n_loc], vb)
         + jnp.einsum('brnhql,blhd->brnqhd', p[..., n_loc:], ctx_v))
    return o.reshape(B, T, H, D)

def merge_heads(oa, ob, w_out):
    B, S = oa.shape[0], oa.shape[1]
    return jnp.concatenate([oa.reshape(B, S, -1), ob.reshape(B, S, -1)], axis=-1) @ w_out

def sgu_mixer(xn, w_in, v_g, w_s, b_s, w_out):
    B, S, _ = xn.shape
    u, v = jnp.split(jax.nn.gelu(xn @ w_in, approximate=False), 2, axis=-1)
    v = rms_norm(v, v_g)
    nc = S // SGU_CHUNK
    gw = SGU_WIDTH // SGU_GROUPS
    vg = v.reshape(B, nc, SGU_CHUNK, SGU_GROUPS, gw)
    sv = jnp.einsum('gts,bcsgd->bctgd', w_s, vg) + b_s.T[None, None, :, :, None]
    gated = u.reshape(B, nc, SGU_CHUNK, SGU_GROUPS, gw) * sv
    return gated.reshape(B, S, SGU_WIDTH) @ w_out

def setup_inputs(seed: int = 0) -> dict:
    key = jax.random.key(seed)
    ks = jax.random.split(key, 27)
    nrm = lambda k, shape, scale: jax.random.normal(k, shape, jnp.float32) * scale
    D = D_MODEL
    return {
        'x_prompt': nrm(ks[0], (BATCH, SEQ, D), 1.0),
        'x_sample': nrm(ks[1], (DEC_BATCH, DEC_SEQ, D), 1.0),
        'cache_na_k': nrm(ks[2], (DEC_BATCH, N_ATTN_LAYERS, PAST_LEN, NA_HEADS, HEAD_DIM), 1.0),
        'cache_na_v': nrm(ks[3], (DEC_BATCH, N_ATTN_LAYERS, PAST_LEN, NA_HEADS, HEAD_DIM), 1.0),
        'cache_gqa_k': nrm(ks[4], (DEC_BATCH, N_ATTN_LAYERS, PAST_LEN, GQA_KV_HEADS, HEAD_DIM), 1.0),
        'cache_gqa_v': nrm(ks[5], (DEC_BATCH, N_ATTN_LAYERS, PAST_LEN, GQA_KV_HEADS, HEAD_DIM), 1.0),
        'c': nrm(ks[6], (DEC_BATCH, D), 1.0),
        'c_ctx': nrm(ks[7], (D,), 1.0),
        'norm_g': 1.0 + nrm(ks[8], (DEPTH, 3, D), 0.1),
        'mod_w': nrm(ks[9], (DEPTH, D, N_MOD * D), 0.5 * D ** -0.5),
        'mod_b': nrm(ks[10], (DEPTH, N_MOD * D), 0.01),
        'ffn1_w_gu': nrm(ks[11], (DEPTH, D, 2 * FFN_HIDDEN), D ** -0.5),
        'ffn1_w_down': nrm(ks[12], (DEPTH, FFN_HIDDEN, D), FFN_HIDDEN ** -0.5),
        'ffn2_w_gu': nrm(ks[13], (DEPTH, D, 2 * FFN_HIDDEN), D ** -0.5),
        'ffn2_w_down': nrm(ks[14], (DEPTH, FFN_HIDDEN, D), FFN_HIDDEN ** -0.5),
        'attn_w_in': nrm(ks[15], (N_ATTN_LAYERS, D, QKV_WIDTH), D ** -0.5),
        'attn_w_out': nrm(ks[16], (N_ATTN_LAYERS, ATTN_OUT_WIDTH, D), ATTN_OUT_WIDTH ** -0.5),
        'na_q_g': 1.0 + nrm(ks[17], (N_ATTN_LAYERS, HEAD_DIM), 0.1),
        'na_k_g': 1.0 + nrm(ks[18], (N_ATTN_LAYERS, HEAD_DIM), 0.1),
        'na_rpb': nrm(ks[19], (N_ATTN_LAYERS, NA_HEADS, 2 * NA_WIN_R - 1, 2 * NA_WIN_C - 1), 0.1),
        'gqa_q_g': 1.0 + nrm(ks[20], (N_ATTN_LAYERS, HEAD_DIM), 0.1),
        'gqa_k_g': 1.0 + nrm(ks[21], (N_ATTN_LAYERS, HEAD_DIM), 0.1),
        'sgu_w_in': nrm(ks[22], (N_SGU_LAYERS, D, 2 * SGU_WIDTH), D ** -0.5),
        'sgu_v_g': 1.0 + nrm(ks[23], (N_SGU_LAYERS, SGU_WIDTH), 0.1),
        'sgu_w_s': nrm(ks[24], (N_SGU_LAYERS, SGU_GROUPS, SGU_CHUNK, SGU_CHUNK), 0.5 * SGU_CHUNK ** -0.5),
        'sgu_b_s': 1.0 + nrm(ks[25], (N_SGU_LAYERS, SGU_GROUPS, SGU_CHUNK), 0.1),
        'sgu_w_out': nrm(ks[26], (N_SGU_LAYERS, SGU_WIDTH, D), SGU_WIDTH ** -0.5),
    }

def reference(x_prompt, x_sample, cache_na_k, cache_na_v, cache_gqa_k, cache_gqa_v, c, c_ctx,
              norm_g, mod_w, mod_b, ffn1_w_gu, ffn1_w_down, ffn2_w_gu, ffn2_w_down,
              attn_w_in, attn_w_out, na_q_g, na_k_g, na_rpb, gqa_q_g, gqa_k_g,
              sgu_w_in, sgu_v_g, sgu_w_s, sgu_b_s, sgu_w_out):
    hp = x_prompt
    hs = x_sample
    na_k_list, na_v_list, gqa_k_list, gqa_v_list = [], [], [], []
    for i in range(DEPTH):
        m_ctx = modulation(c_ctx[None, :], mod_w[i], mod_b[i])
        m_lat = modulation(c, mod_w[i], mod_b[i])

        hp = hp + 0.5 * adaln_gate(m_ctx, 0) * swiglu(adaln_input(hp, m_ctx, 0, norm_g[i, 0]), ffn1_w_gu[i], ffn1_w_down[i])
        hs = hs + 0.5 * adaln_gate(m_lat, 0) * swiglu(adaln_input(hs, m_lat, 0, norm_g[i, 0]), ffn1_w_gu[i], ffn1_w_down[i])

        xp = adaln_input(hp, m_ctx, 1, norm_g[i, 1])
        xs = adaln_input(hs, m_lat, 1, norm_g[i, 1])
        if i % 2 == 0:
            e = i // 2
            qa, ka, va, qb, kb, vb = attn_project(xp, attn_w_in[e], na_q_g[e], na_k_g[e], gqa_q_g[e], gqa_k_g[e])
            out_p = merge_heads(dense_attention(qa, ka, va), dense_attention(qb, kb, vb), attn_w_out[e])
            na_k_list.append(ka)
            na_v_list.append(va)
            gqa_k_list.append(kb)
            gqa_v_list.append(vb)
            qa, ka, va, qb, kb, vb = attn_project(xs, attn_w_in[e], na_q_g[e], na_k_g[e], gqa_q_g[e], gqa_k_g[e])
            oa = neighbourhood_attention(qa, ka, va, cache_na_k[:, e], cache_na_v[:, e], na_rpb[e])
            ob = dense_attention(axial_rope(qb),
                                 jnp.concatenate([axial_rope(kb), cache_gqa_k[:, e]], axis=1),
                                 jnp.concatenate([vb, cache_gqa_v[:, e]], axis=1))
            out_s = merge_heads(oa, ob, attn_w_out[e])
        else:
            o = i // 2
            out_p = sgu_mixer(xp, sgu_w_in[o], sgu_v_g[o], sgu_w_s[o], sgu_b_s[o], sgu_w_out[o])
            out_s = sgu_mixer(xs, sgu_w_in[o], sgu_v_g[o], sgu_w_s[o], sgu_b_s[o], sgu_w_out[o])
        hp = hp + adaln_gate(m_ctx, 1) * out_p
        hs = hs + adaln_gate(m_lat, 1) * out_s

        hp = hp + 0.5 * adaln_gate(m_ctx, 2) * swiglu(adaln_input(hp, m_ctx, 2, norm_g[i, 2]), ffn2_w_gu[i], ffn2_w_down[i])
        hs = hs + 0.5 * adaln_gate(m_lat, 2) * swiglu(adaln_input(hs, m_lat, 2, norm_g[i, 2]), ffn2_w_gu[i], ffn2_w_down[i])

    new_na_k = jnp.stack(na_k_list, axis=1)
    new_na_v = jnp.stack(na_v_list, axis=1)
    new_gqa_k = jnp.stack(gqa_k_list, axis=1)
    new_gqa_v = jnp.stack(gqa_v_list, axis=1)
    return (hp, hs, new_na_k, new_na_v, new_gqa_k, new_gqa_v)


_drawn_inputs = setup_inputs


def setup_inputs(seed=0):
    import zlib

    import numpy as np

    out = dict(_drawn_inputs(seed))
    spreads = {}
    factors = {'cache_na_k': 3.616,
     'cache_na_v': 2.94,
     'cache_gqa_k': 6.513,
     'cache_gqa_v': 5.299,
     'mod_b': 4.036,
     'na_q_g': 8.0,
     'na_rpb': 8.0,
     'gqa_q_g': 8.0,
     'sgu_v_g': 5.726,
     'sgu_b_s': 2.825}
    for name, (base, spread) in spreads.items():
        noise = np.random.default_rng([zlib.crc32(name.encode()), seed]).standard_normal(out[name].shape)
        drawn = base * np.exp(spread * noise) if base else spread * noise
        out[name] = __import__('jax').numpy.asarray(drawn.astype(out[name].dtype))
    for name, factor in factors.items():
        out[name] = (out[name] * factor).astype(out[name].dtype)
    return out
```

```python
from contextlib import ExitStack

import numpy as np
import concourse.bass as bass
from concourse import mybir

ALU = mybir.AluOpType
ACT = mybir.ActivationFunctionType
AX = mybir.AxisListType
F32 = mybir.dt.float32
F32R = mybir.dt.float32r

P = 128
D = 1024
KD = D // P
NCTX, NLAT = 128, 256
T = NCTX + NLAT
TT = T // P
CTX, LAT = slice(0, NCTX), slice(NCTX, T)
DEPTH = 2
F = 2816
GU = F // 256
KF = F // P
NMOD = 9
HD = 64
NH = 8
KVW = 128
GRID = 64
ROWS = NLAT // GRID
SW = 2 * D
KS = SW // P
NG = 8
EPS = 1e-6
PW = 2048
MB = 256
NMB = NMOD * D // MB
MOD_FIRST = 2 * D // MB
TOEP = 2 * GRID - 1
NDR = 15
BANDC = 31
ORDER = (4, 5, 6, 7, 0, 1, 2, 3)

Q_F = (0, 46, 79, 136)
Q_IN0, Q_OUT0 = 33, 42
Q_V, Q_U, Q_OUT1 = 112, 120, 128
Q_END = 169
MOD_AT = (10, 32, 54, 72)
NORMS = 6


def build(nc, t_in, t_out, toep_dram):
    (x_prompt, x_sample, ck_na, cv_na, ck_g, cv_g, c, c_ctx, norm_g, mod_w, mod_b, w_gu1, w_dn1, w_gu2, w_dn2,
     w_attn, w_o, na_q_g, na_k_g, na_rpb, g_q_g, g_k_g, w_sgu, v_g, w_s, b_s, w_sgo, rope, mask, consts) = t_in
    y_p, y_s, o_nak, o_nav, o_gk, o_gv = t_out

    ctx = ExitStack()
    with ctx:
        def sb(name, shape, dt=F32, scope=ctx):
            return scope.enter_context(nc.sbuf_tensor(name, shape, dt))

        def sem(name):
            return ctx.enter_context(nc.semaphore(name))

        h = sb("h", [P, KD, T])
        raw = [sb(f"raw{i}", [P, PW]) for i in range(2)]
        w_hi = [sb(f"w_hi{i}", [P, PW], F32R) for i in range(2)]
        w_lo = [sb(f"w_lo{i}", [P, PW], F32R) for i in range(2)]
        mraw = [sb(f"mraw{i}", [P, KD, MB]) for i in range(2)]
        tmp = sb("tmp", [P, 4, T])
        sq = sb("sq", [P, 2, T])
        sqsum = sb("sqsum", [P, T])
        ident = sb("ident", [P, P])
        ones = sb("ones", [P, P])
        modT = sb("modT", [P, DEPTH * NMOD * KD, 2])
        mbT = sb("mbT", [P, DEPTH * NMOD * KD])
        ngT = sb("ngT", [P, DEPTH * 3 * KD])
        vgT = sb("vgT", [P, KS])
        cT = sb("cT", [P, KD, 2])
        aT = sb("aT", [P, KD, 2])
        gT = sb("gT", [P, KD, 2])
        ms = sb("ms", [P, TT])
        rs = sb("rs", [P, TT])
        mhalf = sb("mhalf", [P, 16])
        hms = sb("hms", [P, 12])
        hrs = sb("hrs", [P, 12])
        nmax = sb("nmax", [P, 3])
        rsum = sb("rsum", [P, 3])
        rinv = sb("rinv", [P, 3])
        vss = sb("vss", [P, TT, KD])

        with ExitStack() as s:
            y_tok = sb("y_tok", [P, TT, D], scope=s)
        x_hi = sb("x_hi", [P, KD, T], F32R)
        x_lo = sb("x_lo", [P, KD, T], F32R)

        with ExitStack() as s:
            svb = sb("svb", [P, KS, T], scope=s)
        with ExitStack() as s:
            bias = sb("bias", [P, 2, NH, NLAT], scope=s)
            kc_na = sb("kc_na", [P, NH * HD], scope=s)
            vc_na = sb("vc_na", [P, NH * HD], scope=s)
            kc_g = sb("kc_g", [P, KVW], scope=s)
            vc_g = sb("vc_g", [P, KVW], scope=s)
            ropeT = sb("ropeT", [P, 2, 2, HD], scope=s)
            gain = sb("gain", [P, 4, HD], scope=s)
            maskT = sb("maskT", [P, GRID], scope=s)
            perm = sb("perm", [P, P], scope=s)
        sb("region_d", [P, KS, T])

        with ExitStack() as s:
            x_tok = sb("x_tok", [P, TT, D], scope=s)
            vec = sb("vec", [P, 5, P], scope=s)
            toep = sb("toep", [NH * NDR, TOEP], scope=s)
        with ExitStack() as s:
            q_na = sb("q_na", [P, TT, NH, HD], scope=s)
            k_na = sb("k_na", [P, TT, NH, HD], scope=s)
            qk_g = sb("qk_g", [P, TT, NH + 2, HD], scope=s)
            v_na = sb("v_na", [P, TT, NH * HD], scope=s)
            vg_ = sb("vg_", [P, TT, KVW], scope=s)
            qT_na = sb("qT_na", [P, 4, T], scope=s)
            kT_na = sb("kT_na", [P, 4, T + P], scope=s)
            qT_g = sb("qT_g", [P, 4, T], scope=s)
            kT_g = sb("kT_g", [P, T + P], scope=s)
            prob = sb("prob", [P, 3, T], scope=s)
            pT_lat = sb("pT_lat", [P, 2, 3, NLAT], scope=s)
            pT_ctx = sb("pT_ctx", [P, 2, NCTX], scope=s)
        with ExitStack() as s:
            v_tok = sb("v_tok", [P, TT, SW], scope=s)
            ws_row = sb("ws_row", [P, NG, P], scope=s)
            wsT = sb("wsT", [P, NG, P], scope=s)
            wsn = sb("wsn", [P, TT, NG, P], scope=s)
            bsb = sb("bsb", [P, NG, P], scope=s)
            vsq = sb("vsq", [P, TT, 256], scope=s)
        act_hi = sb("act_hi", [P, KF, T], F32R)
        act_lo = sb("act_lo", [P, KF, T], F32R)
        ps = ctx.enter_context(nc.psum_tensor("ps", [P, 8, 512], F32))

        raw_in = [sem(f"raw_in{i}") for i in range(2)]
        hi_done = sem("hi_done")
        lo_done = sem("lo_done")
        pe_done = sem("pe_done")
        mraw_in = [sem(f"mraw_in{i}") for i in range(2)]
        mod_pe = sem("mod_pe")
        mod_done = sem("mod_done")
        silu_done = sem("silu_done")
        mul_done = sem("mul_done")
        acth_done = sem("acth_done")
        actl_done = sem("actl_done")
        out_done = sem("out_done")
        h_done = sem("h_done")
        sq_done = sem("sq_done")
        acc_done = sem("acc_done")
        stat_done = sem("stat_done")
        ms_done = sem("ms_done")
        rs_done = sem("rs_done")
        diag_done = sem("diag_done")
        rb_done = sem("rb_done")
        t_done = sem("t_done")
        xm_done = sem("xm_done")
        xh_done = sem("xh_done")
        x_done = sem("x_done")
        mvec = sem("mvec")
        x_in = sem("x_in")
        vec_in = sem("vec_in")
        c_in = sem("c_in")
        const_in = sem("const_in")
        ones_set = sem("ones_set")
        zero_set = sem("zero_set")
        vecT_pe = sem("vecT_pe")
        vecT_done = sem("vecT_done")
        c_pe = sem("c_pe")
        c_done = sem("c_done")
        xT_pe = sem("xT_pe")
        toep_in = sem("toep_in")
        toep_out = sem("toep_out")
        bias_in = sem("bias_in")
        bias_done = sem("bias_done")
        tab_in = sem("tab_in")
        gain_done = sem("gain_done")
        hsq_done = sem("hsq_done")
        hms_sum = sem("hms_sum")
        hms_done = sem("hms_done")
        hrs_done = sem("hrs_done")
        dve_self = sem("dve_self")
        act_self = sem("act_self")
        qkv_act = sem("qkv_act")
        qkv_dve = sem("qkv_dve")
        rope_done = sem("rope_done")
        tr_pe = sem("tr_pe")
        tr_act = sem("tr_act")
        tr_dve = sem("tr_dve")
        s_pe = sem("s_pe")
        nmax_done = sem("nmax_done")
        exp_done = sem("exp_done")
        prob_done = sem("prob_done")
        pT_pe = sem("pT_pe")
        pT_done = sem("pT_done")
        o_pe = sem("o_pe")
        oh_done = sem("oh_done")
        ol_done = sem("ol_done")
        ws_in = sem("ws_in")
        ws_pe = sem("ws_pe")
        wsT_done = sem("wsT_done")
        gelu_v = sem("gelu_v")
        vss_done = sem("vss_done")
        vms_done = sem("vms_done")
        vrs_done = sem("vrs_done")
        wsn_done = sem("wsn_done")
        sv_pe = sem("sv_pe")
        sv_done = sem("sv_done")
        yT_pe = sem("yT_pe")
        y_done = sem("y_done")
        stored = sem("stored")

        block = ctx.enter_context(nc.Block())

        dve_steps = [0]

        def gu_src(w_gu, layer, g0, i, up):
            v = w_gu[layer].rearrange("(k p) n -> p k n", p=P)
            return v[:, :, bass.ds(F * up + 256 * (g0 + i), 256)]

        def dn_src(w, j0, i):
            v = w.rearrange("(j c p) n -> p j c n", c=2, p=P)
            return v[:, bass.ds(j0 + 2 * i, 1), :, :]

        def col_src(w, g):
            return w.rearrange("(k p) n -> p k n", p=P)[:, :, 256 * g:256 * g + 256]

        FFN = [(w_gu1, w_dn1, 0), (w_gu2, w_dn2, 0), (w_gu1, w_dn1, 1), (w_gu2, w_dn2, 1)]

        def loop_pairs(f, eng, pair, start=0):
            def mod(g):
                b = MOD_AT[f] + 2 * g if f < 3 else NMB * DEPTH
                return b if b < (MOD_AT[f + 1] if f < 3 else 0) else None
            cuts = {0: [0, 1, GU], 1: [0, 1, 2, GU], 2: [0, 1, 9, GU], 3: [0, 1, GU]}[f][start:]
            for a, b in zip(cuts, cuts[1:]):
                if b - a == 1:
                    pair(a, 0, mod(a))
                else:
                    with eng.Fori(0, b - a) as i:
                        pair(a, i, mod(a))

        def panels_after_first(n, step, eng):
            its = (n - 2) // 2
            with eng.Fori(0, its) as i:
                step(1, i)
                step(2, i)
            for j in range(1 + 2 * its, n - 1):
                step(j, 0)

        def hsq_view(w):
            return tmp[:, 0:2, :].rearrange("p a t -> p (a t)")[:, 0:TT * w].rearrange("p (a w) -> p a w", a=TT)

        def rot_view():
            return tmp[:, 0:2, :].rearrange("p a t -> p (a t)")[:, 0:(NH + 2) * HD].rearrange("p (h d) -> p h d", d=HD)

        def tr_groups():
            return ([(qT_na[:, n, :], T) for n in range(4)] + [(kT_na[:, n, :], T + P) for n in range(4)]
                    + [(qT_g[:, n, :], T) for n in range(4)] + [(kT_g[:, :], T + P)])

        @block.sync
        def _(sp):
            def panel(q0, i, src, shape):
                if q0 >= 2:
                    sp.wait_ge(lo_done, q0 + 2 * i - 1)
                dst = raw[q0 % 2][:, :].rearrange(shape[0], **shape[1])
                sp.dma_start(dst, src).then_inc(raw_in[q0 % 2], 16)

            KN = ("p (k n) -> p k n", dict(k=KD))
            JCN = ("p (j c n) -> p j c n", dict(j=1, c=2))

            def mod_block(b0, i):
                if b0 >= 2:
                    sp.wait_ge(mod_pe, b0 + 2 * i - 1)
                layer = b0 // NMB
                v = mod_w[layer].rearrange("(k p) n -> p k n", p=P)
                sp.dma_start(mraw[b0 % 2][:, :, :], v[:, :, bass.ds(MB * (b0 - NMB * layer + 2 * i), MB)]) \
                    .then_inc(mraw_in[b0 % 2], 16)

            def for_panels(n, step, eng):
                its = (n - 2) // 2
                with eng.Fori(0, its) as i:
                    step(1, i)
                    step(2, i)
                for j in range(1 + 2 * its, n):
                    step(j, 0)

            def down(q0, w, n):
                panel(q0, 0, dn_src(w, 0, 0), JCN)
                for_panels(n, lambda j0, i: panel(q0 + j0, i, dn_src(w, j0, i), JCN), sp)

            def gate_up(f):
                w_gu, _, layer = FFN[f]

                def pair(g0, i, b):
                    panel(Q_F[f] + 2 * g0, i, gu_src(w_gu, layer, g0, i, 0), KN)
                    panel(Q_F[f] + 2 * g0 + 1, i, gu_src(w_gu, layer, g0, i, 1), KN)
                    if b is not None:
                        mod_block(b, i)
                        mod_block(b + 1, i)
                loop_pairs(f, sp, pair, start=1 if f == 0 else 0)

            sp.dma_start(vec[0:8, 0, :], c_ctx.rearrange("(k p) -> k p", p=P)).then_inc(c_in, 16)
            sp.dma_start(vec[8:16, 0, :], c.rearrange("b (k p) -> (b k) p", p=P)).then_inc(c_in, 16)
            sp.dma_start(ident[:, :], consts[0]).then_inc(const_in, 16)
            mod_block(0, 0)
            mod_block(1, 0)
            sp.dma_start(x_tok[:, 0, :], x_prompt[0]).then_inc(x_in, 16)
            sp.dma_start(x_tok[:, 1:3, :], x_sample[0].rearrange("(a p) n -> p a n", p=P)).then_inc(x_in, 16)
            for layer in range(DEPTH):
                sp.dma_start(vec[0:NMOD * KD, 1 + layer, :], mod_b[layer].rearrange("(m p) -> m p", p=P)).then_inc(vec_in, 16)
            sp.dma_start(vec[0:DEPTH * 3 * KD, 3, :], norm_g.rearrange("l j (k p) -> (l j k) p", p=P)).then_inc(vec_in, 16)
            sp.dma_start(vec[0:KS, 4, :], v_g[0].rearrange("(k p) -> k p", p=P)).then_inc(vec_in, 16)
            for b in range(2, MOD_FIRST):
                mod_block(b, 0)
            panel(0, 0, gu_src(w_gu1, 0, 0, 0, 0), KN)
            panel(1, 0, gu_src(w_gu1, 0, 0, 0, 1), KN)
            mod_block(MOD_FIRST, 0)
            mod_block(MOD_FIRST + 1, 0)
            mod_block(MOD_AT[0], 0)
            mod_block(MOD_AT[0] + 1, 0)
            sp.wait_ge(zero_set, 1)
            sp.dma_start(toep[:, GRID - 16:GRID - 16 + BANDC], na_rpb[0].rearrange("h r c -> (h r) c")) \
                .then_inc(toep_in, 16)
            sp.dma_start(kc_na[:, :], ck_na[0, 0].rearrange("s h d -> s (h d)")).then_inc(tab_in, 16)
            sp.dma_start(vc_na[:, :], cv_na[0, 0].rearrange("s h d -> s (h d)")).then_inc(tab_in, 16)
            sp.dma_start(kc_g[:, :], ck_g[0, 0].rearrange("s h d -> s (h d)")).then_inc(tab_in, 16)
            sp.dma_start(vc_g[:, :], cv_g[0, 0].rearrange("s h d -> s (h d)")).then_inc(tab_in, 16)
            sp.dma_start(ropeT[:, :, :, :], rope.rearrange("c (a p) d -> p c a d", p=P)).then_inc(tab_in, 16)
            sp.dma_start(maskT[:, :], mask).then_inc(tab_in, 16)
            sp.dma_start(perm[:, :], consts[1]).then_inc(tab_in, 16)
            for n, g in enumerate((na_q_g, na_k_g, g_q_g, g_k_g)):
                sp.dma_start(gain[:, n, :], g[0].rearrange("(o d) -> o d", o=1).to_broadcast([P, HD])).then_inc(tab_in, 16)
            sp.wait_ge(toep_in, 16)
            sp.dma_start(toep_dram, toep[:, :]).then_inc(toep_out, 16)
            sp.wait_ge(toep_out, 16)
            for r in range(ROWS):
                for hh in range(NH):
                    src = bass.AP(toep_dram.tensor, (NDR * hh + 7 - r) * TOEP, [[1, GRID], [TOEP, ROWS], [1, GRID]])
                    dst = bias[GRID * (r % 2):GRID * (r % 2) + GRID, r // 2, hh, :].rearrange("p (a b) -> p a b", a=ROWS)
                    sp.dma_start(dst, src).then_inc(bias_in, 16)

            gate_up(0)
            down(Q_F[0] + 2 * GU, w_dn1[0], GU)
            for g in range(9):
                panel(Q_IN0 + g, 0, col_src(w_attn[0], g), KN)
            down(Q_OUT0, w_o[0], KD // 2)
            sp.wait_ge(qkv_dve, 9)
            sp.wait_ge(qkv_act, 3)
            sp.dma_start(o_nak[0, 0], k_na[:, 0, :, :]).then_inc(stored, 16)
            sp.dma_start(o_nav[0, 0].rearrange("s h d -> s (h d)"), v_na[:, 0, :]).then_inc(stored, 16)
            sp.dma_start(o_gk[0, 0], qk_g[:, 0, NH:NH + 2, :]).then_inc(stored, 16)
            sp.dma_start(o_gv[0, 0].rearrange("s h d -> s (h d)"), vg_[:, 0, :]).then_inc(stored, 16)
            gate_up(1)
            down(Q_F[1] + 2 * GU, w_dn2[0], GU)
            gate_up(2)
            down(Q_F[2] + 2 * GU, w_dn1[1], GU)
            for g in range(8):
                panel(Q_V + g, 0, col_src(w_sgu[0], 8 + g), KN)
                if g == 1:
                    sp.wait_ge(pe_done, Q_V)
                    sp.dma_start(ws_row[:, :, :], w_s[0].rearrange("g t s -> t g s")).then_inc(ws_in, 16)
                    sp.dma_start(bsb[:, :, :], b_s[0].rearrange("(o g) t -> o g t", o=1).to_broadcast([P, NG, P])) \
                        .then_inc(ws_in, 16)
            for g in range(8):
                panel(Q_U + g, 0, col_src(w_sgu[0], g), KN)
            down(Q_OUT1, w_sgo[0], KS // 2)
            gate_up(3)
            down(Q_F[3] + 2 * GU, w_dn2[1], GU)
            for half in (1, 0):
                cols = slice(512 * half, 512 * half + 512)
                sp.wait_ge(y_done, 4 if half else 8)
                sp.dma_start(y_p[0][:, cols], y_tok[:, 0, cols]).then_inc(stored, 16)
                sp.dma_start(y_s[0].rearrange("(a p) n -> p a n", p=P)[:, :, cols], y_tok[:, 1:3, cols]).then_inc(stored, 16)
            sp.wait_ge(stored, 16 * 8)

        @block.gpsimd
        def _(pool):
            nc.gpsimd.memset(ones[:, :], 1.0).then_inc(ones_set, 1)
            nc.gpsimd.memset(mhalf[:, :], -0.5).then_inc(ones_set, 1)
            nc.gpsimd.memset(toep[:, :], 0.0).then_inc(zero_set, 1)

            def norm(n):
                for k in range(1, KD - 1):
                    pool.wait_ge(sq_done, KD * n + k + 1)
                    if k == 1:
                        if n:
                            pool.wait_ge(stat_done, n)
                        nc.gpsimd.tensor_tensor(sqsum[:, :], sq[:, 0, :], sq[:, 1, :], ALU.add).then_inc(acc_done, 1)
                    else:
                        pool.wait_ge(acc_done, 6 * n + k - 1)
                        nc.gpsimd.tensor_tensor(sqsum[:, :], sqsum[:, :], sq[:, k % 2, :], ALU.add).then_inc(acc_done, 1)
                pool.wait_ge(ms_done, n + 1)
                nc.gpsimd.tensor_tensor(rs[:, :], ms[:, :], mhalf[:, 0:TT], ALU.pow).then_inc(rs_done, 1)

            pool.wait_ge(ones_set, 2)
            norm(0)
            pool.wait_ge(bias_in, 16 * ROWS * NH)
            pool.wait_ge(tab_in, 16 * 11)
            for qt in range(2):
                bv = bias[:, qt, :, :].rearrange("p h (r k) -> p (h r) k", k=GRID)
                nc.gpsimd.tensor_tensor(bv, bv, maskT[:, None, :].to_broadcast([P, NH * ROWS, GRID]), ALU.add) \
                    .then_inc(bias_done, 1)
            norm(1)
            for m in range(7):
                pool.wait_ge(hms_done, m + 1)
                w = 12 if m < 6 else 6
                nc.gpsimd.tensor_tensor(hrs[:, 0:w], hms[:, 0:w], mhalf[:, 0:w], ALU.pow).then_inc(hrs_done, 1)
            norm(2)
            norm(3)
            norm(4)
            pool.wait_ge(vms_done, 1)
            nc.gpsimd.tensor_tensor(rs[:, :], ms[:, :], mhalf[:, 0:TT], ALU.pow).then_inc(vrs_done, 1)
            norm(5)

        @block.scalar
        def _(act):
            steps = [0]

            def split(q0, i):
                if q0 >= Q_END:
                    return
                act.wait_ge(raw_in[q0 % 2], 16 * (q0 // 2 + 1 + i))
                if q0 >= 2:
                    act.wait_ge(pe_done, q0 + 2 * i - 1)
                nc.scalar.activation(w_hi[q0 % 2][:, :], raw[q0 % 2][:, :], ACT.Copy).then_inc(hi_done, 1)

            def squares(n):
                for k, m in enumerate(ORDER):
                    act.wait_ge(h_done, KD * n + k + 1)
                    if k >= 2:
                        act.wait_ge(acc_done, 6 * n + max(1, k - 2))
                    elif n:
                        act.wait_ge(stat_done, n)
                    nc.scalar.activation(sq[:, k % 2, :], h[:, m, :], ACT.Square).then_inc(sq_done, 1)

            def make_x(n, j):
                layer, seg = j
                base = (layer * NMOD + 3 * seg) * KD
                act.wait_ge(mvec, n + 1)
                for k in range(KD):
                    act.wait_ge(t_done, KD * n + k + 1)
                    for cond, cols in ((0, CTX), (1, LAT)):
                        last = nc.scalar.activation(tmp[:, k % 4, cols], tmp[:, k % 4, cols], ACT.Identity,
                                                    bias=modT[:, base + k, cond:cond + 1], scale=aT[:, k, cond:cond + 1])
                    last.then_inc(xm_done, 1)
                    act.wait_ge(xm_done, KD * n + k + 1)
                    nc.scalar.activation(x_hi[:, k, :], tmp[:, k % 4, :], ACT.Copy).then_inc(xh_done, 1)

            def ffn(f):
                q = Q_F[f]

                def pair(g0, i, b):
                    done = (PAIRS[f] + g0) + i
                    act.wait_ge(pe_done, q + 2 * g0 + 1 + 2 * i)
                    if PAIRS[f] + g0:
                        act.wait_ge(actl_done, done)
                    nc.scalar.activation(tmp[:, 0:2, :], ps[:, 0:2, 0:T], ACT.Silu).then_inc(silu_done, 1)
                    split(q + 2 * g0 + 2, i)
                    act.wait_ge(mul_done, done + 1)
                    nc.scalar.activation(act_hi[:, bass.ds(2 * g0 + 2 * i, 2), :], tmp[:, 0:2, :], ACT.Copy) \
                        .then_inc(acth_done, 1)
                    split(q + 2 * g0 + 3, i)
                loop_pairs(f, act, pair)

            def down(q0, n):
                split(q0 + 2, 0)
                panels_after_first(n, lambda j0, i: split(q0 + j0 + 2, i), act)

            act.wait_ge(c_pe, 1)
            nc.scalar.activation(cT[:, :, :].rearrange("p k c -> p c k"),
                                 ps[:, 0, 0:16].rearrange("p (c k) -> p c k", c=2), ACT.Silu).then_inc(c_done, 1)
            squares(0)
            split(0, 0)
            split(1, 0)
            make_x(0, (0, 0))
            act.wait_ge(toep_out, 16)
            ffn(0)
            down(Q_F[0] + 2 * GU, GU)
            squares(1)
            make_x(1, (0, 1))
            split(Q_IN0 + 1, 0)
            for g in range(9):
                act.wait_ge(pe_done, Q_IN0 + g + 1)
                if g in (4, 5, 8):
                    for t in range(TT):
                        dst, cols = (v_na[:, t, 256 * (g - 4):256 * (g - 4) + 256], slice(0, 256)) if g < 8 \
                            else (vg_[:, t, :], slice(128, 256))
                        last = nc.scalar.activation(dst, ps[:, QBANK[g % 2][t], cols], ACT.Copy)
                    last.then_inc(qkv_act, 1)
                if g not in (4, 5):
                    m = g if g < 4 else g - 2
                    w = 256 if g < 8 else 128
                    if m:
                        act.wait_ge(hms_sum, m)
                    for t in range(TT):
                        last = nc.scalar.activation(hsq_view(w)[:, t, :], ps[:, QBANK[g % 2][t], 0:w], ACT.Square)
                    last.then_inc(hsq_done, 1)
                split(Q_IN0 + g + 2, 0)
            for g, (dst, n) in enumerate(tr_groups()):
                if g % 2 == 0:
                    act.wait_ge(tr_pe, g + 1)
                    nc.scalar.activation(dst, ps[:, g % 8, 0:n], ACT.Copy).then_inc(tr_act, 1)

            def softmax(b):
                n = NCTX if b % 3 == 0 else T
                act.wait_ge(nmax_done, b + 1)
                if b >= 3:
                    act.wait_ge(pT_pe, b - 2)
                nc.scalar.activation(prob[:, b % 3, 0:n], ps[:, b % 3, 0:n], ACT.Exp, bias=nmax[:, b % 3:b % 3 + 1],
                                     accum_out=rsum[:, b % 3:b % 3 + 1]).then_inc(exp_done, 1)

            def put_pT(b):
                hh, kind = divmod(b, 3)
                act.wait_ge(pT_pe, b + 1)
                if hh >= 2 and kind == 0:
                    act.wait_ge(o_pe, hh - 1)
                if kind == 0:
                    nc.scalar.activation(pT_ctx[:, hh % 2, :], ps[:, 3 + b % 3, 0:P], ACT.Copy).then_inc(pT_done, 1)
                else:
                    nc.scalar.activation(pT_lat[:, hh % 2, :, P * (kind - 1):P * kind],
                                         ps[:, 3 + b % 3, 0:T].rearrange("p (k q) -> p k q", k=3), ACT.Copy) \
                        .then_inc(pT_done, 1)

            def o_hi(pair):
                act.wait_ge(o_pe, 2 * pair + 2)
                nc.scalar.activation(x_hi[:, pair, :], ps[:, 6 + pair % 2, 0:T], ACT.Copy).then_inc(oh_done, 1)

            for b in range(48 + 2):
                if b < 48:
                    softmax(b)
                if b >= 2:
                    put_pT(b - 2)
                if b >= 11 and (b - 11) % 6 == 0:
                    o_hi((b - 11) // 6)
            o_hi(7)
            down(Q_OUT0, KD // 2)
            squares(2)
            make_x(2, (0, 2))
            split(Q_F[1] + 1, 0)
            act.wait_ge(stored, 16 * 4)
            ffn(1)
            down(Q_F[1] + 2 * GU, GU)
            squares(3)
            make_x(3, (1, 0))
            split(Q_F[2] + 1, 0)
            ffn(2)
            down(Q_F[2] + 2 * GU, GU)
            squares(4)
            make_x(4, (1, 1))
            split(Q_V + 1, 0)
            for g in range(2):
                act.wait_ge(ws_pe, g + 1)
                nc.scalar.activation(wsT[:, 4 * g:4 * g + 4, :], ps[:, 4 + g, :].rearrange("p (g t) -> p g t", g=4), ACT.Copy) \
                    .then_inc(wsT_done, 1)
            for g in range(8):
                act.wait_ge(pe_done, Q_V + g + 1)
                for t in range(TT):
                    last = nc.scalar.activation(v_tok[:, t, 256 * g:256 * g + 256], ps[:, QBANK[g % 2][t], 0:256], ACT.Gelu)
                last.then_inc(gelu_v, 1)
                act.wait_ge(gelu_v, g + 1)
                if g:
                    act.wait_ge(vss_done, g)
                for t in range(TT):
                    last = nc.scalar.activation(vsq[:, t, :], v_tok[:, t, 256 * g:256 * g + 256], ACT.Square,
                                                accum_out=vss[:, t, g:g + 1])
                last.then_inc(vss_done, 1)
                split(Q_V + g + 2, 0)
            for g in range(8):
                done = UPAIR + g
                act.wait_ge(pe_done, Q_U + g + 1)
                act.wait_ge(actl_done, done)
                bk = 2 * (g % 2)
                nc.scalar.activation(tmp[:, 0:2, :], ps[:, bk:bk + 2, 0:T], ACT.Gelu).then_inc(silu_done, 1)
                act.wait_ge(mul_done, done + 1)
                nc.scalar.activation(act_hi[:, 2 * g:2 * g + 2, :], tmp[:, 0:2, :], ACT.Copy).then_inc(acth_done, 1)
                split(Q_U + g + 2, 0)
            down(Q_OUT1, KS // 2)
            squares(5)
            make_x(5, (1, 2))
            split(Q_F[3] + 1, 0)
            ffn(3)
            down(Q_F[3] + 2 * GU, GU)
            for k, m in enumerate(ORDER):
                act.wait_ge(yT_pe, k + 1)
                nc.scalar.activation(y_tok[:, :, P * m:P * m + P], ps[:, m, 0:T].rearrange("p (a n) -> p a n", a=TT), ACT.Copy) \
                    .then_inc(y_done, 1)

        @block.vector
        def _(dve):
            def link(ins):
                dve_steps[0] += 1
                ins.then_inc(dve_self, 1)
                dve.wait_ge(dve_self, dve_steps[0])

            def split(q0, i):
                if q0 >= Q_END:
                    return
                dve.wait_ge(hi_done, q0 + 2 * i + 1)
                nc.vector.tensor_tensor(w_lo[q0 % 2][:, :], raw[q0 % 2][:, :], w_hi[q0 % 2][:, :].bitcast(F32),
                                        ALU.subtract).then_inc(lo_done, 1)

            def mod_out(b0, i):
                dve.wait_ge(mod_pe, b0 + 2 * i + 1)
                nc.vector.tensor_tensor(modT[:, bass.ds(2 * b0 + 4 * i, 2), :],
                                        ps[:, 6 + b0 % 2, 0:4].rearrange("p (a c) -> p a c", c=2),
                                        mbT[:, bass.ds(2 * b0 + 4 * i, 2), None].to_broadcast([P, 2, 2]), ALU.add) \
                    .then_inc(mod_done, 1)

            def vectors(n, j):
                layer, seg = j
                base = (layer * NMOD + 3 * seg) * KD
                dve.wait_ge(mod_done, (base + 2 * KD) // 2)
                if n:
                    dve.wait_ge(xm_done, KD * n)
                nc.vector.scalar_tensor_tensor(
                    aT[:, :, :], modT[:, base + KD:base + 2 * KD, :], 1.0,
                    ngT[:, (layer * 3 + seg) * KD:(layer * 3 + seg + 1) * KD, None].to_broadcast([P, KD, 2]),
                    ALU.add, ALU.mult).then_inc(mvec, 1)

            def gate(n, j, w):
                layer, seg = j
                base = (layer * NMOD + 3 * seg + 2) * KD
                dve.wait_ge(mod_done, (base + KD) // 2)
                link(nc.vector.tensor_scalar(gT[:, :, :], modT[:, base:base + KD, :], w, None, ALU.mult))

            def make_x(n, bank5=5):
                dve.wait_ge(stat_done, n + 1)
                nc.vector.tensor_scalar(ms[:, :], ps[:, 4, 0:TT], 1.0 / D, EPS, ALU.mult, ALU.add).then_inc(ms_done, 1)
                dve.wait_ge(rs_done, n + 1)
                nc.vector.tensor_tensor(sqsum[:, :].rearrange("p (a q) -> p a q", a=TT),
                                        ident[:, None, :].to_broadcast([P, TT, P]),
                                        rs[:, :, None].to_broadcast([P, TT, P]), ALU.mult).then_inc(diag_done, 1)
                dve.wait_ge(rb_done, n + 1)

                def t_of(k):
                    if k >= 4:
                        dve.wait_ge(xh_done, KD * n + k - 3)
                    nc.vector.tensor_tensor(tmp[:, k % 4, :], h[:, k, :], ps[:, 5, 0:T], ALU.mult).then_inc(t_done, 1)

                t_of(0)
                t_of(1)
                for k in range(KD):
                    dve.wait_ge(xh_done, KD * n + k + 1)
                    nc.vector.tensor_tensor(x_lo[:, k, :], tmp[:, k % 4, :], x_hi[:, k, :].bitcast(F32), ALU.subtract) \
                        .then_inc(x_done, 1)
                    if k + 2 < KD:
                        t_of(k + 2)

            def ffn(f):
                q = Q_F[f]

                def pair(g0, i, b):
                    done = PAIRS[f] + g0 + i
                    if b is not None:
                        mod_out(b, i)
                    split(q + 2 * g0 + 2, i)
                    dve.wait_ge(pe_done, q + 2 * g0 + 2 + 2 * i)
                    dve.wait_ge(silu_done, done + 1)
                    nc.vector.tensor_tensor(tmp[:, 0:2, :], ps[:, 2:4, 0:T], tmp[:, 0:2, :], ALU.mult).then_inc(mul_done, 1)
                    if b is not None:
                        mod_out(b + 1, i)
                    dve.wait_ge(acth_done, done + 1)
                    nc.vector.tensor_tensor(act_lo[:, bass.ds(2 * g0 + 2 * i, 2), :], tmp[:, 0:2, :],
                                            act_hi[:, bass.ds(2 * g0 + 2 * i, 2), :].bitcast(F32), ALU.subtract) \
                        .then_inc(actl_done, 1)
                    split(q + 2 * g0 + 3, i)
                loop_pairs(f, dve, pair)

            def down(q0, n, idx, j, w):
                split(q0 + 2, 0)
                panels_after_first(n, lambda j0, i: split(q0 + j0 + 2, i), dve)
                gate(idx, j, w)
                for k, m in enumerate(ORDER):
                    dve.wait_ge(out_done, KD * idx + k + 1)
                    for cond, cols in ((0, CTX), (1, LAT)):
                        last = nc.vector.scalar_tensor_tensor(h[:, m, cols], ps[:, m, cols], gT[:, m, cond:cond + 1],
                                                              h[:, m, cols], ALU.mult, ALU.add)
                    last.then_inc(h_done, 1)

            dve.wait_ge(vecT_pe, 1)
            for layer in range(DEPTH):
                nc.vector.tensor_copy(mbT[:, layer * 72:layer * 72 + 72], ps[:, 1, 128 * layer:128 * layer + 72])
            nc.vector.tensor_copy(ngT[:, :], ps[:, 1, 256:256 + 48])
            nc.vector.tensor_copy(vgT[:, :], ps[:, 1, 384:384 + KS]).then_inc(vecT_done, 1)
            dve.wait_ge(vecT_done, 1)
            for k, m in enumerate(ORDER):
                dve.wait_ge(xT_pe, k + 1)
                nc.vector.tensor_copy(h[:, m, :], ps[:, 2 + k % 4, 0:T]).then_inc(h_done, 1)
            for b in range(MOD_FIRST):
                mod_out(b, 0)
            vectors(0, (0, 0))
            split(0, 0)
            split(1, 0)
            make_x(0)
            mod_out(MOD_FIRST, 0)
            mod_out(MOD_FIRST + 1, 0)
            ffn(0)
            dve.wait_ge(tab_in, 16 * 11)
            for n in (0, 2):
                link(nc.vector.tensor_scalar(gain[:, n, :], gain[:, n, :], HD ** -0.5, None, ALU.mult))
            down(Q_F[0] + 2 * GU, GU, 0, (0, 0), 0.5)
            vectors(1, (0, 1))
            make_x(1)
            split(Q_IN0 + 1, 0)

            for g in range(9):
                if g not in (4, 5):
                    m = g if g < 4 else g - 2
                    nh = 4 if g < 8 else 2
                    w = nh * HD
                    dve.wait_ge(hsq_done, m + 1)
                    nc.vector.tensor_reduce(hms[:, 0:TT * nh],
                                            hsq_view(w)[:, :, :].rearrange("p a (h d) -> p (a h) d", d=HD),
                                            AX.X, ALU.add).then_inc(hms_sum, 1)
                    dve.wait_ge(hms_sum, m + 1)
                    nc.vector.tensor_scalar(hms[:, 0:TT * nh], hms[:, 0:TT * nh], 1.0 / HD, EPS, ALU.mult, ALU.add) \
                        .then_inc(hms_done, 1)
                    dve.wait_ge(hrs_done, m + 1)
                    if g < 2:
                        dst, gn = q_na[:, :, 4 * g:4 * g + 4, :], 0
                    elif g < 4:
                        dst, gn = k_na[:, :, 4 * g - 8:4 * g - 4, :], 1
                    elif g < 8:
                        dst, gn = qk_g[:, :, g - 6:g + 1:2, :], 2
                    else:
                        dst, gn = qk_g[:, :, NH:NH + 2, :], 3
                    for t in range(TT):
                        last = nc.vector.tensor_tensor(
                            dst[:, t], ps[:, QBANK[g % 2][t], 0:w].rearrange("p (h d) -> p h d", d=HD),
                            hrs[:, t * nh:(t + 1) * nh, None].to_broadcast([P, nh, HD]), ALU.mult)
                    link(last)
                    for t in range(TT):
                        last = nc.vector.tensor_tensor(dst[:, t], dst[:, t],
                                                       gain[:, gn, None, :].to_broadcast([P, nh, HD]), ALU.mult)
                    last.then_inc(qkv_dve, 1)
                else:
                    dve.sem_inc(qkv_dve, 1)
                split(Q_IN0 + g + 2, 0)
            dve.wait_ge(qkv_dve, 9)
            rt = rot_view()
            for t in (1, 2):
                xv = qk_g[:, t, :, :]
                x5 = xv.rearrange("p h (a b d) -> p b h a d", a=2, b=2)
                r5 = rt.rearrange("p h (a b d) -> p b h a d", a=2, b=2)
                s5 = ropeT[:, 1, t - 1, :].rearrange("p (a b d) -> p b a d", a=2, b=2)
                for part in range(2):
                    last = nc.vector.tensor_tensor(r5[:, part], x5[:, 1 - part],
                                                   s5[:, part, None].to_broadcast([P, NH + 2, 2, 16]), ALU.mult)
                link(last)
                link(nc.vector.tensor_tensor(xv, xv, ropeT[:, 0, t - 1, None, :].to_broadcast([P, NH + 2, HD]), ALU.mult))
                last = nc.vector.tensor_tensor(xv, xv, rt, ALU.add)
                link(last)
            dve.sem_inc(rope_done, 1)
            for g, (dst, n) in enumerate(tr_groups()):
                if g % 2 == 1:
                    dve.wait_ge(tr_pe, g + 1)
                    nc.vector.tensor_copy(dst, ps[:, g % 8, 0:n]).then_inc(tr_dve, 1)

            def top(b):
                n = NCTX if b % 3 == 0 else T
                dve.wait_ge(s_pe, b + 1)
                if b >= 3:
                    dve.wait_ge(exp_done, b - 2)
                nc.vector.tensor_reduce(nmax[:, b % 3:b % 3 + 1], ps[:, b % 3, 0:n], AX.X, ALU.max, negate=True) \
                    .then_inc(nmax_done, 1)

            def normalise(b):
                n = NCTX if b % 3 == 0 else T
                dve.wait_ge(exp_done, b + 1)
                link(nc.vector.reciprocal(rinv[:, b % 3:b % 3 + 1], rsum[:, b % 3:b % 3 + 1]))
                nc.vector.tensor_scalar(prob[:, b % 3, 0:n], prob[:, b % 3, 0:n], rinv[:, b % 3:b % 3 + 1], None,
                                        ALU.mult).then_inc(prob_done, 1)

            def o_lo(pair):
                dve.wait_ge(oh_done, pair + 1)
                nc.vector.tensor_tensor(x_lo[:, pair, :], ps[:, 6 + pair % 2, 0:T], x_hi[:, pair, :].bitcast(F32),
                                        ALU.subtract).then_inc(ol_done, 1)

            for b in range(48 + 1):
                if b < 48:
                    top(b)
                if b >= 1:
                    normalise(b - 1)
                if b >= 12 and (b - 12) % 6 == 0:
                    o_lo((b - 12) // 6)
            o_lo(7)
            down(Q_OUT0, KD // 2, 1, (0, 1), 1.0)
            vectors(2, (0, 2))
            make_x(2)
            split(Q_F[1] + 1, 0)
            ffn(1)
            down(Q_F[1] + 2 * GU, GU, 2, (0, 2), 0.5)
            vectors(3, (1, 0))
            make_x(3)
            split(Q_F[2] + 1, 0)
            ffn(2)
            down(Q_F[2] + 2 * GU, GU, 3, (1, 0), 0.5)
            vectors(4, (1, 1))
            make_x(4)
            split(Q_V + 1, 0)
            for g in range(8):
                split(Q_V + g + 2, 0)
            dve.wait_ge(vss_done, 8)
            link(nc.vector.tensor_reduce(ms[:, :], vss[:, :, :], AX.X, ALU.add))
            nc.vector.tensor_scalar(ms[:, :], ms[:, :], 1.0 / SW, EPS, ALU.mult, ALU.add).then_inc(vms_done, 1)
            dve.wait_ge(vrs_done, 1)
            dve.wait_ge(wsT_done, 2)
            for t in range(TT):
                last = nc.vector.tensor_scalar(wsn[:, t, :, :], wsT[:, :, :], rs[:, t:t + 1], None, ALU.mult)
            last.then_inc(wsn_done, 1)
            dve.wait_ge(ws_in, 32)
            for d in range(KS):
                dve.wait_ge(sv_pe, d + 1)
                nc.vector.scalar_tensor_tensor(svb[:, d, :].rearrange("p (a t) -> p a t", a=TT),
                                               ps[:, d % 8, 0:T].rearrange("p (a t) -> p a t", a=TT), vgT[:, d:d + 1],
                                               bsb[:, d // 2, None, :].to_broadcast([P, TT, P]), ALU.mult, ALU.add) \
                    .then_inc(sv_done, 1)
            dve.wait_ge(sv_done, KS)
            for g in range(8):
                done = UPAIR + g
                dve.wait_ge(silu_done, done + 1)
                nc.vector.tensor_tensor(tmp[:, 0:2, :], tmp[:, 0:2, :], svb[:, 2 * g:2 * g + 2, :], ALU.mult) \
                    .then_inc(mul_done, 1)
                dve.wait_ge(acth_done, done + 1)
                nc.vector.tensor_tensor(act_lo[:, 2 * g:2 * g + 2, :], tmp[:, 0:2, :],
                                        act_hi[:, 2 * g:2 * g + 2, :].bitcast(F32), ALU.subtract).then_inc(actl_done, 1)
                split(Q_U + g + 2, 0)
            down(Q_OUT1, KS // 2, 4, (1, 1), 1.0)
            vectors(5, (1, 2))
            make_x(5)
            split(Q_F[3] + 1, 0)
            ffn(3)
            down(Q_F[3] + 2 * GU, GU, 5, (1, 2), 0.5)

        @block.tensor
        def _(pe):
            mm = nc.tensor.matmul

            def three(out, w, cols, xs, start, stop):
                mm(out, w[0][:, cols], xs[0], start=start, stop=False)
                mm(out, w[0][:, cols], xs[1], start=False, stop=False)
                return mm(out, w[1][:, cols], xs[0], start=False, stop=stop)

            def slot(q0):
                return w_hi[q0 % 2], w_lo[q0 % 2]

            def mod_mm(b0, i):
                pe.wait_ge(mraw_in[b0 % 2], 16 * (b0 // 2 + 1 + i))
                if b0 >= 2:
                    pe.wait_ge(mod_done, b0 + 2 * i - 1)
                for a in range(2):
                    for k in range(KD):
                        last = mm(ps[:, 6 + b0 % 2, 2 * a:2 * a + 2], mraw[b0 % 2][:, k, P * a:P * a + P], cT[:, k, :],
                                  start=(k == 0), stop=(k == KD - 1))
                last.then_inc(mod_pe, 1)

            def feature_major(q0, i, bank, first_x=None):
                pe.wait_ge(lo_done, q0 + 2 * i + 1)
                for a in range(2):
                    for k in range(KD):
                        if first_x is not None and a == 0:
                            pe.wait_ge(x_done, first_x + k + 1)
                        last = three(ps[:, bank + a, 0:T], slot(q0), slice(256 * k + P * a, 256 * k + P * a + P),
                                     (x_hi[:, k, :], x_lo[:, k, :]), k == 0, k == KD - 1)
                last.then_inc(pe_done, 1)

            def token_major(q0, i, banks, first_x=None):
                pe.wait_ge(lo_done, q0 + 2 * i + 1)
                hi, lo = slot(q0)
                for t in range(TT):
                    tok = slice(P * t, P * t + P)
                    out = ps[:, banks[t], 0:256]
                    for k in range(KD):
                        if first_x is not None and t == 0:
                            pe.wait_ge(x_done, first_x + k + 1)
                        cols = slice(256 * k, 256 * k + 256)
                        mm(out, x_hi[:, k, tok], hi[:, cols], start=(k == 0), stop=False)
                        mm(out, x_hi[:, k, tok], lo[:, cols], start=False, stop=False)
                        last = mm(out, x_lo[:, k, tok], hi[:, cols], start=False, stop=(k == KD - 1))
                last.then_inc(pe_done, 1)

            def norm(n, last_sq_bank=None):
                pe.wait_ge(acc_done, 6 * n + 6)
                pe.wait_ge(sq_done, KD * n + KD)
                for t in range(TT):
                    tok = slice(P * t, P * t + P)
                    mm(ps[:, 4, t:t + 1], sqsum[:, tok], ones[:, 0:1], start=True, stop=False)
                    last = mm(ps[:, 4, t:t + 1], sq[:, 1, tok], ones[:, 0:1], start=False, stop=True)
                last.then_inc(stat_done, 1)
                pe.wait_ge(diag_done, n + 1)
                mm(ps[:, 5, 0:T], ones[:, :], sqsum[:, :], start=True, stop=True).then_inc(rb_done, 1)

            def ffn(f, n):
                q = Q_F[f]

                def pair(g0, i, b):
                    done = PAIRS[f] + g0 + i
                    first = g0 == 0
                    if not first:
                        pe.wait_ge(silu_done, done)
                    feature_major(q + 2 * g0, i, 0, KD * n if first else None)
                    if b is not None:
                        mod_mm(b, i)
                    if not first:
                        pe.wait_ge(mul_done, done)
                    feature_major(q + 2 * g0 + 1, i, 2)
                    if b is not None:
                        mod_mm(b + 1, i)
                loop_pairs(f, pe, pair)

            def down(q0, n, idx, hi, lo, ready=None):
                def panel(j0, i, first=False, final=False):
                    pe.wait_ge(lo_done, q0 + j0 + 2 * i + 1)
                    if ready is not None and (first or final):
                        ready(pe, first)
                    for k, m in enumerate(ORDER):
                        if first and k == 4 and ready is not None:
                            ready(pe, None)
                        for c in range(2):
                            kk = slice(2 * j0 + c, 2 * j0 + c + 1) if isinstance(i, int) else bass.ds(2 * j0 + c + 4 * i, 1)
                            last = three(ps[:, m, 0:T], slot(q0 + j0), slice(1024 * c + P * m, 1024 * c + P * m + P),
                                         (hi[:, kk, :], lo[:, kk, :]), first and c == 0, final and c == 1)
                        if final:
                            last.then_inc(out_done, 1)
                    if not final:
                        last.then_inc(pe_done, 1)
                    else:
                        pe.wait_ge(out_done, KD * idx + KD)
                        pe.sem_inc(pe_done, 1)

                panel(0, 0, first=True)
                panels_after_first(n, panel, pe)
                panel(n - 1, 0, final=True)

            def ready_ffn(f):
                def waits(eng, first):
                    if first:
                        eng.wait_ge(actl_done, PAIRS[f] + GU - 1)
                        eng.wait_ge(mod_done, MOD_AT[f + 1] if f < 3 else MOD_AT[3])
                    elif first is None:
                        eng.wait_ge(mul_done, PAIRS[f] + GU)
                    else:
                        eng.wait_ge(actl_done, PAIRS[f] + GU)
                return waits

            pe.wait_ge(const_in, 16)
            pe.wait_ge(c_in, 32)
            nc.tensor.transpose(ps[:, 0, 0:16], vec[0:16, 0, :], ident[0:16, 0:16]).then_inc(c_pe, 1)
            pe.wait_ge(vec_in, 16 * 4)
            for r, n in ((1, 72), (2, 72), (3, 48), (4, KS)):
                last = nc.tensor.transpose(ps[:, 1, 128 * (r - 1):128 * (r - 1) + n], vec[0:n, r, :], ident[0:n, 0:n])
            last.then_inc(vecT_pe, 1)
            pe.wait_ge(x_in, 32)
            for k, m in enumerate(ORDER):
                if k >= 4:
                    pe.wait_ge(h_done, k - 3)
                for t in range(TT):
                    last = nc.tensor.transpose(ps[:, 2 + k % 4, P * t:P * t + P], x_tok[:, t, P * m:P * m + P], ident[:, :])
                last.then_inc(xT_pe, 1)
            pe.wait_ge(ones_set, 2)
            pe.wait_ge(c_done, 1)
            for b in range(MOD_FIRST):
                mod_mm(b, 0)
            pe.wait_ge(h_done, KD)
            norm(0)
            mod_mm(MOD_FIRST, 0)
            mod_mm(MOD_FIRST + 1, 0)
            ffn(0, 0)
            down(Q_F[0] + 2 * GU, GU, 0, act_hi, act_lo, ready_ffn(0))
            norm(1)

            for g in range(9):
                if g >= 2:
                    pe.wait_ge(qkv_dve, g - 1)
                    if g - 2 >= 4:
                        pe.wait_ge(qkv_act, min(g - 5, 2))
                token_major(Q_IN0 + g, 0, QBANK[g % 2], KD if g == 0 else None)
            pe.wait_ge(qkv_dve, 9)
            pe.wait_ge(qkv_act, 3)
            pe.wait_ge(rope_done, 1)
            pe.wait_ge(tab_in, 16 * 11)
            groups = ([(q_na, n, None) for n in range(4)] + [(k_na, n, kc_na[:, P * n:P * n + P]) for n in range(4)]
                      + [(qk_g, n, None) for n in range(4)] + [(qk_g, 4, kc_g[:, :])])
            for g, (src, n, cache) in enumerate(groups):
                if g >= 8:
                    pe.wait_ge((tr_act, tr_dve)[g % 2], (g - 8) // 2 + 1)
                for t in range(TT):
                    last = nc.tensor.transpose(ps[:, g % 8, P * t:P * t + P],
                                               src[:, t, 2 * n:2 * n + 2, :].rearrange("p h d -> p (h d)"), ident[:, :])
                if cache is not None:
                    last = nc.tensor.transpose(ps[:, g % 8, T:T + P], cache, ident[:, :])
                last.then_inc(tr_pe, 1)
            pe.wait_ge(tr_act, 7)
            pe.wait_ge(tr_dve, 6)
            pe.wait_ge(bias_done, 2)

            def scores(b):
                hh, kind = divmod(b, 3)
                if hh < NH:
                    base, qT, kT = HD * (hh % 2), qT_na[:, hh // 2, :], kT_na[:, hh // 2, :]
                else:
                    g = hh - NH
                    base, qT, kT = HD * (g // 4), qT_g[:, g % 4, :], kT_g[:, :]
                rows = slice(base, base + HD)
                if b >= 3:
                    pe.wait_ge(exp_done, b - 2)
                if kind == 0:
                    mm(ps[:, b % 3, 0:P], qT[rows, 0:P], kT[rows, 0:P], start=True, stop=True).then_inc(s_pe, 1)
                else:
                    na = hh < NH
                    last = mm(ps[:, b % 3, 0:T], qT[rows, P * kind:P * kind + P], kT[rows, P:P + T], start=True, stop=not na)
                    if na:
                        last = mm(ps[:, b % 3, 0:NLAT], perm[:, :], bias[:, kind - 1, hh, :], start=False, stop=True)
                    last.then_inc(s_pe, 1)

            def p_transposes(b):
                pe.wait_ge(prob_done, b + 1)
                if b >= 3:
                    pe.wait_ge(pT_done, b - 2)
                for k in range(1 if b % 3 == 0 else 3):
                    last = nc.tensor.transpose(ps[:, 3 + b % 3, P * k:P * k + P], prob[:, b % 3, P * k:P * k + P], ident[:, :])
                last.then_inc(pT_pe, 1)

            def values(hh):
                pe.wait_ge(pT_done, 3 * hh + 3)
                pair, half = divmod(hh, 2)
                if hh >= 4 and half == 0:
                    pe.wait_ge(ol_done, pair - 1)
                out = ps[HD * half:HD * half + HD, 6 + pair % 2, :]
                if hh < NH:
                    v, cache, cols = v_na, vc_na, slice(HD * hh, HD * hh + HD)
                else:
                    kv = (hh - NH) // 4
                    v, cache, cols = vg_, vc_g, slice(HD * kv, HD * kv + HD)
                mm(out[:, 0:P], v[:, 0, cols], pT_ctx[:, hh % 2, :], start=True, stop=True)
                mm(out[:, P:T], v[:, 1, cols], pT_lat[:, hh % 2, 0, :], start=True, stop=False)
                mm(out[:, P:T], v[:, 2, cols], pT_lat[:, hh % 2, 1, :], start=False, stop=False)
                mm(out[:, P:T], cache[:, cols], pT_lat[:, hh % 2, 2, :], start=False, stop=True).then_inc(o_pe, 1)

            for b in range(48 + 4):
                if b < 48:
                    scores(b)
                if 2 <= b < 50:
                    p_transposes(b - 2)
                if b >= 6 and b % 3 == 0:
                    values(b // 3 - 2)

            def ready_attn(eng, first):
                if first:
                    eng.wait_ge(ol_done, 8)

            down(Q_OUT0, KD // 2, 1, x_hi, x_lo, ready_attn)
            norm(2)
            ffn(1, 2)
            down(Q_F[1] + 2 * GU, GU, 2, act_hi, act_lo, ready_ffn(1))
            norm(3)
            ffn(2, 3)
            down(Q_F[2] + 2 * GU, GU, 3, act_hi, act_lo, ready_ffn(2))
            norm(4)
            for g in range(8):
                if g >= 2:
                    pe.wait_ge(gelu_v, g - 1)
                token_major(Q_V + g, 0, QBANK[g % 2], KD * 4 if g == 0 else None)
                if g == 0:
                    pe.wait_ge(ws_in, 32)
                    for a in range(2):
                        if a:
                            pe.wait_ge(x_done, KD * 5)
                        for n in range(4):
                            last = nc.tensor.transpose(ps[:, 4 + a, P * n:P * n + P], ws_row[:, 4 * a + n, :], ident[:, :])
                        last.then_inc(ws_pe, 1)
            pe.wait_ge(gelu_v, 8)
            pe.wait_ge(wsn_done, 1)
            for d in range(KS):
                if d >= 8:
                    pe.wait_ge(sv_done, d - 7)
                for t in range(TT):
                    last = mm(ps[:, d % 8, P * t:P * t + P], v_tok[:, t, P * d:P * d + P], wsn[:, t, d // 2, :],
                              start=True, stop=True)
                last.then_inc(sv_pe, 1)
            pe.wait_ge(sv_done, KS)
            for g in range(8):
                if g >= 2:
                    pe.wait_ge(silu_done, UPAIR + g - 1)
                feature_major(Q_U + g, 0, 2 * (g % 2))

            def ready_sgu(eng, first):
                if first:
                    eng.wait_ge(actl_done, UPAIR + 7)
                elif first is None:
                    eng.wait_ge(silu_done, UPAIR + 8)
                else:
                    eng.wait_ge(actl_done, UPAIR + 8)

            down(Q_OUT1, KS // 2, 4, act_hi, act_lo, ready_sgu)
            norm(5)
            ffn(3, 5)
            down(Q_F[3] + 2 * GU, GU, 5, act_hi, act_lo, ready_ffn(3))
            for k, m in enumerate(ORDER):
                pe.wait_ge(h_done, KD * 6 + k + 1)
                for t in range(TT):
                    last = nc.tensor.transpose(ps[:, m, P * t:P * t + P], h[:, m, P * t:P * t + P], ident[:, :])
                last.then_inc(yT_pe, 1)


PAIRS = (0, GU, 2 * GU, 3 * GU + 8)
UPAIR = 3 * GU
QBANK = ((0, 1, 2), (3, 6, 7))

_NAMES = ['x_prompt', 'x_sample', 'cache_na_k', 'cache_na_v', 'cache_gqa_k', 'cache_gqa_v', 'c', 'c_ctx', 'norm_g', 'mod_w',
          'mod_b', 'ffn1_w_gu', 'ffn1_w_down', 'ffn2_w_gu', 'ffn2_w_down', 'attn_w_in', 'attn_w_out', 'na_q_g', 'na_k_g',
          'na_rpb', 'gqa_q_g', 'gqa_k_g', 'sgu_w_in', 'sgu_v_g', 'sgu_w_s', 'sgu_b_s', 'sgu_w_out']
_OUTS = [(1, NCTX, D), (1, NLAT, D), (1, 1, NCTX, NH, HD), (1, 1, NCTX, NH, HD), (1, 1, NCTX, 2, HD), (1, 1, NCTX, 2, HD)]


def shape_constants():
    t = np.arange(NLAT)
    half = HD // 2
    freqs = 10000.0 ** (-np.arange(0, half, 2, dtype=np.float64) / half)
    rope = np.zeros((2, NLAT, HD), np.float32)
    for a, pos in enumerate((t // GRID, t % GRID)):
        ang = pos[:, None] * freqs[None, :]
        for b in range(2):
            at = slice(a * half + b * 16, a * half + b * 16 + 16)
            rope[0, :, at] = np.cos(ang)
            rope[1, :, at] = np.sin(ang) * (1 if b else -1)
    j = np.arange(P)
    qcol = (GRID - 1 - j % GRID)[:, None]
    start = np.clip(qcol - 8, 0, GRID - 16)
    kcol = np.arange(GRID)[None, :]
    mask = np.where((kcol >= start) & (kcol < start + 16), 0.0, -1e30).astype(np.float32)
    consts = np.zeros((2, P, P), np.float32)
    consts[0, j, j] = 1.0
    consts[1, j, GRID * (j // GRID) + GRID - 1 - j % GRID] = 1.0
    return rope, mask, consts


def kernel(**inputs):
    import concourse.bacc as bacc
    from concourse.bass_utils import run_bass_kernel_spmd as run

    nc = bacc.Bacc("TRN2", target_bir_lowering=False, num_devices=1)
    arrays = {n: np.ascontiguousarray(inputs[n]) for n in _NAMES}
    for n, a in zip(("rope_table", "window_mask", "consts"), shape_constants()):
        arrays[n] = a
    ins = [nc.dram_tensor(n, a.shape, F32, kind="ExternalInput").ap() for n, a in arrays.items()]
    outs = [nc.dram_tensor(f"out_{i}", s, F32, kind="ExternalOutput").ap() for i, s in enumerate(_OUTS)]
    toep = nc.dram_tensor("toep_scratch", (NH * NDR, TOEP), F32, kind="Internal").ap()
    build(nc, ins, outs, toep)
    r = run(nc, [arrays], core_ids=[0])
    return tuple(r.results[0][f"out_{i}"] for i in range(len(_OUTS)))
```

```python
from contextlib import ExitStack

import numpy as np
import concourse.bass as bass
from concourse import mybir

ALU = mybir.AluOpType
ACT = mybir.ActivationFunctionType
AX = mybir.AxisListType
F32 = mybir.dt.float32
F32R = mybir.dt.float32r

P = 128
D = 1024
KD = D // P
NCTX, NLAT = 128, 256
T = NCTX + NLAT
TT = T // P
CTX, LAT = slice(0, NCTX), slice(NCTX, T)
DEPTH = 2
F = 2816
GU = F // 256
KF = F // P
NMOD = 9
HD = 64
NH = 8
KVW = 128
GRID = 64
ROWS = NLAT // GRID
SW = 2 * D
KS = SW // P
NG = 8
EPS = 1e-6
PW = 2048
MB = 256
NMB = NMOD * D // MB
MOD_FIRST = 2 * D // MB
TOEP = 2 * GRID - 1
NDR = 15
BANDC = 31
ORDER = (4, 5, 6, 7, 0, 1, 2, 3)

Q_F = (0, 46, 79, 136)
Q_IN0, Q_OUT0 = 33, 42
Q_V, Q_U, Q_OUT1 = 112, 120, 128
Q_END = 169
MOD_GU = GU - 1
MOD_DN = (8, 8, 8)
MOD_IN, MOD_OUT, MOD_SG = 4, 2, 4
MOD_AT = (8, 32, 50)
MOD_M = MOD_AT[0] + MOD_GU + MOD_DN[0]
MOD_V = MOD_AT[2] + MOD_GU + MOD_DN[2]
SPARE = T


def outs_until(block):
    sizes = [MOD_FIRST] + [1] * MOD_GU + [MOD_DN[0], MOD_IN, MOD_OUT] + [1] * MOD_GU + [MOD_DN[1]] + [1] * MOD_GU + [MOD_DN[2], MOD_SG]
    n = have = 0
    while have < block:
        have += sizes[n]
        n += 1
    return n


def build(nc, t_in, t_out, toep_dram):
    (x_prompt, x_sample, ck_na, cv_na, ck_g, cv_g, c, c_ctx, norm_g, mod_w, mod_b, w_gu1, w_dn1, w_gu2, w_dn2,
     w_attn, w_o, na_q_g, na_k_g, na_rpb, g_q_g, g_k_g, w_sgu, v_g, w_s, b_s, w_sgo, rope, mask, consts) = t_in
    y_p, y_s, o_nak, o_nav, o_gk, o_gv = t_out

    ctx = ExitStack()
    with ctx:
        def sb(name, shape, dt=F32, scope=ctx):
            return scope.enter_context(nc.sbuf_tensor(name, shape, dt))

        def sem(name):
            return ctx.enter_context(nc.semaphore(name))

        h = sb("h", [P, KD, T])
        raw = [sb(f"raw{i}", [P, PW]) for i in range(2)]
        w_hi = [sb(f"w_hi{i}", [P, PW], F32R) for i in range(2)]
        w_lo = [sb(f"w_lo{i}", [P, PW], F32R) for i in range(2)]
        mraw = [sb(f"mraw{i}", [P, KD, MB]) for i in range(2)]
        tmp = sb("tmp", [P, 4, T])
        with ExitStack() as s:
            macc = sb("macc", [P, 2, 2, MB], scope=s)
        sq = sb("sq", [P, 4, T])
        sqsum = sb("sqsum", [P, T])
        ident = sb("ident", [P, P])
        ones = sb("ones", [P, P])
        modT = sb("modT", [P, DEPTH * NMOD * KD, 2])
        mbT = sb("mbT", [P, DEPTH * NMOD * KD])
        ngT = sb("ngT", [P, DEPTH * 3 * KD])
        vgT = sb("vgT", [P, KS])
        cT = sb("cT", [P, KD, 2])
        aT = sb("aT", [P, KD, 2])
        gT = sb("gT", [P, KD, 2])
        ms = sb("ms", [P, TT])
        rs = sb("rs", [P, TT])
        mhalf = sb("mhalf", [P, 16])
        hms = sb("hms", [P, 12])
        hrs = sb("hrs", [P, 12])
        nmax = sb("nmax", [P, 3])
        rsum = sb("rsum", [P, 3])
        rinv = sb("rinv", [P, 3])
        vss = sb("vss", [P, TT, KD])

        with ExitStack() as s:
            y_tok = sb("y_tok", [P, TT, D], scope=s)
        with ExitStack() as s:
            mod_row = sb("mod_row", [2, MOD_FIRST * MB], scope=s)
        x_hi = sb("x_hi", [P, KD, T], F32R)
        x_lo = sb("x_lo", [P, KD, T], F32R)

        with ExitStack() as s:
            svb = sb("svb", [P, KS, T], scope=s)
        with ExitStack() as s:
            bias = sb("bias", [P, 2, NH, NLAT], scope=s)
            kc_na = sb("kc_na", [P, NH * HD], scope=s)
            vc_na = sb("vc_na", [P, NH * HD], scope=s)
            kc_g = sb("kc_g", [P, KVW], scope=s)
            vc_g = sb("vc_g", [P, KVW], scope=s)
            ropeT = sb("ropeT", [P, 2, 2, HD], scope=s)
            gain = sb("gain", [P, 4, HD], scope=s)
            maskT = sb("maskT", [P, GRID], scope=s)
            perm = sb("perm", [P, P], scope=s)
        sb("region_d", [P, KS, T])

        with ExitStack() as s:
            x_tok = sb("x_tok", [P, TT, D], scope=s)
            vec = sb("vec", [P, 5, P], scope=s)
            toep = sb("toep", [NH * NDR, TOEP], scope=s)
            mfirst = sb("mfirst", [P, MOD_FIRST - 2, KD, MB], scope=s)
        with ExitStack() as s:
            q_na = sb("q_na", [P, TT, NH, HD], scope=s)
            k_na = sb("k_na", [P, TT, NH, HD], scope=s)
            qk_g = sb("qk_g", [P, TT, NH + 2, HD], scope=s)
            v_na = sb("v_na", [P, TT, NH * HD], scope=s)
            vg_ = sb("vg_", [P, TT, KVW], scope=s)
            qT_na = sb("qT_na", [P, 4, T], scope=s)
            kT_na = sb("kT_na", [P, 4, T + P], scope=s)
            qT_g = sb("qT_g", [P, 4, T], scope=s)
            kT_g = sb("kT_g", [P, T + P], scope=s)
            prob = sb("prob", [P, 3, T], scope=s)
            pT_lat = sb("pT_lat", [P, 2, 3, NLAT], scope=s)
            pT_ctx = sb("pT_ctx", [P, 2, NCTX], scope=s)
        with ExitStack() as s:
            v_tok = sb("v_tok", [P, TT, SW], scope=s)
            ws_row = sb("ws_row", [P, NG, P], scope=s)
            wsT = sb("wsT", [P, NG, P], scope=s)
            wsn = sb("wsn", [P, TT, NG, P], scope=s)
            bsb = sb("bsb", [P, NG, P], scope=s)
            vsq = sb("vsq", [P, TT, 256], scope=s)
        act_hi = sb("act_hi", [P, KF, T], F32R)
        act_lo = sb("act_lo", [P, KF, T], F32R)
        ps = ctx.enter_context(nc.psum_tensor("ps", [P, 8, 512], F32))

        raw_in = [sem(f"raw_in{i}") for i in range(2)]
        hi_done = sem("hi_done")
        lo_done = sem("lo_done")
        pe_done = sem("pe_done")
        mraw_in = [sem(f"mraw_in{i}") for i in range(2)]
        mfirst_in = [sem(f"mfirst_in{i}") for i in range(MOD_FIRST - 2)]
        mod_pe = sem("mod_pe")
        row_done = sem("row_done")
        rowT_pe = sem("rowT_pe")
        mchain = sem("mchain")
        macc_done = sem("macc_done")
        msum_done = sem("msum_done")
        mod_done = sem("mod_done")
        silu_done = sem("silu_done")
        mul_done = sem("mul_done")
        acth_done = sem("acth_done")
        actl_done = sem("actl_done")
        out_done = sem("out_done")
        h_done = sem("h_done")
        sq_done = sem("sq_done")
        acc_done = sem("acc_done")
        stat_done = sem("stat_done")
        ms_done = sem("ms_done")
        rs_done = sem("rs_done")
        diag_done = sem("diag_done")
        rb_done = sem("rb_done")
        t_done = sem("t_done")
        xm_done = sem("xm_done")
        xh_done = sem("xh_done")
        x_done = sem("x_done")
        mvec = sem("mvec")
        x_in = sem("x_in")
        vec_in = sem("vec_in")
        c_in = sem("c_in")
        const_in = sem("const_in")
        ones_set = sem("ones_set")
        zero_set = sem("zero_set")
        vecT_pe = sem("vecT_pe")
        vecT_done = sem("vecT_done")
        c_pe = sem("c_pe")
        c_done = sem("c_done")
        xT_pe = sem("xT_pe")
        toep_in = sem("toep_in")
        toep_out = sem("toep_out")
        bias_in = sem("bias_in")
        bias_done = sem("bias_done")
        tab_in = sem("tab_in")
        gain_done = sem("gain_done")
        hsq_done = sem("hsq_done")
        hms_sum = sem("hms_sum")
        hms_done = sem("hms_done")
        hrs_done = sem("hrs_done")
        gained = sem("gained")
        dve_self = sem("dve_self")
        act_self = sem("act_self")
        qkv_act = sem("qkv_act")
        qkv_dve = sem("qkv_dve")
        rope_done = sem("rope_done")
        tr_pe = sem("tr_pe")
        tr_act = sem("tr_act")
        tr_dve = sem("tr_dve")
        s_pe = sem("s_pe")
        nmax_done = sem("nmax_done")
        exp_done = sem("exp_done")
        prob_done = sem("prob_done")
        pT_pe = sem("pT_pe")
        pT_done = sem("pT_done")
        o_pe = sem("o_pe")
        oh_done = sem("oh_done")
        ol_done = sem("ol_done")
        ws_in = sem("ws_in")
        ws_pe = sem("ws_pe")
        wsT_done = sem("wsT_done")
        gelu_v = sem("gelu_v")
        vss_done = sem("vss_done")
        vms_done = sem("vms_done")
        vrs_done = sem("vrs_done")
        wsn_done = sem("wsn_done")
        sv_pe = sem("sv_pe")
        sv_done = sem("sv_done")
        yT_pe = sem("yT_pe")
        y_done = sem("y_done")
        stored = sem("stored")

        block = ctx.enter_context(nc.Block())

        dve_steps = [0]

        def gu_src(w_gu, layer, g0, i, up):
            v = w_gu[layer].rearrange("(k p) n -> p k n", p=P)
            return v[:, :, bass.ds(F * up + 256 * (g0 + i), 256)]

        def dn_src(w, j0, i):
            v = w.rearrange("(j c p) n -> p j c n", c=2, p=P)
            return v[:, bass.ds(j0 + 2 * i, 1), :, :]

        def col_src(w, g):
            return w.rearrange("(k p) n -> p k n", p=P)[:, :, 256 * g:256 * g + 256]

        FFN = [(w_gu1, w_dn1, 0), (w_gu2, w_dn2, 0), (w_gu1, w_dn1, 1), (w_gu2, w_dn2, 1)]

        def loop_pairs(f, eng, pair, straight=1, first=0):
            block = lambda g: MOD_AT[f] + g - 1 if f < 3 and g else None
            for g in range(first, straight):
                pair(g, 0, block(g))
            its = (GU - straight) // 2
            with eng.Fori(0, its) as i:
                pair(straight, 2 * i, block(straight))
                pair(straight + 1, 2 * i, block(straight + 1))
            for g in range(straight + 2 * its, GU):
                pair(g, 0, block(g))

        def steps_beside_blocks(eng, first, blocks, end, step):
            for lo, hi, beside in ((first, first + blocks, True), (first + blocks, end, False)):
                its = (hi - lo) // 2
                if its > 1:
                    with eng.Fori(0, its) as i:
                        step(lo, i, beside)
                        step(lo + 1, i, beside)
                    lo += 2 * its
                for j in range(lo, hi):
                    step(j, 0, beside)

        def hsq_view(w):
            return tmp[:, 0:2, :].rearrange("p a t -> p (a t)")[:, 0:TT * w].rearrange("p (a w) -> p a w", a=TT)

        def rot_view():
            return tmp[:, 0:2, :].rearrange("p a t -> p (a t)")[:, 0:(NH + 2) * HD].rearrange("p (h d) -> p h d", d=HD)

        def heads_of(g):
            if g < 2:
                return q_na[:, :, 4 * g:4 * g + 4, :], 4, 0
            if g < 4:
                return k_na[:, :, 4 * g - 8:4 * g - 4, :], 4, 1
            if g < 8:
                return qk_g[:, :, g - 6:g + 1:2, :], 4, 2
            return qk_g[:, :, NH:NH + 2, :], 2, 3

        def tr_groups():
            return ([(qT_na[:, n, :], T) for n in range(4)] + [(kT_na[:, n, :], T + P) for n in range(4)]
                    + [(qT_g[:, n, :], T) for n in range(4)] + [(kT_g[:, :], T + P)])

        @block.sync
        def _(sp):
            def panel(q0, i, src, shape):
                if q0 >= 2:
                    sp.wait_ge(lo_done, q0 + 2 * i - 1)
                dst = raw[q0 % 2][:, :].rearrange(shape[0], **shape[1])
                sp.dma_start(dst, src).then_inc(raw_in[q0 % 2], 16)

            KN = ("p (k n) -> p k n", dict(k=KD))
            JCN = ("p (j c n) -> p j c n", dict(j=1, c=2))

            def mod_block(b0, ii):
                if b0 >= MOD_FIRST + 2:
                    sp.wait_ge(macc_done, b0 + ii - MOD_FIRST - 1)
                elif b0 >= MOD_FIRST:
                    sp.wait_ge(mod_pe, b0 - MOD_FIRST + 1)
                layer = b0 // NMB
                v = mod_w[layer].rearrange("(k p) n -> p k n", p=P)
                sp.dma_start(mraw[b0 % 2][:, :, :], v[:, :, bass.ds(MB * (b0 - NMB * layer + ii), MB)]) \
                    .then_inc(mraw_in[b0 % 2], 16)

            def down(q0, w, n, block=0, blocks=0):
                def step(j0, i, beside):
                    panel(q0 + j0, i, dn_src(w, j0, i), JCN)
                    if beside:
                        mod_block(block + j0 - 2, 2 * i)
                step(0, 0, False)
                step(1, 0, False)
                steps_beside_blocks(sp, 2, blocks, n, step)

            def gate_up(f):
                w_gu, _, layer = FFN[f]

                def pair(g0, ii, b):
                    panel(Q_F[f] + 2 * g0, ii, gu_src(w_gu, layer, g0, ii, 0), KN)
                    panel(Q_F[f] + 2 * g0 + 1, ii, gu_src(w_gu, layer, g0, ii, 1), KN)
                    if b is not None:
                        mod_block(b, ii)
                loop_pairs(f, sp, pair, straight=(3, 5, 1, 1)[f], first=1 if f == 0 else 0)

            sp.dma_start(vec[0:8, 0, :], c_ctx.rearrange("(k p) -> k p", p=P)).then_inc(c_in, 16)
            sp.dma_start(vec[8:16, 0, :], c.rearrange("b (k p) -> (b k) p", p=P)).then_inc(c_in, 16)
            sp.dma_start(ident[:, :], consts[0]).then_inc(const_in, 16)
            mod_block(0, 0)
            mod_block(1, 0)
            sp.dma_start(x_tok[:, 0, :], x_prompt[0]).then_inc(x_in, 16)
            sp.dma_start(x_tok[:, 1:3, :], x_sample[0].rearrange("(a p) n -> p a n", p=P)).then_inc(x_in, 16)
            for layer in range(DEPTH):
                sp.dma_start(vec[0:NMOD * KD, 1 + layer, :], mod_b[layer].rearrange("(m p) -> m p", p=P)).then_inc(vec_in, 16)
            sp.dma_start(vec[0:DEPTH * 3 * KD, 3, :], norm_g.rearrange("l j (k p) -> (l j k) p", p=P)).then_inc(vec_in, 16)
            sp.dma_start(vec[0:KS, 4, :], v_g[0].rearrange("(k p) -> k p", p=P)).then_inc(vec_in, 16)
            for b in range(2, MOD_FIRST):
                v = mod_w[0].rearrange("(k p) n -> p k n", p=P)
                sp.dma_start(mfirst[:, b - 2, :, :], v[:, :, MB * b:MB * b + MB]).then_inc(mfirst_in[b - 2], 16)
            panel(0, 0, gu_src(w_gu1, 0, 0, 0, 0), KN)
            panel(1, 0, gu_src(w_gu1, 0, 0, 0, 1), KN)
            sp.wait_ge(zero_set, 1)
            sp.dma_start(toep[:, GRID - 16:GRID - 16 + BANDC], na_rpb[0].rearrange("h r c -> (h r) c")) \
                .then_inc(toep_in, 16)
            sp.dma_start(kc_na[:, :], ck_na[0, 0].rearrange("s h d -> s (h d)")).then_inc(tab_in, 16)
            sp.dma_start(vc_na[:, :], cv_na[0, 0].rearrange("s h d -> s (h d)")).then_inc(tab_in, 16)
            sp.dma_start(kc_g[:, :], ck_g[0, 0].rearrange("s h d -> s (h d)")).then_inc(tab_in, 16)
            sp.dma_start(vc_g[:, :], cv_g[0, 0].rearrange("s h d -> s (h d)")).then_inc(tab_in, 16)
            sp.dma_start(ropeT[:, :, :, :], rope.rearrange("c (a p) d -> p c a d", p=P)).then_inc(tab_in, 16)
            sp.dma_start(maskT[:, :], mask).then_inc(tab_in, 16)
            sp.dma_start(perm[:, :], consts[1]).then_inc(tab_in, 16)
            for n, g in enumerate((na_q_g, na_k_g, g_q_g, g_k_g)):
                sp.dma_start(gain[:, n, :], g[0].rearrange("(o d) -> o d", o=1).to_broadcast([P, HD])).then_inc(tab_in, 16)
            sp.wait_ge(toep_in, 16)
            sp.dma_start(toep_dram, toep[:, :]).then_inc(toep_out, 16)
            sp.wait_ge(toep_out, 16)
            for r in range(ROWS):
                for hh in range(NH):
                    src = bass.AP(toep_dram.tensor, (NDR * hh + 7 - r) * TOEP, [[1, GRID], [TOEP, ROWS], [1, GRID]])
                    dst = bias[GRID * (r % 2):GRID * (r % 2) + GRID, r // 2, hh, :].rearrange("p (a b) -> p a b", a=ROWS)
                    sp.dma_start(dst, src).then_inc(bias_in, 16)

            gate_up(0)
            down(Q_F[0] + 2 * GU, w_dn1[0], GU, MOD_AT[0] + MOD_GU, MOD_DN[0])
            for g in range(9):
                panel(Q_IN0 + g, 0, col_src(w_attn[0], g), KN)
                if 4 <= g < 4 + MOD_IN:
                    mod_block(MOD_M + g - 4, 0)
            down(Q_OUT0, w_o[0], KD // 2, MOD_M + MOD_IN, MOD_OUT)
            sp.wait_ge(gained, 7)
            sp.wait_ge(qkv_act, 3)
            sp.dma_start(o_nak[0, 0], k_na[:, 0, :, :]).then_inc(stored, 16)
            sp.dma_start(o_nav[0, 0].rearrange("s h d -> s (h d)"), v_na[:, 0, :]).then_inc(stored, 16)
            sp.dma_start(o_gk[0, 0], qk_g[:, 0, NH:NH + 2, :]).then_inc(stored, 16)
            sp.dma_start(o_gv[0, 0].rearrange("s h d -> s (h d)"), vg_[:, 0, :]).then_inc(stored, 16)
            gate_up(1)
            down(Q_F[1] + 2 * GU, w_dn2[0], GU, MOD_AT[1] + MOD_GU, MOD_DN[1])
            gate_up(2)
            down(Q_F[2] + 2 * GU, w_dn1[1], GU, MOD_AT[2] + MOD_GU, MOD_DN[2])
            for g in range(8):
                panel(Q_V + g, 0, col_src(w_sgu[0], 8 + g), KN)
                if 2 <= g < 2 + MOD_SG:
                    mod_block(MOD_V + g - 2, 0)
                if g == 1:
                    sp.wait_ge(pe_done, Q_V)
                    sp.dma_start(ws_row[:, :, :], w_s[0].rearrange("g t s -> t g s")).then_inc(ws_in, 16)
                    sp.dma_start(bsb[:, :, :], b_s[0].rearrange("(o g) t -> o g t", o=1).to_broadcast([P, NG, P])) \
                        .then_inc(ws_in, 16)
            for g in range(8):
                panel(Q_U + g, 0, col_src(w_sgu[0], g), KN)
            down(Q_OUT1, w_sgo[0], KS // 2)
            gate_up(3)
            down(Q_F[3] + 2 * GU, w_dn2[1], GU)
            for half in (1, 0):
                cols = slice(512 * half, 512 * half + 512)
                sp.wait_ge(y_done, 4 if half else 8)
                sp.dma_start(y_p[0][:, cols], y_tok[:, 0, cols]).then_inc(stored, 16)
                sp.dma_start(y_s[0].rearrange("(a p) n -> p a n", p=P)[:, :, cols], y_tok[:, 1:3, cols]).then_inc(stored, 16)
            sp.wait_ge(stored, 16 * 8)

        @block.gpsimd
        def _(pool):
            nc.gpsimd.memset(ones[:, :], 1.0).then_inc(ones_set, 1)
            nc.gpsimd.memset(mhalf[:, :], -0.5).then_inc(ones_set, 1)
            nc.gpsimd.memset(toep[:, :], 0.0).then_inc(zero_set, 1)

            def norm(n):
                for k in range(1, 4):
                    pool.wait_ge(sq_done, KD * n + k + 1)
                    if k == 1:
                        if n:
                            pool.wait_ge(rb_done, n)
                        nc.gpsimd.tensor_tensor(sqsum[:, :], sq[:, 0, :], sq[:, 1, :], ALU.add).then_inc(acc_done, 1)
                    else:
                        pool.wait_ge(acc_done, 3 * n + k - 1)
                        nc.gpsimd.tensor_tensor(sqsum[:, :], sqsum[:, :], sq[:, k, :], ALU.add).then_inc(acc_done, 1)
                pool.wait_ge(ms_done, n + 1)
                nc.gpsimd.tensor_tensor(rs[:, :], ms[:, :], mhalf[:, 0:TT], ALU.pow).then_inc(rs_done, 1)

            pool.wait_ge(ones_set, 2)
            norm(0)
            pool.wait_ge(bias_in, 16 * ROWS * NH)
            pool.wait_ge(tab_in, 16 * 11)
            for qt in range(2):
                bv = bias[:, qt, :, :].rearrange("p h (r k) -> p (h r) k", k=GRID)
                nc.gpsimd.tensor_tensor(bv, bv, maskT[:, None, :].to_broadcast([P, NH * ROWS, GRID]), ALU.add) \
                    .then_inc(bias_done, 1)
            norm(1)
            pool.wait_ge(gain_done, 2)
            for m in range(7):
                pool.wait_ge(hms_done, m + 1)
                w = 12 if m < 6 else 6
                nc.gpsimd.tensor_tensor(hrs[:, 0:w], hms[:, 0:w], mhalf[:, 0:w], ALU.pow).then_inc(hrs_done, 1)
                g = m if m < 4 else m + 2
                dst, nh, gn = heads_of(g)
                pool.wait_ge(qkv_dve, g + 1)
                nc.gpsimd.tensor_tensor(dst, dst, gain[:, gn, None, None, :].to_broadcast([P, TT, nh, HD]), ALU.mult) \
                    .then_inc(gained, 1)
            norm(2)
            norm(3)
            norm(4)
            pool.wait_ge(vms_done, 1)
            nc.gpsimd.tensor_tensor(rs[:, :], ms[:, :], mhalf[:, 0:TT], ALU.pow).then_inc(vrs_done, 1)
            norm(5)

        @block.scalar
        def _(act):
            steps = [0]

            def split(q0, i):
                if q0 >= Q_END:
                    return
                act.wait_ge(raw_in[q0 % 2], 16 * (q0 // 2 + 1 + i))
                if q0 >= 2:
                    act.wait_ge(pe_done, q0 + 2 * i - 1)
                nc.scalar.activation(w_hi[q0 % 2][:, :], raw[q0 % 2][:, :], ACT.Copy).then_inc(hi_done, 1)

            def squares(n):
                for k, m in enumerate(ORDER):
                    act.wait_ge(h_done, KD * n + k + 1)
                    if k >= 4:
                        act.wait_ge(acc_done, 3 * n + max(1, k - 4))
                    elif n:
                        act.wait_ge(stat_done, n)
                    nc.scalar.activation(sq[:, k % 4, :], h[:, m, :], ACT.Square).then_inc(sq_done, 1)

            def make_x(n, j):
                layer, seg = j
                base = (layer * NMOD + 3 * seg) * KD
                act.wait_ge(mvec, n + 1)
                for k in range(KD):
                    act.wait_ge(t_done, KD * n + k + 1)
                    for cond, cols in ((0, CTX), (1, LAT)):
                        last = nc.scalar.activation(tmp[:, k % 4, cols], tmp[:, k % 4, cols], ACT.Identity,
                                                    bias=modT[:, base + k, cond:cond + 1], scale=aT[:, k, cond:cond + 1])
                    last.then_inc(xm_done, 1)
                    act.wait_ge(xm_done, KD * n + k + 1)
                    nc.scalar.activation(x_hi[:, k, :], tmp[:, k % 4, :], ACT.Copy).then_inc(xh_done, 1)

            def ffn(f):
                q = Q_F[f]

                def pair(g0, i, b):
                    done = PAIRS[f] + g0 + i
                    if g0 == 0:
                        split(q + 2, 0)
                    act.wait_ge(pe_done, q + 2 * g0 + 1 + 2 * i)
                    if PAIRS[f] + g0:
                        act.wait_ge(actl_done, done)
                    nc.scalar.activation(tmp[:, 0:2, :], ps[:, 0:2, 0:T], ACT.Silu).then_inc(silu_done, 1)
                    if g0:
                        split(q + 2 * g0 + 2, i)
                    act.wait_ge(mul_done, done + 1)
                    nc.scalar.activation(act_hi[:, bass.ds(2 * g0 + 2 * i, 2), :], tmp[:, 0:2, :], ACT.Copy) \
                        .then_inc(acth_done, 1)
                    split(q + 2 * g0 + 3, i)
                loop_pairs(f, act, pair)

            def down(q0, n):
                steps_beside_blocks(act, 0, 0, min(n - 1, Q_END - 2 - q0), lambda j0, i, beside: split(q0 + j0 + 2, i))

            act.wait_ge(c_pe, 1)
            nc.scalar.activation(cT[:, :, :].rearrange("p k c -> p c k"),
                                 ps[:, 0, 0:16].rearrange("p (c k) -> p c k", c=2), ACT.Silu).then_inc(c_done, 1)
            squares(0)
            for a in range(MOD_FIRST // 2):
                act.wait_ge(mod_pe, 2 * a + 2)
                nc.scalar.activation(mod_row[:, 512 * a:512 * a + 512], ps[0:2, ROW_BANK[a], :], ACT.Copy) \
                    .then_inc(row_done, 1)
            split(0, 0)
            split(1, 0)
            make_x(0, (0, 0))
            act.wait_ge(toep_out, 16)
            ffn(0)
            down(Q_F[0] + 2 * GU, GU)
            squares(1)
            split(Q_IN0 + 1, 0)
            make_x(1, (0, 1))
            for g in range(9):
                act.wait_ge(pe_done, Q_IN0 + g + 1)
                if g in (4, 5, 8):
                    for t in range(TT):
                        dst, cols = (v_na[:, t, 256 * (g - 4):256 * (g - 4) + 256], slice(0, 256)) if g < 8 \
                            else (vg_[:, t, :], slice(128, 256))
                        last = nc.scalar.activation(dst, ps[:, QBANK[g % 2][t], cols], ACT.Copy)
                    last.then_inc(qkv_act, 1)
                if g not in (4, 5):
                    m = g if g < 4 else g - 2
                    w = 256 if g < 8 else 128
                    if m:
                        act.wait_ge(hms_sum, m)
                    for t in range(TT):
                        last = nc.scalar.activation(hsq_view(w)[:, t, :], ps[:, QBANK[g % 2][t], 0:w], ACT.Square)
                    last.then_inc(hsq_done, 1)
                split(Q_IN0 + g + 2, 0)
            for g, (dst, n) in enumerate(tr_groups()):
                if g not in TR_DVE:
                    act.wait_ge(tr_pe, g + 1)
                    nc.scalar.activation(dst, ps[:, TR_BANK[g % 8], 0:n], ACT.Copy).then_inc(tr_act, 1)

            def softmax(b):
                n = NCTX if b % 3 == 0 else T
                act.wait_ge(nmax_done, b + 1)
                if b >= 3:
                    act.wait_ge(pT_pe, b - 2)
                nc.scalar.activation(prob[:, b % 3, 0:n], ps[:, b % 3, 0:n], ACT.Exp, bias=nmax[:, b % 3:b % 3 + 1],
                                     accum_out=rsum[:, b % 3:b % 3 + 1]).then_inc(exp_done, 1)

            def put_pT(b):
                hh, kind = divmod(b, 3)
                act.wait_ge(pT_pe, b + 1)
                if hh >= 2 and kind == 0:
                    act.wait_ge(o_pe, hh - 1)
                if kind == 0:
                    nc.scalar.activation(pT_ctx[:, hh % 2, :], ps[:, 3 + b % 3, 0:P], ACT.Copy).then_inc(pT_done, 1)
                else:
                    nc.scalar.activation(pT_lat[:, hh % 2, :, P * (kind - 1):P * kind],
                                         ps[:, 3 + b % 3, 0:T].rearrange("p (k q) -> p k q", k=3), ACT.Copy) \
                        .then_inc(pT_done, 1)

            def o_hi(pair):
                act.wait_ge(o_pe, 2 * pair + 2)
                nc.scalar.activation(x_hi[:, pair, :], ps[:, 6 + pair % 2, 0:T], ACT.Copy).then_inc(oh_done, 1)

            for b in range(48 + 2):
                if b < 48:
                    softmax(b)
                if b >= 2:
                    put_pT(b - 2)
                if b >= 11 and (b - 11) % 6 == 0:
                    o_hi((b - 11) // 6)
            o_hi(7)
            down(Q_OUT0, KD // 2)
            squares(2)
            split(Q_F[1] + 1, 0)
            make_x(2, (0, 2))
            act.wait_ge(stored, 16 * 4)
            ffn(1)
            down(Q_F[1] + 2 * GU, GU)
            squares(3)
            split(Q_F[2] + 1, 0)
            make_x(3, (1, 0))
            ffn(2)
            down(Q_F[2] + 2 * GU, GU)
            squares(4)
            split(Q_V + 1, 0)
            make_x(4, (1, 1))
            for g in range(2):
                act.wait_ge(ws_pe, g + 1)
                nc.scalar.activation(wsT[:, 4 * g:4 * g + 4, :], ps[:, 4 + g, :].rearrange("p (g t) -> p g t", g=4), ACT.Copy) \
                    .then_inc(wsT_done, 1)
            for g in range(8):
                act.wait_ge(pe_done, Q_V + g + 1)
                for t in range(TT):
                    last = nc.scalar.activation(v_tok[:, t, 256 * g:256 * g + 256], ps[:, QBANK[g % 2][t], 0:256], ACT.Gelu)
                last.then_inc(gelu_v, 1)
                split(Q_V + g + 2, 0)
                act.wait_ge(gelu_v, g + 1)
                if g:
                    act.wait_ge(vss_done, g)
                for t in range(TT):
                    last = nc.scalar.activation(vsq[:, t, :], v_tok[:, t, 256 * g:256 * g + 256], ACT.Square,
                                                accum_out=vss[:, t, g:g + 1])
                last.then_inc(vss_done, 1)
            for g in range(8):
                done = UPAIR + g
                act.wait_ge(pe_done, Q_U + g + 1)
                act.wait_ge(actl_done, done)
                bk = 2 * (g % 2)
                nc.scalar.activation(tmp[:, 0:2, :], ps[:, bk:bk + 2, 0:T], ACT.Gelu).then_inc(silu_done, 1)
                split(Q_U + g + 2, 0)
                act.wait_ge(mul_done, done + 1)
                nc.scalar.activation(act_hi[:, 2 * g:2 * g + 2, :], tmp[:, 0:2, :], ACT.Copy).then_inc(acth_done, 1)
            down(Q_OUT1, KS // 2)
            squares(5)
            split(Q_F[3] + 1, 0)
            make_x(5, (1, 2))
            ffn(3)
            down(Q_F[3] + 2 * GU, GU)
            for k, m in enumerate(ORDER):
                act.wait_ge(yT_pe, k + 1)
                nc.scalar.activation(y_tok[:, :, P * m:P * m + P], ps[:, m, 0:T].rearrange("p (a n) -> p a n", a=TT), ACT.Copy) \
                    .then_inc(y_done, 1)

        @block.vector
        def _(dve):
            def link(ins):
                dve_steps[0] += 1
                ins.then_inc(dve_self, 1)
                dve.wait_ge(dve_self, dve_steps[0])

            def split(q0, i):
                if q0 >= Q_END:
                    return
                dve.wait_ge(hi_done, q0 + 2 * i + 1)
                nc.vector.tensor_tensor(w_lo[q0 % 2][:, :], raw[q0 % 2][:, :], w_hi[q0 % 2][:, :].bitcast(F32),
                                        ALU.subtract).then_inc(lo_done, 1)

            def mod_sum(b0, ii):
                m = b0 - MOD_FIRST
                dve.wait_ge(mraw_in[b0 % 2], 16 * (m // 2 + 2) + 8 * ii)
                if m >= 2:
                    dve.wait_ge(msum_done, m + ii - 1)
                for k in range(KD):
                    for cond in range(2):
                        acc = macc[:, b0 % 2, cond, :]
                        w, cc = mraw[b0 % 2][:, k, :], cT[:, k, cond:cond + 1]
                        if k == 0:
                            last = nc.vector.tensor_scalar(acc, w, cc, None, ALU.mult)
                        else:
                            dve.wait_ge(mchain, 15 * m + 15 * ii + 2 * k + cond - 1)
                            last = nc.vector.scalar_tensor_tensor(acc, w, cc, acc, ALU.mult, ALU.add)
                        if (k, cond) != (KD - 1, 1):
                            last.then_inc(mchain, 1)
                last.then_inc(macc_done, 1)

            def mod_out(b0, ii, n, src, wait):
                dve.wait_ge(*wait)
                nc.vector.tensor_tensor(modT[:, bass.ds(2 * b0 + 2 * ii, 2 * n), :], src.rearrange("p (a c) -> p a c", c=2),
                                        mbT[:, bass.ds(2 * b0 + 2 * ii, 2 * n), None].to_broadcast([P, 2 * n, 2]), ALU.add) \
                    .then_inc(mod_done, 1)

            def vectors(n, j):
                layer, seg = j
                base = (layer * NMOD + 3 * seg) * KD
                dve.wait_ge(mod_done, outs_until((base + 2 * KD) // 2))
                if n:
                    dve.wait_ge(xm_done, KD * n)
                nc.vector.scalar_tensor_tensor(
                    aT[:, :, :], modT[:, base + KD:base + 2 * KD, :], 1.0,
                    ngT[:, (layer * 3 + seg) * KD:(layer * 3 + seg + 1) * KD, None].to_broadcast([P, KD, 2]),
                    ALU.add, ALU.mult).then_inc(mvec, 1)

            def gate(n, j, w):
                layer, seg = j
                base = (layer * NMOD + 3 * seg + 2) * KD
                dve.wait_ge(mod_done, outs_until((base + KD) // 2))
                link(nc.vector.tensor_scalar(gT[:, :, :], modT[:, base:base + KD, :], w, None, ALU.mult))

            def rms(n, q=None):
                def half(a):
                    cols = slice(PW // 2 * a, PW // 2 * a + PW // 2)
                    return nc.vector.tensor_tensor(w_lo[q % 2][:, cols], raw[q % 2][:, cols],
                                                   w_hi[q % 2][:, cols].bitcast(F32), ALU.subtract)
                dve.wait_ge(stat_done, n + 1)
                nc.vector.tensor_scalar(ms[:, :], ps[:, 4, 0:TT], 1.0 / D, EPS, ALU.mult, ALU.add).then_inc(ms_done, 1)
                if q is not None:
                    dve.wait_ge(hi_done, q + 1)
                    half(0)
                dve.wait_ge(rs_done, n + 1)
                nc.vector.tensor_tensor(sqsum[:, :].rearrange("p (a q) -> p a q", a=TT),
                                        ident[:, None, :].to_broadcast([P, TT, P]),
                                        rs[:, :, None].to_broadcast([P, TT, P]), ALU.mult).then_inc(diag_done, 1)
                if q is not None:
                    half(1).then_inc(lo_done, 1)

            def make_x(n):
                dve.wait_ge(rb_done, n + 1)

                def t_of(k):
                    if k >= 4:
                        dve.wait_ge(xh_done, KD * n + k - 3)
                    nc.vector.tensor_tensor(tmp[:, k % 4, :], h[:, k, :], ps[:, 5, 0:T], ALU.mult).then_inc(t_done, 1)

                t_of(0)
                t_of(1)
                for k in range(KD):
                    dve.wait_ge(xh_done, KD * n + k + 1)
                    nc.vector.tensor_tensor(x_lo[:, k, :], tmp[:, k % 4, :], x_hi[:, k, :].bitcast(F32), ALU.subtract) \
                        .then_inc(x_done, 1)
                    if k + 2 < KD:
                        t_of(k + 2)

            def ffn(f):
                q = Q_F[f]

                def pair(g0, ii, b):
                    done = PAIRS[f] + g0 + ii
                    if b is not None:
                        mod_sum(b, ii)
                    split(q + 2 * g0 + 2, ii)
                    dve.wait_ge(pe_done, q + 2 * g0 + 2 + 2 * ii)
                    dve.wait_ge(silu_done, done + 1)
                    nc.vector.tensor_tensor(tmp[:, 0:2, :], ps[:, 2:4, 0:T], tmp[:, 0:2, :], ALU.mult).then_inc(mul_done, 1)
                    if b is not None:
                        mod_out(b, ii, 1, ps[:, 6 + b % 2, 0:4], (msum_done, b + ii - MOD_FIRST + 1))
                    dve.wait_ge(acth_done, done + 1)
                    nc.vector.tensor_tensor(act_lo[:, bass.ds(2 * g0 + 2 * ii, 2), :], tmp[:, 0:2, :],
                                            act_hi[:, bass.ds(2 * g0 + 2 * ii, 2), :].bitcast(F32), ALU.subtract) \
                        .then_inc(actl_done, 1)
                    split(q + 2 * g0 + 3, ii)
                loop_pairs(f, dve, pair)

            def down(q0, n, idx, j, w, block=0, blocks=0):
                def step(j0, i, beside):
                    split(q0 + j0 + 2, i)
                    if beside:
                        mod_sum(block + j0, 2 * i)
                steps_beside_blocks(dve, 0, blocks, n - 2, step)
                gate(idx, j, w)
                for k, m in enumerate(ORDER):
                    dve.wait_ge(out_done, KD * idx + k + 1)
                    for cond, cols in ((0, CTX), (1, LAT)):
                        last = nc.vector.scalar_tensor_tensor(h[:, m, cols], ps[:, m, cols], gT[:, m, cond:cond + 1],
                                                              h[:, m, cols], ALU.mult, ALU.add)
                    last.then_inc(h_done, 1)
                    if k == 1:
                        split(q0 + n, 0)
                    if m == 5 and blocks:
                        mod_out(block, 0, blocks, ps[:, 5, SPARE:SPARE + 4 * blocks],
                                (msum_done, block + blocks - MOD_FIRST))

            dve.wait_ge(vecT_pe, 1)
            for layer in range(DEPTH):
                nc.vector.tensor_copy(mbT[:, layer * 72:layer * 72 + 72], ps[:, 1, 128 * layer:128 * layer + 72])
            nc.vector.tensor_copy(ngT[:, :], ps[:, 1, 256:256 + 48])
            nc.vector.tensor_copy(vgT[:, :], ps[:, 1, 384:384 + KS]).then_inc(vecT_done, 1)
            dve.wait_ge(vecT_done, 1)
            for k, m in enumerate(ORDER):
                dve.wait_ge(xT_pe, k + 1)
                nc.vector.tensor_copy(h[:, m, :], ps[:, 2 + k % 4, 0:T]).then_inc(h_done, 1)
            rms(0)
            mod_out(0, 0, MOD_FIRST, ps[:, 2, 0:4 * MOD_FIRST], (rowT_pe, 1))
            vectors(0, (0, 0))
            split(0, 0)
            split(1, 0)
            make_x(0)
            ffn(0)
            dve.wait_ge(tab_in, 16 * 11)
            for n in (0, 2):
                nc.vector.tensor_scalar(gain[:, n, :], gain[:, n, :], HD ** -0.5, None, ALU.mult).then_inc(gain_done, 1)
            down(Q_F[0] + 2 * GU, GU, 0, (0, 0), 0.5, MOD_AT[0] + MOD_GU, MOD_DN[0])
            vectors(1, (0, 1))
            rms(1, Q_IN0 + 1)
            make_x(1)

            def rotate(hs):
                n = hs.stop - hs.start
                rt = rot_view()[:, hs, :]
                for t in (1, 2):
                    xv = qk_g[:, t, hs, :]
                    x5 = xv.rearrange("p h (a b d) -> p b h a d", a=2, b=2)
                    r5 = rt.rearrange("p h (a b d) -> p b h a d", a=2, b=2)
                    s5 = ropeT[:, 1, t - 1, :].rearrange("p (a b d) -> p b a d", a=2, b=2)
                    for part in range(2):
                        last = nc.vector.tensor_tensor(r5[:, part], x5[:, 1 - part],
                                                       s5[:, part, None].to_broadcast([P, n, 2, 16]), ALU.mult)
                    link(last)
                    link(nc.vector.tensor_tensor(xv, xv, ropeT[:, 0, t - 1, None, :].to_broadcast([P, n, HD]), ALU.mult))
                    link(nc.vector.tensor_tensor(xv, xv, rt, ALU.add))

            for g in range(9):
                if g == 8:
                    mod_out(MOD_M, 0, MOD_IN, ps[:, 4, 0:4 * MOD_IN], (msum_done, MOD_M + MOD_IN - MOD_FIRST))
                if g not in (4, 5):
                    m = g if g < 4 else g - 2
                    nh = 4 if g < 8 else 2
                    w = nh * HD
                    dve.wait_ge(hsq_done, m + 1)
                    nc.vector.tensor_reduce(hms[:, 0:TT * nh],
                                            hsq_view(w)[:, :, :].rearrange("p a (h d) -> p (a h) d", d=HD),
                                            AX.X, ALU.add).then_inc(hms_sum, 1)
                    dve.wait_ge(hms_sum, m + 1)
                    nc.vector.tensor_scalar(hms[:, 0:TT * nh], hms[:, 0:TT * nh], 1.0 / HD, EPS, ALU.mult, ALU.add) \
                        .then_inc(hms_done, 1)
                    split(Q_IN0 + g + 2, 0)
                    if g == 8:
                        dve.wait_ge(gained, 6)
                        rotate(slice(0, NH))
                    dve.wait_ge(hrs_done, m + 1)
                    dst = heads_of(g)[0]
                    for t in range(TT):
                        last = nc.vector.tensor_tensor(
                            dst[:, t], ps[:, QBANK[g % 2][t], 0:w].rearrange("p (h d) -> p h d", d=HD),
                            hrs[:, t * nh:(t + 1) * nh, None].to_broadcast([P, nh, HD]), ALU.mult)
                    last.then_inc(qkv_dve, 1)
                else:
                    dve.sem_inc(qkv_dve, 1)
                    split(Q_IN0 + g + 2, 0)
                if 2 <= g < 2 + MOD_IN:
                    mod_sum(MOD_M + g - 2, 0)
            dve.wait_ge(gained, 7)
            rotate(slice(NH, NH + 2))
            dve.sem_inc(rope_done, 1)
            for g, (dst, n) in enumerate(tr_groups()):
                if g in TR_DVE:
                    dve.wait_ge(tr_pe, g + 1)
                    nc.vector.tensor_copy(dst, ps[:, TR_BANK[g % 8], 0:n]).then_inc(tr_dve, 1)

            def top(b):
                n = NCTX if b % 3 == 0 else T
                dve.wait_ge(s_pe, b + 1)
                if b >= 3:
                    dve.wait_ge(exp_done, b - 2)
                nc.vector.tensor_reduce(nmax[:, b % 3:b % 3 + 1], ps[:, b % 3, 0:n], AX.X, ALU.max, negate=True) \
                    .then_inc(nmax_done, 1)

            def normalise(b):
                n = NCTX if b % 3 == 0 else T
                dve.wait_ge(exp_done, b + 1)
                link(nc.vector.reciprocal(rinv[:, b % 3:b % 3 + 1], rsum[:, b % 3:b % 3 + 1]))
                nc.vector.tensor_scalar(prob[:, b % 3, 0:n], prob[:, b % 3, 0:n], rinv[:, b % 3:b % 3 + 1], None,
                                        ALU.mult).then_inc(prob_done, 1)

            def o_lo(pair):
                dve.wait_ge(oh_done, pair + 1)
                nc.vector.tensor_tensor(x_lo[:, pair, :], ps[:, 6 + pair % 2, 0:T], x_hi[:, pair, :].bitcast(F32),
                                        ALU.subtract).then_inc(ol_done, 1)

            for b in range(48 + 1):
                if b < 48:
                    top(b)
                if b >= 1:
                    normalise(b - 1)
                if b >= 12 and (b - 12) % 6 == 0:
                    o_lo((b - 12) // 6)
            o_lo(7)
            down(Q_OUT0, KD // 2, 1, (0, 1), 1.0, MOD_M + MOD_IN, MOD_OUT)
            vectors(2, (0, 2))
            rms(2, Q_F[1] + 1)
            make_x(2)
            ffn(1)
            down(Q_F[1] + 2 * GU, GU, 2, (0, 2), 0.5, MOD_AT[1] + MOD_GU, MOD_DN[1])
            vectors(3, (1, 0))
            rms(3, Q_F[2] + 1)
            make_x(3)
            ffn(2)
            down(Q_F[2] + 2 * GU, GU, 3, (1, 0), 0.5, MOD_AT[2] + MOD_GU, MOD_DN[2])
            vectors(4, (1, 1))
            rms(4, Q_V + 1)
            make_x(4)
            for g in range(8):
                split(Q_V + g + 2, 0)
                if g < MOD_SG:
                    mod_sum(MOD_V + g, 0)
            dve.wait_ge(vss_done, 8)
            link(nc.vector.tensor_reduce(ms[:, :], vss[:, :, :], AX.X, ALU.add))
            nc.vector.tensor_scalar(ms[:, :], ms[:, :], 1.0 / SW, EPS, ALU.mult, ALU.add).then_inc(vms_done, 1)
            dve.wait_ge(vrs_done, 1)
            dve.wait_ge(wsT_done, 2)
            for t in range(TT):
                last = nc.vector.tensor_scalar(wsn[:, t, :, :], wsT[:, :, :], rs[:, t:t + 1], None, ALU.mult)
            last.then_inc(wsn_done, 1)
            mod_out(MOD_V, 0, MOD_SG, ps[:, 4, 0:4 * MOD_SG], (msum_done, MOD_V + MOD_SG - MOD_FIRST))
            dve.wait_ge(ws_in, 32)
            for d in range(KS):
                dve.wait_ge(sv_pe, d + 1)
                nc.vector.scalar_tensor_tensor(svb[:, d, :].rearrange("p (a t) -> p a t", a=TT),
                                               ps[:, (d + 2) % 8, 0:T].rearrange("p (a t) -> p a t", a=TT), vgT[:, d:d + 1],
                                               bsb[:, d // 2, None, :].to_broadcast([P, TT, P]), ALU.mult, ALU.add) \
                    .then_inc(sv_done, 1)
            dve.wait_ge(sv_done, KS)
            for g in range(8):
                split(Q_U + g + 2, 0)
                done = UPAIR + g
                dve.wait_ge(silu_done, done + 1)
                nc.vector.tensor_tensor(tmp[:, 0:2, :], tmp[:, 0:2, :], svb[:, 2 * g:2 * g + 2, :], ALU.mult) \
                    .then_inc(mul_done, 1)
                dve.wait_ge(acth_done, done + 1)
                nc.vector.tensor_tensor(act_lo[:, 2 * g:2 * g + 2, :], tmp[:, 0:2, :],
                                        act_hi[:, 2 * g:2 * g + 2, :].bitcast(F32), ALU.subtract).then_inc(actl_done, 1)
            down(Q_OUT1, KS // 2, 4, (1, 1), 1.0)
            vectors(5, (1, 2))
            rms(5, Q_F[3] + 1)
            make_x(5)
            ffn(3)
            down(Q_F[3] + 2 * GU, GU, 5, (1, 2), 0.5)

        @block.tensor
        def _(pe):
            mm = nc.tensor.matmul

            def three(out, w, cols, xs, start, stop):
                mm(out, w[0][:, cols], xs[0], start=start, stop=False)
                mm(out, w[0][:, cols], xs[1], start=False, stop=False)
                return mm(out, w[1][:, cols], xs[0], start=False, stop=stop)

            def slot(q0):
                return w_hi[q0 % 2], w_lo[q0 % 2]

            def mod_rows(b):
                if b < 2:
                    pe.wait_ge(mraw_in[b], 16)
                else:
                    pe.wait_ge(mfirst_in[b - 2], 16)
                w = mraw[b] if b < 2 else mfirst[:, b - 2]
                for k in range(KD):
                    last = mm(ps[0:2, ROW_BANK[b // 2], MB * (b % 2):MB * (b % 2) + MB], cT[:, k, :], w[:, k, :],
                              start=(k == 0), stop=(k == KD - 1))
                last.then_inc(mod_pe, 1)

            def row_transposes(a):
                pe.wait_ge(row_done, a + 1)
                for c in range(4 * a, 4 * a + 4):
                    last = nc.tensor.transpose(ps[:, 2, 2 * c:2 * c + 2], mod_row[:, P * c:P * c + P], ident[0:2, 0:2])
                if a == MOD_FIRST // 2 - 1:
                    last.then_inc(rowT_pe, 1)

            def mod_psum(b0, ii, bank, col, alone):
                pe.wait_ge(macc_done, b0 + ii - MOD_FIRST + 1)
                for a in range(2):
                    for cond in range(2):
                        last = mm(ps[:, bank, bass.ds(col + 2 * a + cond, 1)], macc[:, b0 % 2, cond, P * a:P * a + P],
                                  ones[:, 0:1], start=alone, stop=True, skip_group_check=not alone)
                last.then_inc(msum_done, 1)

            def feature_major(q0, bank, order):
                for a, k in order:
                    last = three(ps[:, bank + a, 0:T], slot(q0), slice(256 * k + P * a, 256 * k + P * a + P),
                                 (x_hi[:, k, :], x_lo[:, k, :]), k == 0, k == KD - 1)
                return last

            def token_major(q0, banks, order):
                hi, lo = slot(q0)
                for t, k in order:
                    tok, cols = slice(P * t, P * t + P), slice(256 * k, 256 * k + 256)
                    out = ps[:, banks[t], 0:256]
                    mm(out, x_hi[:, k, tok], hi[:, cols], start=(k == 0), stop=False)
                    mm(out, x_hi[:, k, tok], lo[:, cols], start=False, stop=False)
                    last = mm(out, x_lo[:, k, tok], hi[:, cols], start=False, stop=(k == KD - 1))
                return last

            def project(make, q0, i, bank):
                pe.wait_ge(lo_done, q0 + 2 * i + 1)
                tiles = 2 if make is feature_major else TT
                make(q0, bank, [(a, k) for a in range(tiles) for k in range(KD)]).then_inc(pe_done, 1)

            def project_first(make, q, banks, n):
                tiles = range(2 if make is feature_major else TT)
                shared = 3
                pe.wait_ge(lo_done, q + 2)
                for k in range(shared):
                    pe.wait_ge(x_done, KD * n + k + 1)
                    for a in range(2):
                        make(q + a, banks[a], [(t, k) for t in tiles])
                for k in range(shared, KD):
                    pe.wait_ge(x_done, KD * n + k + 1)
                    last = make(q, banks[0], [(t, k) for t in tiles])
                last.then_inc(pe_done, 1)
                make(q + 1, banks[1], [(t, k) for t in tiles for k in range(shared, KD)]).then_inc(pe_done, 1)

            def norm(n):
                norm_sums(n)
                norm_spread(n)

            def norm_sums(n):
                for k in (4, 5, None, 6, 7):
                    if k is None:
                        pe.wait_ge(acc_done, 3 * n + 3)
                    else:
                        pe.wait_ge(sq_done, KD * n + k + 1)
                    for t in range(TT):
                        part = sqsum[:, P * t:P * t + P] if k is None else sq[:, k % 4, P * t:P * t + P]
                        last = mm(ps[:, 4, t:t + 1], part, ones[:, 0:1], start=(k == 4 and t == 0), stop=(k == 7),
                                  skip_group_check=True)
                last.then_inc(stat_done, 1)

            def norm_spread(n):
                pe.wait_ge(diag_done, n + 1)
                mm(ps[:, 5, 0:T], ones[:, :], sqsum[:, :], start=True, stop=True).then_inc(rb_done, 1)

            def ffn(f, n):
                q = Q_F[f]

                def pair(g0, ii, b):
                    done = PAIRS[f] + g0 + ii
                    if g0 == 0:
                        project_first(feature_major, q, (0, 2), n)
                        return
                    pe.wait_ge(silu_done, done)
                    project(feature_major, q + 2 * g0, ii, 0)
                    pe.wait_ge(mul_done, done)
                    project(feature_major, q + 2 * g0 + 1, ii, 2)
                    if b is not None:
                        pe.wait_ge(mod_done, outs_until(b - 1) + ii)
                        mod_psum(b, ii, 6 + b % 2, 0, True)
                loop_pairs(f, pe, pair)

            def down(q0, n, idx, hi, lo, ready=None, block=0, blocks=0):
                def panel(j0, i, beside=False, first=False, final=False):
                    pe.wait_ge(lo_done, q0 + j0 + 2 * i + 1)
                    if ready is not None and (first or final):
                        ready(pe, first)
                    for k, m in enumerate(ORDER):
                        if first and k == 2 and blocks:
                            pe.wait_ge(mod_done, outs_until(block))
                        if first and k == 4 and ready is not None:
                            ready(pe, None)
                        for c in range(2):
                            kk = slice(2 * j0 + c, 2 * j0 + c + 1) if isinstance(i, int) else bass.ds(2 * j0 + c + 4 * i, 1)
                            last = three(ps[:, m, 0:T], slot(q0 + j0), slice(1024 * c + P * m, 1024 * c + P * m + P),
                                         (hi[:, kk, :], lo[:, kk, :]), first and c == 0, final and c == 1)
                        if final:
                            last.then_inc(out_done, 1)
                        elif k == 3 and beside:
                            mod_psum(block + j0 - 2, 2 * i, 5, SPARE + 4 * (j0 - 2) + 8 * i, False)
                    if not final:
                        last.then_inc(pe_done, 1)
                    else:
                        pe.wait_ge(out_done, KD * idx + KD)
                        pe.sem_inc(pe_done, 1)

                panel(0, 0, first=True)
                panel(1, 0)
                steps_beside_blocks(pe, 2, min(blocks, n - 3), n - 1, panel)
                for b in range(n - 3, blocks):
                    mod_psum(block + b, 0, 5, SPARE + 4 * b, False)
                panel(n - 1, 0, final=True)

            def ready_ffn(f):
                def waits(eng, first):
                    if first:
                        eng.wait_ge(actl_done, PAIRS[f] + GU - 1)
                    elif first is None:
                        eng.wait_ge(mul_done, PAIRS[f] + GU)
                    else:
                        eng.wait_ge(actl_done, PAIRS[f] + GU)
                return waits

            pe.wait_ge(const_in, 16)
            pe.wait_ge(c_in, 32)
            nc.tensor.transpose(ps[:, 0, 0:16], vec[0:16, 0, :], ident[0:16, 0:16]).then_inc(c_pe, 1)
            pe.wait_ge(c_done, 1)
            mod_rows(0)
            mod_rows(1)
            pe.wait_ge(vec_in, 16 * 4)
            for r, n in ((1, 72), (2, 72), (3, 48), (4, KS)):
                last = nc.tensor.transpose(ps[:, 1, 128 * (r - 1):128 * (r - 1) + n], vec[0:n, r, :], ident[0:n, 0:n])
            last.then_inc(vecT_pe, 1)
            pe.wait_ge(x_in, 32)
            for k, m in enumerate(ORDER):
                if k >= 4:
                    pe.wait_ge(h_done, k - 3)
                for t in range(TT):
                    last = nc.tensor.transpose(ps[:, 2 + k % 4, P * t:P * t + P], x_tok[:, t, P * m:P * m + P], ident[:, :])
                last.then_inc(xT_pe, 1)
            mod_rows(2)
            pe.wait_ge(ones_set, 2)
            pe.wait_ge(h_done, KD)
            norm_sums(0)
            mod_rows(3)
            norm_spread(0)
            pe.wait_ge(vecT_done, 1)
            mod_rows(4)
            mod_rows(5)
            for a in range(3):
                row_transposes(a)
            mod_rows(6)
            mod_rows(7)
            row_transposes(3)
            ffn(0, 0)
            down(Q_F[0] + 2 * GU, GU, 0, act_hi, act_lo, ready_ffn(0), MOD_AT[0] + MOD_GU, MOD_DN[0])
            norm(1)

            project_first(token_major, Q_IN0, QBANK, 1)
            for g in range(2, 9):
                pe.wait_ge(qkv_dve, g - 1)
                if g - 2 >= 4:
                    pe.wait_ge(qkv_act, min(g - 5, 2))
                project(token_major, Q_IN0 + g, 0, QBANK[g % 2])
                if 4 <= g < 4 + MOD_IN:
                    mod_psum(MOD_M + g - 4, 0, 4, 4 * (g - 4), True)
            pe.wait_ge(gained, 4)
            groups = ([(q_na, n, None) for n in range(4)] + [(k_na, n, kc_na[:, P * n:P * n + P]) for n in range(4)]
                      + [(qk_g, n, None) for n in range(4)] + [(qk_g, 4, kc_g[:, :])])
            for g, (src, n, cache) in enumerate(groups):
                bank = TR_BANK[g % 8]
                if g == 1:
                    pe.wait_ge(mod_done, outs_until(MOD_M + MOD_IN))
                elif g == 2:
                    pe.wait_ge(qkv_dve, 8)
                elif g == 4:
                    pe.wait_ge(tab_in, 16 * 11)
                elif g == 5:
                    pe.wait_ge(qkv_dve, 9)
                    pe.wait_ge(qkv_act, 3)
                elif g >= 8:
                    if g == 8:
                        pe.wait_ge(rope_done, 1)
                    pe.wait_ge(tr_act, g - 7)
                for t in range(TT):
                    last = nc.tensor.transpose(ps[:, bank, P * t:P * t + P],
                                               src[:, t, 2 * n:2 * n + 2, :].rearrange("p h d -> p (h d)"), ident[:, :])
                if cache is not None:
                    last = nc.tensor.transpose(ps[:, bank, T:T + P], cache, ident[:, :])
                last.then_inc(tr_pe, 1)
            pe.wait_ge(tr_act, 11)
            pe.wait_ge(tr_dve, 2)
            pe.wait_ge(bias_done, 2)

            def scores(b):
                hh, kind = divmod(b, 3)
                if hh < NH:
                    base, qT, kT = HD * (hh % 2), qT_na[:, hh // 2, :], kT_na[:, hh // 2, :]
                else:
                    g = hh - NH
                    base, qT, kT = HD * (g // 4), qT_g[:, g % 4, :], kT_g[:, :]
                rows = slice(base, base + HD)
                if b >= 3:
                    pe.wait_ge(exp_done, b - 2)
                if kind == 0:
                    mm(ps[:, b % 3, 0:P], qT[rows, 0:P], kT[rows, 0:P], start=True, stop=True).then_inc(s_pe, 1)
                else:
                    na = hh < NH
                    last = mm(ps[:, b % 3, 0:T], qT[rows, P * kind:P * kind + P], kT[rows, P:P + T], start=True, stop=not na)
                    if na:
                        last = mm(ps[:, b % 3, 0:NLAT], perm[:, :], bias[:, kind - 1, hh, :], start=False, stop=True)
                    last.then_inc(s_pe, 1)

            def p_transposes(b):
                pe.wait_ge(prob_done, b + 1)
                if b >= 3:
                    pe.wait_ge(pT_done, b - 2)
                for k in range(1 if b % 3 == 0 else 3):
                    last = nc.tensor.transpose(ps[:, 3 + b % 3, P * k:P * k + P], prob[:, b % 3, P * k:P * k + P], ident[:, :])
                last.then_inc(pT_pe, 1)

            def values(hh):
                pe.wait_ge(pT_done, 3 * hh + 3)
                pair, half = divmod(hh, 2)
                if hh >= 4 and half == 0:
                    pe.wait_ge(ol_done, pair - 1)
                out = ps[HD * half:HD * half + HD, 6 + pair % 2, :]
                if hh < NH:
                    v, cache, cols = v_na, vc_na, slice(HD * hh, HD * hh + HD)
                else:
                    kv = (hh - NH) // 4
                    v, cache, cols = vg_, vc_g, slice(HD * kv, HD * kv + HD)
                mm(out[:, 0:P], v[:, 0, cols], pT_ctx[:, hh % 2, :], start=True, stop=True)
                mm(out[:, P:T], v[:, 1, cols], pT_lat[:, hh % 2, 0, :], start=True, stop=False)
                mm(out[:, P:T], v[:, 2, cols], pT_lat[:, hh % 2, 1, :], start=False, stop=False)
                mm(out[:, P:T], cache[:, cols], pT_lat[:, hh % 2, 2, :], start=False, stop=True).then_inc(o_pe, 1)

            for b in range(48 + 4):
                if b < 48:
                    scores(b)
                if 2 <= b < 50:
                    p_transposes(b - 2)
                if b >= 6 and b % 3 == 0:
                    values(b // 3 - 2)

            def ready_attn(eng, first):
                if first:
                    eng.wait_ge(ol_done, 8)

            down(Q_OUT0, KD // 2, 1, x_hi, x_lo, ready_attn, MOD_M + MOD_IN, MOD_OUT)
            norm(2)
            ffn(1, 2)
            down(Q_F[1] + 2 * GU, GU, 2, act_hi, act_lo, ready_ffn(1), MOD_AT[1] + MOD_GU, MOD_DN[1])
            norm(3)
            ffn(2, 3)
            down(Q_F[2] + 2 * GU, GU, 3, act_hi, act_lo, ready_ffn(2), MOD_AT[2] + MOD_GU, MOD_DN[2])
            norm(4)
            project_first(token_major, Q_V, QBANK, 4)
            pe.wait_ge(ws_in, 32)
            for a in range(2):
                for n in range(4):
                    last = nc.tensor.transpose(ps[:, 4 + a, P * n:P * n + P], ws_row[:, 4 * a + n, :], ident[:, :])
                last.then_inc(ws_pe, 1)
            for g in range(2, 8):
                pe.wait_ge(gelu_v, g - 1)
                project(token_major, Q_V + g, 0, QBANK[g % 2])
                if g < 2 + MOD_SG:
                    if g == 2:
                        pe.wait_ge(wsT_done, 1)
                    mod_psum(MOD_V + g - 2, 0, 4, 4 * (g - 2), True)
            pe.wait_ge(gelu_v, 7)
            project(feature_major, Q_U, 0, 0)
            pe.wait_ge(gelu_v, 8)
            pe.wait_ge(wsn_done, 1)
            for d in range(KS):
                if d == 2:
                    pe.wait_ge(mod_done, outs_until(DEPTH * NMB))
                if d == 6:
                    pe.wait_ge(silu_done, UPAIR + 1)
                if d >= 8:
                    pe.wait_ge(sv_done, d - 7)
                for t in range(TT):
                    last = mm(ps[:, (d + 2) % 8, P * t:P * t + P], v_tok[:, t, P * d:P * d + P], wsn[:, t, d // 2, :],
                              start=True, stop=True)
                last.then_inc(sv_pe, 1)
            for g in range(1, 8):
                if g == 1:
                    pe.wait_ge(sv_done, 10)
                else:
                    if g == 2:
                        pe.wait_ge(sv_done, KS)
                    pe.wait_ge(silu_done, UPAIR + g - 1)
                project(feature_major, Q_U + g, 0, 2 * (g % 2))

            def ready_sgu(eng, first):
                if first:
                    eng.wait_ge(actl_done, UPAIR + 7)
                elif first is None:
                    eng.wait_ge(silu_done, UPAIR + 8)
                else:
                    eng.wait_ge(actl_done, UPAIR + 8)

            down(Q_OUT1, KS // 2, 4, act_hi, act_lo, ready_sgu)
            norm(5)
            ffn(3, 5)
            down(Q_F[3] + 2 * GU, GU, 5, act_hi, act_lo, ready_ffn(3))
            for k, m in enumerate(ORDER):
                pe.wait_ge(h_done, KD * 6 + k + 1)
                for t in range(TT):
                    last = nc.tensor.transpose(ps[:, m, P * t:P * t + P], h[:, m, P * t:P * t + P], ident[:, :])
                last.then_inc(yT_pe, 1)


PAIRS = (0, GU, 2 * GU, 3 * GU + 8)
UPAIR = 3 * GU
QBANK = ((0, 1, 2), (3, 6, 7))
TR_BANK = (5, 4, 3, 6, 7, 0, 1, 2)
TR_DVE = (9, 11)
ROW_BANK = (6, 7, 0, 1)

_NAMES = ['x_prompt', 'x_sample', 'cache_na_k', 'cache_na_v', 'cache_gqa_k', 'cache_gqa_v', 'c', 'c_ctx', 'norm_g', 'mod_w',
          'mod_b', 'ffn1_w_gu', 'ffn1_w_down', 'ffn2_w_gu', 'ffn2_w_down', 'attn_w_in', 'attn_w_out', 'na_q_g', 'na_k_g',
          'na_rpb', 'gqa_q_g', 'gqa_k_g', 'sgu_w_in', 'sgu_v_g', 'sgu_w_s', 'sgu_b_s', 'sgu_w_out']
_OUTS = [(1, NCTX, D), (1, NLAT, D), (1, 1, NCTX, NH, HD), (1, 1, NCTX, NH, HD), (1, 1, NCTX, 2, HD), (1, 1, NCTX, 2, HD)]


def shape_constants():
    t = np.arange(NLAT)
    half = HD // 2
    freqs = 10000.0 ** (-np.arange(0, half, 2, dtype=np.float64) / half)
    rope = np.zeros((2, NLAT, HD), np.float32)
    for a, pos in enumerate((t // GRID, t % GRID)):
        ang = pos[:, None] * freqs[None, :]
        for b in range(2):
            at = slice(a * half + b * 16, a * half + b * 16 + 16)
            rope[0, :, at] = np.cos(ang)
            rope[1, :, at] = np.sin(ang) * (1 if b else -1)
    j = np.arange(P)
    qcol = (GRID - 1 - j % GRID)[:, None]
    start = np.clip(qcol - 8, 0, GRID - 16)
    kcol = np.arange(GRID)[None, :]
    mask = np.where((kcol >= start) & (kcol < start + 16), 0.0, -1e30).astype(np.float32)
    consts = np.zeros((2, P, P), np.float32)
    consts[0, j, j] = 1.0
    consts[1, j, GRID * (j // GRID) + GRID - 1 - j % GRID] = 1.0
    return rope, mask, consts


def kernel(**inputs):
    import concourse.bacc as bacc
    from concourse.bass_utils import run_bass_kernel_spmd as run

    nc = bacc.Bacc("TRN2", target_bir_lowering=False, num_devices=1)
    arrays = {n: np.ascontiguousarray(inputs[n]) for n in _NAMES}
    for n, a in zip(("rope_table", "window_mask", "consts"), shape_constants()):
        arrays[n] = a
    ins = [nc.dram_tensor(n, a.shape, F32, kind="ExternalInput").ap() for n, a in arrays.items()]
    outs = [nc.dram_tensor(f"out_{i}", s, F32, kind="ExternalOutput").ap() for i, s in enumerate(_OUTS)]
    toep = nc.dram_tensor("toep_scratch", (NH * NDR, TOEP), F32, kind="Internal").ap()
    build(nc, ins, outs, toep)
    r = run(nc, [arrays], core_ids=[0])
    return tuple(r.results[0][f"out_{i}"] for i in range(len(_OUTS)))
```

```python
from contextlib import ExitStack

import numpy as np
import concourse.bass as bass
from concourse import mybir

ALU = mybir.AluOpType
ACT = mybir.ActivationFunctionType
AX = mybir.AxisListType
F32 = mybir.dt.float32
F32R = mybir.dt.float32r

P = 128
D = 1024
KD = D // P
NCTX, NLAT = 128, 256
T = NCTX + NLAT
TT = T // P
CTX, LAT = slice(0, NCTX), slice(NCTX, T)
DEPTH = 2
F = 2816
GU = F // 256
KF = F // P
NMOD = 9
HD = 64
NH = 8
KVW = 128
GRID = 64
ROWS = NLAT // GRID
SW = 2 * D
KS = SW // P
NG = 8
EPS = 1e-6
PW = 2048
MB = 256
NMB = NMOD * D // MB
MOD_FIRST = 2 * D // MB
TOEP = 2 * GRID - 1
NDR = 15
BANDC = 31
ORDER = (4, 5, 6, 7, 0, 1, 2, 3)

Q_F = (0, 46, 79, 136)
Q_IN0, Q_OUT0 = 33, 42
Q_V, Q_U, Q_OUT1 = 112, 120, 128
Q_END = 169
MOD_SUM = MOD_FIRST - 1
MOD_GU = GU - 1
MOD_DN = (8, 8, 8)
MOD_IN, MOD_OUT, MOD_SG = 4, 2, 4
MOD_AT = (8, 32, 50)
MOD_M = MOD_AT[0] + MOD_GU + MOD_DN[0]
MOD_V = MOD_AT[2] + MOD_GU + MOD_DN[2]
SPARE = T


def outs_until(block):
    pairs = [1] * MOD_GU
    sizes = [MOD_FIRST, *pairs, MOD_DN[0], MOD_IN, MOD_OUT, *pairs, MOD_DN[1], *pairs, MOD_DN[2], MOD_SG]
    n = have = 0
    while have < block:
        have += sizes[n]
        n += 1
    return n


def build(nc, t_in, t_out, toep_dram):
    (x_prompt, x_sample, ck_na, cv_na, ck_g, cv_g, c, c_ctx, norm_g, mod_w, mod_b, w_gu1, w_dn1, w_gu2, w_dn2,
     w_attn, w_o, na_q_g, na_k_g, na_rpb, g_q_g, g_k_g, w_sgu, v_g, w_s, b_s, w_sgo, rope, mask, consts) = t_in
    y_p, y_s, o_nak, o_nav, o_gk, o_gv = t_out

    ctx = ExitStack()
    with ctx:
        def sb(name, shape, dt=F32, scope=ctx):
            return scope.enter_context(nc.sbuf_tensor(name, shape, dt))

        def sem(name):
            return ctx.enter_context(nc.semaphore(name))

        h = sb("h", [P, KD, T])
        raw = [sb(f"raw{i}", [P, PW]) for i in range(2)]
        w_hi = [sb(f"w_hi{i}", [P, PW], F32R) for i in range(2)]
        w_lo = [sb(f"w_lo{i}", [P, PW], F32R) for i in range(2)]
        mraw = [sb(f"mraw{i}", [P, KD, MB]) for i in range(2)]
        tmp = sb("tmp", [P, 4, T])
        with ExitStack() as s:
            macc = sb("macc", [P, 2, 2, MB], scope=s)
        sq = sb("sq", [P, 4, T])
        sqsum = sb("sqsum", [P, T])
        ident = sb("ident", [P, P])
        ones = sb("ones", [P, P])
        modT = sb("modT", [P, DEPTH * NMOD * KD, 2])
        mbT = sb("mbT", [P, DEPTH * NMOD * KD])
        ngT = sb("ngT", [P, DEPTH * 3 * KD])
        vgT = sb("vgT", [P, KS])
        cT = sb("cT", [P, KD, 2])
        aT = sb("aT", [P, KD, 2])
        gT = sb("gT", [P, KD, 2])
        ms = sb("ms", [P, TT])
        rs = sb("rs", [P, TT])
        mhalf = sb("mhalf", [P, 16])
        hms = sb("hms", [P, 12])
        hrs = sb("hrs", [P, 12])
        nmax = sb("nmax", [P, 4])
        rsum = sb("rsum", [P, 4])
        rinv = sb("rinv", [P, 4])
        vss = sb("vss", [P, TT, KD])

        with ExitStack() as s:
            y_tok = sb("y_tok", [P, TT, D], scope=s)
        with ExitStack() as s:
            mod_row = sb("mod_row", [2, MOD_FIRST * MB], scope=s)
        x_hi = sb("x_hi", [P, KD, T], F32R)
        x_lo = sb("x_lo", [P, KD, T], F32R)

        with ExitStack() as s:
            svb = sb("svb", [P, KS, T], scope=s)
        with ExitStack() as s:
            bias = sb("bias", [P, 2, NH, NLAT], scope=s)
            kc_na = sb("kc_na", [P, NH * HD], scope=s)
            vc_na = sb("vc_na", [P, NH * HD], scope=s)
            kc_g = sb("kc_g", [P, KVW], scope=s)
            vc_g = sb("vc_g", [P, KVW], scope=s)
            ropeT = sb("ropeT", [P, 2, 2, HD], scope=s)
            gain = sb("gain", [P, 4, HD], scope=s)
            maskT = sb("maskT", [P, GRID], scope=s)
            perm = sb("perm", [P, P], scope=s)
        sb("region_d", [P, KS, T])

        with ExitStack() as s:
            x_tok = sb("x_tok", [P, TT, D], scope=s)
            vec = sb("vec", [P, 5, P], scope=s)
            toep = sb("toep", [NH * NDR, TOEP], scope=s)
            mfirst = sb("mfirst", [P, MOD_FIRST - 2, KD, MB], scope=s)
        with ExitStack() as s:
            q_na = sb("q_na", [P, TT, NH, HD], scope=s)
            k_na = sb("k_na", [P, TT, NH, HD], scope=s)
            qk_g = sb("qk_g", [P, TT, NH + 2, HD], scope=s)
            v_na = sb("v_na", [P, TT, NH * HD], scope=s)
            vg_ = sb("vg_", [P, TT, KVW], scope=s)
            qT_na = sb("qT_na", [P, 4, T], scope=s)
            kT_na = sb("kT_na", [P, 4, T + P], scope=s)
            qT_g = sb("qT_g", [P, 4, T], scope=s)
            kT_g = sb("kT_g", [P, T + P], scope=s)
            prob = sb("prob", [P, 4, T], scope=s)
            pT_lat = sb("pT_lat", [P, 2, 3, NLAT], scope=s)
            pT_ctx = sb("pT_ctx", [P, 2, NCTX], scope=s)
        with ExitStack() as s:
            v_tok = sb("v_tok", [P, TT, SW], scope=s)
            ws_row = sb("ws_row", [P, NG, P], scope=s)
            wsT = sb("wsT", [P, NG, P], scope=s)
            wsn = sb("wsn", [P, TT, NG, P], scope=s)
            bsb = sb("bsb", [P, NG, P], scope=s)
            vsq = sb("vsq", [P, TT, 256], scope=s)
        act_hi = sb("act_hi", [P, KF, T], F32R)
        act_lo = sb("act_lo", [P, KF, T], F32R)
        ps = ctx.enter_context(nc.psum_tensor("ps", [P, 8, 512], F32))

        raw_in = [sem(f"raw_in{i}") for i in range(2)]
        hi_done = sem("hi_done")
        lo_done = sem("lo_done")
        pe_done = sem("pe_done")
        mraw_in = [sem(f"mraw_in{i}") for i in range(2)]
        mfirst_in = [sem(f"mfirst_in{i}") for i in range(MOD_FIRST - 2)]
        mod_pe = sem("mod_pe")
        row_done = sem("row_done")
        rowT_pe = sem("rowT_pe")
        mchain = sem("mchain")
        macc_done = sem("macc_done")
        msum_done = sem("msum_done")
        mod_done = sem("mod_done")
        silu_done = sem("silu_done")
        mul_done = sem("mul_done")
        acth_done = sem("acth_done")
        actl_done = sem("actl_done")
        out_done = sem("out_done")
        h_done = sem("h_done")
        sq_done = sem("sq_done")
        acc_done = sem("acc_done")
        stat_done = sem("stat_done")
        ms_done = sem("ms_done")
        rs_done = sem("rs_done")
        diag_done = sem("diag_done")
        rb_done = sem("rb_done")
        t_done = sem("t_done")
        xm_done = sem("xm_done")
        xh_done = sem("xh_done")
        x_done = sem("x_done")
        mvec = sem("mvec")
        x_in = sem("x_in")
        vec_in = sem("vec_in")
        c_in = sem("c_in")
        const_in = sem("const_in")
        ones_set = sem("ones_set")
        zero_set = sem("zero_set")
        vecT_pe = sem("vecT_pe")
        vecT_done = sem("vecT_done")
        c_pe = sem("c_pe")
        c_done = sem("c_done")
        xT_pe = sem("xT_pe")
        toep_in = sem("toep_in")
        toep_out = sem("toep_out")
        bias_in = sem("bias_in")
        bias_done = sem("bias_done")
        tab_in = sem("tab_in")
        gain_done = sem("gain_done")
        hsq_done = sem("hsq_done")
        hms_sum = sem("hms_sum")
        hms_done = sem("hms_done")
        hrs_done = sem("hrs_done")
        gained = sem("gained")
        dve_self = sem("dve_self")
        act_self = sem("act_self")
        qkv_act = sem("qkv_act")
        qkv_dve = sem("qkv_dve")
        rope_done = sem("rope_done")
        tr_pe = sem("tr_pe")
        tr_act = sem("tr_act")
        tr_dve = sem("tr_dve")
        s_pe = sem("s_pe")
        nmax_done = sem("nmax_done")
        exp_done = sem("exp_done")
        prob_done = sem("prob_done")
        pT_pe = sem("pT_pe")
        pT_done = sem("pT_done")
        o_pe = sem("o_pe")
        oh_done = sem("oh_done")
        ol_done = sem("ol_done")
        ws_in = sem("ws_in")
        ws_pe = sem("ws_pe")
        wsT_done = sem("wsT_done")
        gelu_v = sem("gelu_v")
        vss_done = sem("vss_done")
        vms_done = sem("vms_done")
        vrs_done = sem("vrs_done")
        wsn_done = sem("wsn_done")
        sv_pe = sem("sv_pe")
        sv_done = sem("sv_done")
        yT_pe = sem("yT_pe")
        y_done = sem("y_done")
        stored = sem("stored")

        block = ctx.enter_context(nc.Block())

        dve_steps = [0]

        def gu_src(w_gu, layer, g0, i, up):
            v = w_gu[layer].rearrange("(k p) n -> p k n", p=P)
            return v[:, :, bass.ds(F * up + 256 * (g0 + i), 256)]

        def dn_src(w, j0, i):
            v = w.rearrange("(j c p) n -> p j c n", c=2, p=P)
            return v[:, bass.ds(j0 + 2 * i, 1), :, :]

        def col_src(w, g):
            return w.rearrange("(k p) n -> p k n", p=P)[:, :, 256 * g:256 * g + 256]

        FFN = [(w_gu1, w_dn1, 0), (w_gu2, w_dn2, 0), (w_gu1, w_dn1, 1), (w_gu2, w_dn2, 1)]

        def loop_pairs(f, eng, pair, straight=1, first=0):
            block = lambda g: MOD_AT[f] + g - 1 if f < 3 and g else None
            for g in range(first, straight):
                pair(g, 0, block(g))
            its = (GU - straight) // 2
            with eng.Fori(0, its) as i:
                pair(straight, 2 * i, block(straight))
                pair(straight + 1, 2 * i, block(straight + 1))
            for g in range(straight + 2 * its, GU):
                pair(g, 0, block(g))

        def steps_beside_blocks(eng, first, blocks, end, step):
            for lo, hi, beside in ((first, first + blocks, True), (first + blocks, end, False)):
                its = (hi - lo) // 2
                if its > 1:
                    with eng.Fori(0, its) as i:
                        step(lo, i, beside)
                        step(lo + 1, i, beside)
                    lo += 2 * its
                for j in range(lo, hi):
                    step(j, 0, beside)

        def hsq_view(w):
            return tmp[:, 0:2, :].rearrange("p a t -> p (a t)")[:, 0:TT * w].rearrange("p (a w) -> p a w", a=TT)

        def rot_view():
            return tmp[:, 2:4, :].rearrange("p a t -> p (a t)")[:, 0:(NH + 2) * HD].rearrange("p (h d) -> p h d", d=HD)

        def heads_of(step):
            c = QKV_ORDER[step]
            if c < 2:
                return q_na[:, :, 4 * c:4 * c + 4, :], 4, 0
            if c < 4:
                return k_na[:, :, 4 * c - 8:4 * c - 4, :], 4, 1
            if c < 8:
                return qk_g[:, :, c - 6:c + 1:2, :], 4, 2
            return qk_g[:, :, NH:NH + 2, :], 2, 3

        def tr_groups():
            return (sum([[(qT_na[:, n, :], T), (kT_na[:, n, :], T + P)] for n in range(4)], [])
                    + [(qT_g[:, n, :], T) for n in range(4)] + [(kT_g[:, :], T + P)])

        @block.sync
        def _(sp):
            def panel(q0, i, src, shape):
                if q0 >= 2:
                    sp.wait_ge(lo_done, q0 + 2 * i - 1)
                dst = raw[q0 % 2][:, :].rearrange(shape[0], **shape[1])
                sp.dma_start(dst, src).then_inc(raw_in[q0 % 2], 16)

            KN = ("p (k n) -> p k n", dict(k=KD))
            JCN = ("p (j c n) -> p j c n", dict(j=1, c=2))

            def mod_block(b0, ii):
                if b0 >= MOD_FIRST + 2:
                    sp.wait_ge(macc_done, b0 + ii - MOD_SUM - 1)
                elif b0 >= MOD_FIRST:
                    sp.wait_ge(mod_pe, b0 - MOD_FIRST + 1)
                layer = b0 // NMB
                v = mod_w[layer].rearrange("(k p) n -> p k n", p=P)
                sp.dma_start(mraw[b0 % 2][:, :, :], v[:, :, bass.ds(MB * (b0 - NMB * layer + ii), MB)]) \
                    .then_inc(mraw_in[b0 % 2], 16)

            def down(q0, w, n, block=0, blocks=0):
                def step(j0, i, beside):
                    panel(q0 + j0, i, dn_src(w, j0, i), JCN)
                    if beside:
                        mod_block(block + j0 - 2, 2 * i)
                step(0, 0, False)
                step(1, 0, False)
                steps_beside_blocks(sp, 2, blocks, n, step)

            def gate_up(f):
                w_gu, _, layer = FFN[f]

                def pair(g0, ii, b):
                    panel(Q_F[f] + 2 * g0, ii, gu_src(w_gu, layer, g0, ii, 0), KN)
                    panel(Q_F[f] + 2 * g0 + 1, ii, gu_src(w_gu, layer, g0, ii, 1), KN)
                    if b is not None:
                        mod_block(b, ii)
                    if f == 0 and g0 == 1:
                        load_bias()
                loop_pairs(f, sp, pair, straight=(3, 5, 1, 1)[f], first=1 if f == 0 else 0)

            def load_bias():
                sp.wait_ge(toep_out, 16)
                for r in range(ROWS):
                    for hh in range(NH):
                        src = bass.AP(toep_dram.tensor, (NDR * hh + 7 - r) * TOEP, [[1, GRID], [TOEP, ROWS], [1, GRID]])
                        dst = bias[GRID * (r % 2):GRID * (r % 2) + GRID, r // 2, hh, :].rearrange("p (a b) -> p a b", a=ROWS)
                        sp.dma_start(dst, src).then_inc(bias_in, 16)

            sp.dma_start(vec[0:8, 0, :], c_ctx.rearrange("(k p) -> k p", p=P)).then_inc(c_in, 16)
            sp.dma_start(vec[8:16, 0, :], c.rearrange("b (k p) -> (b k) p", p=P)).then_inc(c_in, 16)
            sp.dma_start(ident[:, :], consts[0]).then_inc(const_in, 16)
            mod_block(0, 0)
            mod_block(1, 0)
            sp.dma_start(x_tok[:, 0, :], x_prompt[0]).then_inc(x_in, 16)
            sp.dma_start(x_tok[:, 1:3, :], x_sample[0].rearrange("(a p) n -> p a n", p=P)).then_inc(x_in, 16)
            for layer in range(DEPTH):
                sp.dma_start(vec[0:NMOD * KD, 1 + layer, :], mod_b[layer].rearrange("(m p) -> m p", p=P)).then_inc(vec_in, 16)
            sp.dma_start(vec[0:DEPTH * 3 * KD, 3, :], norm_g.rearrange("l j (k p) -> (l j k) p", p=P)).then_inc(vec_in, 16)
            sp.dma_start(vec[0:KS, 4, :], v_g[0].rearrange("(k p) -> k p", p=P)).then_inc(vec_in, 16)
            for b in (MOD_SUM, *range(2, MOD_SUM)):
                v = mod_w[0].rearrange("(k p) n -> p k n", p=P)
                sp.dma_start(mfirst[:, b - 2, :, :], v[:, :, MB * b:MB * b + MB]).then_inc(mfirst_in[b - 2], 16)
            panel(0, 0, gu_src(w_gu1, 0, 0, 0, 0), KN)
            panel(1, 0, gu_src(w_gu1, 0, 0, 0, 1), KN)
            sp.wait_ge(zero_set, 1)
            sp.dma_start(toep[:, GRID - 16:GRID - 16 + BANDC], na_rpb[0].rearrange("h r c -> (h r) c")) \
                .then_inc(toep_in, 16)
            sp.dma_start(kc_na[:, :], ck_na[0, 0].rearrange("s h d -> s (h d)")).then_inc(tab_in, 16)
            sp.dma_start(vc_na[:, :], cv_na[0, 0].rearrange("s h d -> s (h d)")).then_inc(tab_in, 16)
            sp.dma_start(kc_g[:, :], ck_g[0, 0].rearrange("s h d -> s (h d)")).then_inc(tab_in, 16)
            sp.dma_start(vc_g[:, :], cv_g[0, 0].rearrange("s h d -> s (h d)")).then_inc(tab_in, 16)
            sp.dma_start(ropeT[:, :, :, :], rope.rearrange("c (a p) d -> p c a d", p=P)).then_inc(tab_in, 16)
            sp.dma_start(maskT[:, :], mask).then_inc(tab_in, 16)
            sp.dma_start(perm[:, :], consts[1]).then_inc(tab_in, 16)
            for n, g in enumerate((na_q_g, na_k_g, g_q_g, g_k_g)):
                sp.dma_start(gain[:, n, :], g[0].rearrange("(o d) -> o d", o=1).to_broadcast([P, HD])).then_inc(tab_in, 16)
            sp.wait_ge(toep_in, 16)
            sp.dma_start(toep_dram, toep[:, :]).then_inc(toep_out, 16)

            gate_up(0)
            down(Q_F[0] + 2 * GU, w_dn1[0], GU, MOD_AT[0] + MOD_GU, MOD_DN[0])
            for g in range(9):
                panel(Q_IN0 + g, 0, col_src(w_attn[0], QKV_ORDER[g]), KN)
                for b in range(MOD_IN):
                    if MOD_PSUM[b] == g:
                        mod_block(MOD_M + b, 0)
            down(Q_OUT0, w_o[0], KD // 2, MOD_M + MOD_IN, MOD_OUT)
            sp.wait_ge(gained, 7)
            sp.wait_ge(qkv_act, 3)
            sp.dma_start(o_nak[0, 0], k_na[:, 0, :, :]).then_inc(stored, 16)
            sp.dma_start(o_nav[0, 0].rearrange("s h d -> s (h d)"), v_na[:, 0, :]).then_inc(stored, 16)
            sp.dma_start(o_gk[0, 0], qk_g[:, 0, NH:NH + 2, :]).then_inc(stored, 16)
            sp.dma_start(o_gv[0, 0].rearrange("s h d -> s (h d)"), vg_[:, 0, :]).then_inc(stored, 16)
            gate_up(1)
            down(Q_F[1] + 2 * GU, w_dn2[0], GU, MOD_AT[1] + MOD_GU, MOD_DN[1])
            gate_up(2)
            down(Q_F[2] + 2 * GU, w_dn1[1], GU, MOD_AT[2] + MOD_GU, MOD_DN[2])
            for g in range(8):
                panel(Q_V + g, 0, col_src(w_sgu[0], 8 + g), KN)
                if 2 <= g < 2 + MOD_SG:
                    mod_block(MOD_V + g - 2, 0)
                if g == 1:
                    sp.wait_ge(pe_done, Q_V)
                    sp.dma_start(ws_row[:, :, :], w_s[0].rearrange("g t s -> t g s")).then_inc(ws_in, 16)
                    sp.dma_start(bsb[:, :, :], b_s[0].rearrange("(o g) t -> o g t", o=1).to_broadcast([P, NG, P])) \
                        .then_inc(ws_in, 16)
            for g in range(8):
                panel(Q_U + g, 0, col_src(w_sgu[0], g), KN)
            down(Q_OUT1, w_sgo[0], KS // 2)
            gate_up(3)
            down(Q_F[3] + 2 * GU, w_dn2[1], GU)
            for i in range(KD // 2):
                cols = slice(P * ORDER[2 * i], P * ORDER[2 * i] + 2 * P)
                sp.wait_ge(y_done, 2 * i + 2)
                sp.dma_start(y_p[0][:, cols], y_tok[:, 0, cols]).then_inc(stored, 16)
                sp.dma_start(y_s[0].rearrange("(a p) n -> p a n", p=P)[:, :, cols], y_tok[:, 1:3, cols]).then_inc(stored, 16)
            sp.wait_ge(stored, 16 * (4 + KD))

        @block.gpsimd
        def _(pool):
            nc.gpsimd.memset(ones[:, :], 1.0).then_inc(ones_set, 1)
            nc.gpsimd.memset(mhalf[:, :], -0.5).then_inc(ones_set, 1)
            nc.gpsimd.memset(toep[:, :], 0.0).then_inc(zero_set, 1)

            def norm(n):
                for k in range(1, 4):
                    pool.wait_ge(sq_done, KD * n + k + 1)
                    if k == 1:
                        if n:
                            pool.wait_ge(rb_done, n)
                        nc.gpsimd.tensor_tensor(sqsum[:, :], sq[:, 0, :], sq[:, 1, :], ALU.add).then_inc(acc_done, 1)
                    else:
                        pool.wait_ge(acc_done, 3 * n + k - 1)
                        nc.gpsimd.tensor_tensor(sqsum[:, :], sqsum[:, :], sq[:, k, :], ALU.add).then_inc(acc_done, 1)
                pool.wait_ge(ms_done, n + 1)
                nc.gpsimd.tensor_tensor(rs[:, :], ms[:, :], mhalf[:, 0:TT], ALU.pow).then_inc(rs_done, 1)

            pool.wait_ge(ones_set, 2)
            norm(0)
            pool.wait_ge(bias_in, 16 * ROWS * NH)
            pool.wait_ge(tab_in, 16 * 11)
            for qt in range(2):
                bv = bias[:, qt, :, :].rearrange("p h (r k) -> p (h r) k", k=GRID)
                nc.gpsimd.tensor_tensor(bv, bv, maskT[:, None, :].to_broadcast([P, NH * ROWS, GRID]), ALU.add) \
                    .then_inc(bias_done, 1)
            norm(1)
            pool.wait_ge(gain_done, 2)
            for g in range(QK_STEPS):
                dst, nh, gn = heads_of(g)
                w = TT * nh
                pool.wait_ge(hms_done, g + 1)
                nc.gpsimd.tensor_tensor(hrs[:, 0:w], hms[:, 0:w], mhalf[:, 0:w], ALU.pow).then_inc(hrs_done, 1)
                pool.wait_ge(qkv_dve, g + 1)
                nc.gpsimd.tensor_tensor(dst, dst, gain[:, gn, None, None, :].to_broadcast([P, TT, nh, HD]), ALU.mult) \
                    .then_inc(gained, 1)
            norm(2)
            norm(3)
            norm(4)
            pool.wait_ge(vms_done, 1)
            nc.gpsimd.tensor_tensor(rs[:, :], ms[:, :], mhalf[:, 0:TT], ALU.pow).then_inc(vrs_done, 1)
            norm(5)

        @block.scalar
        def _(act):
            steps = [0]

            def split(q0, i):
                if q0 >= Q_END:
                    return
                act.wait_ge(raw_in[q0 % 2], 16 * (q0 // 2 + 1 + i))
                if q0 >= 2:
                    act.wait_ge(pe_done, q0 + 2 * i - 1)
                nc.scalar.activation(w_hi[q0 % 2][:, :], raw[q0 % 2][:, :], ACT.Copy).then_inc(hi_done, 1)

            def squares(n, block=0):
                for k, m in enumerate(ORDER):
                    act.wait_ge(h_done, KD * n + k + 1)
                    if k == 1 and block:
                        act.wait_ge(msum_done, block - MOD_SUM)
                    if k >= 4:
                        act.wait_ge(acc_done, 3 * n + max(1, k - 4))
                    elif n:
                        act.wait_ge(stat_done, n)
                    nc.scalar.activation(sq[:, k % 4, :], h[:, m, :], ACT.Square).then_inc(sq_done, 1)

            def make_x(n, j):
                layer, seg = j
                base = (layer * NMOD + 3 * seg) * KD
                act.wait_ge(mvec, n + 1)
                for k in range(KD):
                    act.wait_ge(t_done, KD * n + k + 1)
                    for cond, cols in ((0, CTX), (1, LAT)):
                        last = nc.scalar.activation(tmp[:, k % 4, cols], tmp[:, k % 4, cols], ACT.Identity,
                                                    bias=modT[:, base + k, cond:cond + 1], scale=aT[:, k, cond:cond + 1])
                    last.then_inc(xm_done, 1)
                    act.wait_ge(xm_done, KD * n + k + 1)
                    nc.scalar.activation(x_hi[:, k, :], tmp[:, k % 4, :], ACT.Copy).then_inc(xh_done, 1)

            def ffn(f):
                q = Q_F[f]

                def pair(g0, i, b):
                    done = PAIRS[f] + g0 + i
                    if g0 == 0:
                        split(q + 2, 0)
                    act.wait_ge(pe_done, q + 2 * g0 + 1 + 2 * i)
                    if PAIRS[f] + g0:
                        act.wait_ge(actl_done, done)
                    nc.scalar.activation(tmp[:, 0:2, :], ps[:, 0:2, 0:T], ACT.Silu).then_inc(silu_done, 1)
                    if g0:
                        split(q + 2 * g0 + 2, i)
                    act.wait_ge(mul_done, done + 1)
                    nc.scalar.activation(act_hi[:, bass.ds(2 * g0 + 2 * i, 2), :], tmp[:, 0:2, :], ACT.Copy) \
                        .then_inc(acth_done, 1)
                    split(q + 2 * g0 + 3, i)
                loop_pairs(f, act, pair)

            def down(q0, n):
                steps_beside_blocks(act, 0, 0, min(n - 1, Q_END - 2 - q0), lambda j0, i, beside: split(q0 + j0 + 2, i))

            act.wait_ge(c_pe, 1)
            nc.scalar.activation(cT[:, :, :].rearrange("p k c -> p c k"),
                                 ps[:, 0, 0:16].rearrange("p (c k) -> p c k", c=2), ACT.Silu).then_inc(c_done, 1)
            squares(0)
            for a in range(MOD_FIRST // 2):
                if a == MOD_FIRST // 2 - 2:
                    split(0, 0)
                    split(1, 0)
                act.wait_ge(mod_pe, min(2 * a + 2, MOD_SUM))
                n = 512 if a < MOD_FIRST // 2 - 1 else MB
                nc.scalar.activation(mod_row[:, 512 * a:512 * a + n], ps[0:2, ROW_BANK[a], 0:n], ACT.Copy) \
                    .then_inc(row_done, 1)
            make_x(0, (0, 0))
            act.wait_ge(toep_out, 16)
            ffn(0)
            down(Q_F[0] + 2 * GU, GU)
            squares(1)
            split(Q_IN0 + 1, 0)
            make_x(1, (0, 1))
            for g, c in enumerate(QKV_ORDER):
                if g == 8:
                    nc.scalar.activation(rsum[:, 0:1], mhalf[:, 0:1], ACT.Exp)
                act.wait_ge(pe_done, Q_IN0 + g + 1)
                if c in (4, 5, 8):
                    for t in range(TT):
                        dst, cols = (v_na[:, t, 256 * (c - 4):256 * (c - 4) + 256], slice(0, 256)) if c < 8 \
                            else (vg_[:, t, :], slice(128, 256))
                        last = nc.scalar.activation(dst, ps[:, QBANK[g % 2][t], cols], ACT.Copy)
                    last.then_inc(qkv_act, 1)
                if g < QK_STEPS:
                    w = heads_of(g)[1] * HD
                    if g:
                        act.wait_ge(hms_sum, g)
                    for t in range(TT):
                        last = nc.scalar.activation(hsq_view(w)[:, t, :], ps[:, QBANK[g % 2][t], 0:w], ACT.Square)
                    last.then_inc(hsq_done, 1)
                if g < 8:
                    split(Q_IN0 + g + 2, 0)
            def put_qk(groups):
                for g in groups:
                    dst, n = tr_groups()[g]
                    act.wait_ge(tr_pe, g + 1)
                    nc.scalar.activation(dst, ps[:, TR_BANK[g % 5], 0:n], ACT.Copy).then_inc(tr_act, 1)

            put_qk(range(5))

            def softmax(b):
                n = NCTX if b % 3 == 0 else T
                act.wait_ge(nmax_done, b + 1)
                if b >= 4:
                    act.wait_ge(pT_pe, b - 3)
                nc.scalar.activation(prob[:, b % 4, 0:n], ps[:, b % 3, 0:n], ACT.Exp, bias=nmax[:, b % 4:b % 4 + 1],
                                     accum_out=rsum[:, b % 4:b % 4 + 1]).then_inc(exp_done, 1)

            def put_pT(b):
                hh, kind = divmod(b, 3)
                act.wait_ge(pT_pe, b + 1)
                if hh >= 2 and kind == 0:
                    act.wait_ge(o_pe, hh - 1)
                if kind == 0:
                    nc.scalar.activation(pT_ctx[:, hh % 2, :], ps[:, 3 + b % 3, 0:P], ACT.Copy).then_inc(pT_done, 1)
                else:
                    nc.scalar.activation(pT_lat[:, hh % 2, :, P * (kind - 1):P * kind],
                                         ps[:, 3 + b % 3, 0:T].rearrange("p (k q) -> p k q", k=3), ACT.Copy) \
                        .then_inc(pT_done, 1)

            def o_hi(pair):
                act.wait_ge(o_pe, 2 * pair + 2)
                nc.scalar.activation(x_hi[:, pair, :], ps[:, 6 + pair % 2, 0:T], ACT.Copy).then_inc(oh_done, 1)

            for b in range(3):
                softmax(b)
            put_qk([g for g in range(5, 13) if g not in TR_DVE])
            for b in range(3, 48 + 3):
                if b < 48:
                    softmax(b)
                put_pT(b - 3)
                if b >= 11 and (b - 11) % 6 == 0:
                    o_hi((b - 11) // 6)
            o_hi(7)
            split(Q_OUT0 + 1, 0)
            down(Q_OUT0, KD // 2)
            squares(2, MOD_AT[1])
            split(Q_F[1] + 1, 0)
            make_x(2, (0, 2))
            act.wait_ge(stored, 16 * 4)
            ffn(1)
            down(Q_F[1] + 2 * GU, GU)
            squares(3)
            split(Q_F[2] + 1, 0)
            make_x(3, (1, 0))
            ffn(2)
            down(Q_F[2] + 2 * GU, GU)
            squares(4)
            split(Q_V + 1, 0)
            make_x(4, (1, 1))
            for g in range(8):
                act.wait_ge(pe_done, Q_V + g + 1)
                for t in range(TT):
                    last = nc.scalar.activation(v_tok[:, t, 256 * g:256 * g + 256], ps[:, QBANK[g % 2][t], 0:256], ACT.Gelu)
                last.then_inc(gelu_v, 1)
                split(Q_V + g + 2, 0)
                act.wait_ge(gelu_v, g + 1)
                if g:
                    act.wait_ge(vss_done, g)
                for t in range(TT):
                    last = nc.scalar.activation(vsq[:, t, :], v_tok[:, t, 256 * g:256 * g + 256], ACT.Square,
                                                accum_out=vss[:, t, g:g + 1])
                last.then_inc(vss_done, 1)
                if g == 0:
                    for a in range(2):
                        act.wait_ge(ws_pe, a + 1)
                        nc.scalar.activation(wsT[:, 4 * a:4 * a + 4, :], ps[:, 4 + a, :].rearrange("p (g t) -> p g t", g=4),
                                             ACT.Copy).then_inc(wsT_done, 1)
            for g in range(8):
                done = UPAIR + g
                act.wait_ge(pe_done, Q_U + g + 1)
                act.wait_ge(actl_done, done)
                bk = 2 * (g % 2)
                nc.scalar.activation(tmp[:, 0:2, :], ps[:, bk:bk + 2, 0:T], ACT.Gelu).then_inc(silu_done, 1)
                split(Q_U + g + 2, 0)
                act.wait_ge(mul_done, done + 1)
                nc.scalar.activation(act_hi[:, 2 * g:2 * g + 2, :], tmp[:, 0:2, :], ACT.Copy).then_inc(acth_done, 1)
            down(Q_OUT1, KS // 2)
            squares(5)
            split(Q_F[3] + 1, 0)
            make_x(5, (1, 2))
            ffn(3)
            down(Q_F[3] + 2 * GU, GU)
            for k, m in enumerate(ORDER):
                act.wait_ge(yT_pe, k + 1)
                nc.scalar.activation(y_tok[:, :, P * m:P * m + P], ps[:, m, 0:T].rearrange("p (a n) -> p a n", a=TT), ACT.Copy) \
                    .then_inc(y_done, 1)

        @block.vector
        def _(dve):
            def link(ins):
                dve_steps[0] += 1
                ins.then_inc(dve_self, 1)
                dve.wait_ge(dve_self, dve_steps[0])

            def split(q0, i):
                if q0 >= Q_END:
                    return
                dve.wait_ge(hi_done, q0 + 2 * i + 1)
                nc.vector.tensor_tensor(w_lo[q0 % 2][:, :], raw[q0 % 2][:, :], w_hi[q0 % 2][:, :].bitcast(F32),
                                        ALU.subtract).then_inc(lo_done, 1)

            def mod_sum(b0, ii):
                m = b0 - MOD_SUM
                if b0 == MOD_SUM:
                    raw_block = mfirst[:, b0 - 2]
                    dve.wait_ge(mfirst_in[b0 - 2], 16)
                else:
                    raw_block = mraw[b0 % 2]
                    dve.wait_ge(mraw_in[b0 % 2], 16 * ((b0 - MOD_FIRST) // 2 + 2) + 8 * ii)
                if m >= 2:
                    dve.wait_ge(msum_done, m + ii - 1)
                for k in range(KD):
                    for cond in range(2):
                        acc = macc[:, b0 % 2, cond, :]
                        w, cc = raw_block[:, k, :], cT[:, k, cond:cond + 1]
                        if k == 0:
                            last = nc.vector.tensor_scalar(acc, w, cc, None, ALU.mult)
                        else:
                            dve.wait_ge(mchain, 15 * m + 15 * ii + 2 * k + cond - 1)
                            last = nc.vector.scalar_tensor_tensor(acc, w, cc, acc, ALU.mult, ALU.add)
                        if (k, cond) != (KD - 1, 1):
                            last.then_inc(mchain, 1)
                last.then_inc(macc_done, 1)

            def mod_out(b0, ii, n, src, wait):
                dve.wait_ge(*wait)
                nc.vector.tensor_tensor(modT[:, bass.ds(2 * b0 + 2 * ii, 2 * n), :], src.rearrange("p (a c) -> p a c", c=2),
                                        mbT[:, bass.ds(2 * b0 + 2 * ii, 2 * n), None].to_broadcast([P, 2 * n, 2]), ALU.add) \
                    .then_inc(mod_done, 1)

            def vectors(n, j):
                layer, seg = j
                base = (layer * NMOD + 3 * seg) * KD
                dve.wait_ge(mod_done, outs_until((base + 2 * KD) // 2))
                if n:
                    dve.wait_ge(xm_done, KD * n)
                nc.vector.scalar_tensor_tensor(
                    aT[:, :, :], modT[:, base + KD:base + 2 * KD, :], 1.0,
                    ngT[:, (layer * 3 + seg) * KD:(layer * 3 + seg + 1) * KD, None].to_broadcast([P, KD, 2]),
                    ALU.add, ALU.mult).then_inc(mvec, 1)

            def gate(n, j, w):
                layer, seg = j
                base = (layer * NMOD + 3 * seg + 2) * KD
                dve.wait_ge(mod_done, outs_until((base + KD) // 2))
                link(nc.vector.tensor_scalar(gT[:, :, :], modT[:, base:base + KD, :], w, None, ALU.mult))

            def rms(n, q=None):
                def half(a):
                    cols = slice(PW // 2 * a, PW // 2 * a + PW // 2)
                    return nc.vector.tensor_tensor(w_lo[q % 2][:, cols], raw[q % 2][:, cols],
                                                   w_hi[q % 2][:, cols].bitcast(F32), ALU.subtract)
                dve.wait_ge(stat_done, n + 1)
                nc.vector.tensor_scalar(ms[:, :], ps[:, 4, 0:TT], 1.0 / D, EPS, ALU.mult, ALU.add).then_inc(ms_done, 1)
                if q is not None:
                    dve.wait_ge(hi_done, q + 1)
                    half(0)
                dve.wait_ge(rs_done, n + 1)
                nc.vector.tensor_tensor(sqsum[:, :].rearrange("p (a q) -> p a q", a=TT),
                                        ident[:, None, :].to_broadcast([P, TT, P]),
                                        rs[:, :, None].to_broadcast([P, TT, P]), ALU.mult).then_inc(diag_done, 1)
                if q is not None:
                    half(1).then_inc(lo_done, 1)

            def make_x(n):
                dve.wait_ge(rb_done, n + 1)

                def t_of(k):
                    if k >= 4:
                        dve.wait_ge(xh_done, KD * n + k - 3)
                    nc.vector.tensor_tensor(tmp[:, k % 4, :], h[:, k, :], ps[:, 5, 0:T], ALU.mult).then_inc(t_done, 1)

                t_of(0)
                t_of(1)
                for k in range(KD):
                    dve.wait_ge(xh_done, KD * n + k + 1)
                    nc.vector.tensor_tensor(x_lo[:, k, :], tmp[:, k % 4, :], x_hi[:, k, :].bitcast(F32), ALU.subtract) \
                        .then_inc(x_done, 1)
                    if k + 2 < KD:
                        t_of(k + 2)

            def ffn(f):
                q = Q_F[f]

                def pair(g0, ii, b):
                    done = PAIRS[f] + g0 + ii
                    if b is not None:
                        mod_sum(b, ii)
                    split(q + 2 * g0 + 2, ii)
                    dve.wait_ge(pe_done, q + 2 * g0 + 2 + 2 * ii)
                    dve.wait_ge(silu_done, done + 1)
                    nc.vector.tensor_tensor(tmp[:, 0:2, :], ps[:, 2:4, 0:T], tmp[:, 0:2, :], ALU.mult).then_inc(mul_done, 1)
                    if b is not None:
                        mod_out(b, ii, 1, ps[:, 6 + b % 2, 0:4], (msum_done, b + ii - MOD_SUM + 1))
                    dve.wait_ge(acth_done, done + 1)
                    nc.vector.tensor_tensor(act_lo[:, bass.ds(2 * g0 + 2 * ii, 2), :], tmp[:, 0:2, :],
                                            act_hi[:, bass.ds(2 * g0 + 2 * ii, 2), :].bitcast(F32), ALU.subtract) \
                        .then_inc(actl_done, 1)
                    split(q + 2 * g0 + 3, ii)
                loop_pairs(f, dve, pair)

            def down(q0, n, idx, j, w, block=0, blocks=0):
                def step(j0, i, beside):
                    split(q0 + j0 + 2, i)
                    if beside:
                        mod_sum(block + j0, 2 * i)
                steps_beside_blocks(dve, 0, blocks, n - 2, step)
                gate(idx, j, w)
                for k, m in enumerate(ORDER):
                    dve.wait_ge(out_done, KD * idx + k + 1)
                    for cond, cols in ((0, CTX), (1, LAT)):
                        last = nc.vector.scalar_tensor_tensor(h[:, m, cols], ps[:, m, cols], gT[:, m, cond:cond + 1],
                                                              h[:, m, cols], ALU.mult, ALU.add)
                    last.then_inc(h_done, 1)
                    if k == 1:
                        split(q0 + n, 0)
                    if m == ORDER[-1] and blocks:
                        mod_out(block, 0, blocks, ps[:, m, SPARE:SPARE + 4 * blocks],
                                (msum_done, block + blocks - MOD_SUM))

            dve.wait_ge(vecT_pe, 1)
            for layer in range(DEPTH):
                nc.vector.tensor_copy(mbT[:, layer * 72:layer * 72 + 72], ps[:, 1, 128 * layer:128 * layer + 72])
            nc.vector.tensor_copy(ngT[:, :], ps[:, 1, 256:256 + 48])
            nc.vector.tensor_copy(vgT[:, :], ps[:, 1, 384:384 + KS]).then_inc(vecT_done, 1)
            dve.wait_ge(vecT_done, 1)
            for k, m in enumerate(ORDER):
                dve.wait_ge(xT_pe, k + 1)
                nc.vector.tensor_copy(h[:, m, :], ps[:, 2 + k % 4, 0:T]).then_inc(h_done, 1)
            rms(0)
            mod_sum(MOD_SUM, 0)
            split(0, 0)
            split(1, 0)
            dve.wait_ge(msum_done, 1)
            mod_out(0, 0, MOD_FIRST, ps[:, 2, 0:4 * MOD_FIRST], (rowT_pe, 1))
            vectors(0, (0, 0))
            make_x(0)
            ffn(0)
            dve.wait_ge(tab_in, 16 * 11)
            for n in (0, 2):
                nc.vector.tensor_scalar(gain[:, n, :], gain[:, n, :], HD ** -0.5, None, ALU.mult).then_inc(gain_done, 1)
            down(Q_F[0] + 2 * GU, GU, 0, (0, 0), 0.5, MOD_AT[0] + MOD_GU, MOD_DN[0])
            vectors(1, (0, 1))
            rms(1, Q_IN0 + 1)
            make_x(1)

            def rotate():
                rt = rot_view()
                for t in (1, 2):
                    xv = qk_g[:, t, :, :]
                    x5 = xv.rearrange("p h (a b d) -> p b h a d", a=2, b=2)
                    r5 = rt.rearrange("p h (a b d) -> p b h a d", a=2, b=2)
                    s5 = ropeT[:, 1, t - 1, :].rearrange("p (a b d) -> p b a d", a=2, b=2)
                    for part in range(2):
                        last = nc.vector.tensor_tensor(r5[:, part], x5[:, 1 - part],
                                                       s5[:, part, None].to_broadcast([P, NH + 2, 2, 16]), ALU.mult)
                    link(last)
                    link(nc.vector.tensor_tensor(xv, xv, ropeT[:, 0, t - 1, None, :].to_broadcast([P, NH + 2, HD]), ALU.mult))
                    link(nc.vector.tensor_tensor(xv, xv, rt, ALU.add))

            for g in range(8):
                if g < QK_STEPS:
                    dst, nh, _ = heads_of(g)
                    dve.wait_ge(hsq_done, g + 1)
                    nc.vector.tensor_reduce(hms[:, 0:TT * nh],
                                            hsq_view(nh * HD)[:, :, :].rearrange("p a (h d) -> p (a h) d", d=HD),
                                            AX.X, ALU.add).then_inc(hms_sum, 1)
                    dve.wait_ge(hms_sum, g + 1)
                    nc.vector.tensor_scalar(hms[:, 0:TT * nh], hms[:, 0:TT * nh], 1.0 / HD, EPS, ALU.mult, ALU.add) \
                        .then_inc(hms_done, 1)
                split(Q_IN0 + g + 2, 0)
                if g < QK_STEPS:
                    dve.wait_ge(hrs_done, g + 1)
                    for t in range(TT):
                        last = nc.vector.tensor_tensor(
                            dst[:, t], ps[:, QBANK[g % 2][t], 0:nh * HD].rearrange("p (h d) -> p h d", d=HD),
                            hrs[:, t * nh:(t + 1) * nh, None].to_broadcast([P, nh, HD]), ALU.mult)
                    last.then_inc(qkv_dve, 1)
                if g in MOD_STEPS:
                    mod_sum(MOD_M + MOD_STEPS.index(g), 0)
            dve.wait_ge(gained, QK_STEPS)
            rotate()
            dve.sem_inc(rope_done, 1)
            mod_out(MOD_M, 0, MOD_IN, ps[:, 4, 0:4 * MOD_IN], (msum_done, MOD_M + MOD_IN - MOD_SUM))

            def top(b):
                n = NCTX if b % 3 == 0 else T
                dve.wait_ge(s_pe, b + 1)
                if b >= 4:
                    dve.wait_ge(exp_done, b - 3)
                nc.vector.tensor_reduce(nmax[:, b % 4:b % 4 + 1], ps[:, b % 3, 0:n], AX.X, ALU.max, negate=True) \
                    .then_inc(nmax_done, 1)

            def normalise(b):
                n = NCTX if b % 3 == 0 else T
                dve.wait_ge(exp_done, b + 1)
                link(nc.vector.reciprocal(rinv[:, b % 4:b % 4 + 1], rsum[:, b % 4:b % 4 + 1]))
                nc.vector.tensor_scalar(prob[:, b % 4, 0:n], prob[:, b % 4, 0:n], rinv[:, b % 4:b % 4 + 1], None,
                                        ALU.mult).then_inc(prob_done, 1)

            def o_lo(pair):
                dve.wait_ge(oh_done, pair + 1)
                nc.vector.tensor_tensor(x_lo[:, pair, :], ps[:, 6 + pair % 2, 0:T], x_hi[:, pair, :].bitcast(F32),
                                        ALU.subtract).then_inc(ol_done, 1)

            for b in range(3):
                top(b)
            normalise(0)
            normalise(1)
            for g in TR_DVE:
                dst, n = tr_groups()[g]
                dve.wait_ge(tr_pe, g + 1)
                nc.vector.tensor_copy(dst, ps[:, TR_BANK[g % 5], 0:n]).then_inc(tr_dve, 1)
            for b in range(3, 48 + 1):
                if b < 48:
                    top(b)
                normalise(b - 1)
                if b >= 12 and (b - 12) % 6 == 0:
                    o_lo((b - 12) // 6)
            o_lo(7)
            split(Q_OUT0 + 1, 0)
            down(Q_OUT0, KD // 2, 1, (0, 1), 1.0, MOD_M + MOD_IN, MOD_OUT)
            vectors(2, (0, 2))
            rms(2, Q_F[1] + 1)
            make_x(2)
            ffn(1)
            down(Q_F[1] + 2 * GU, GU, 2, (0, 2), 0.5, MOD_AT[1] + MOD_GU, MOD_DN[1])
            vectors(3, (1, 0))
            rms(3, Q_F[2] + 1)
            make_x(3)
            ffn(2)
            down(Q_F[2] + 2 * GU, GU, 3, (1, 0), 0.5, MOD_AT[2] + MOD_GU, MOD_DN[2])
            vectors(4, (1, 1))
            rms(4, Q_V + 1)
            make_x(4)
            for g in range(8):
                split(Q_V + g + 2, 0)
                if g < MOD_SG:
                    mod_sum(MOD_V + g, 0)
            dve.wait_ge(vss_done, 8)
            link(nc.vector.tensor_reduce(ms[:, :], vss[:, :, :], AX.X, ALU.add))
            nc.vector.tensor_scalar(ms[:, :], ms[:, :], 1.0 / SW, EPS, ALU.mult, ALU.add).then_inc(vms_done, 1)
            dve.wait_ge(vrs_done, 1)
            dve.wait_ge(wsT_done, 2)
            for t in range(TT):
                last = nc.vector.tensor_scalar(wsn[:, t, :, :], wsT[:, :, :], rs[:, t:t + 1], None, ALU.mult)
            last.then_inc(wsn_done, 1)
            mod_out(MOD_V, 0, MOD_SG, ps[:, 4, 0:4 * MOD_SG], (msum_done, MOD_V + MOD_SG - MOD_SUM))
            dve.wait_ge(ws_in, 32)
            for d in range(KS):
                dve.wait_ge(sv_pe, d + 1)
                nc.vector.scalar_tensor_tensor(svb[:, d, :].rearrange("p (a t) -> p a t", a=TT),
                                               ps[:, (d + 2) % 8, 0:T].rearrange("p (a t) -> p a t", a=TT), vgT[:, d:d + 1],
                                               bsb[:, d // 2, None, :].to_broadcast([P, TT, P]), ALU.mult, ALU.add) \
                    .then_inc(sv_done, 1)
            dve.wait_ge(sv_done, KS)
            for g in range(8):
                split(Q_U + g + 2, 0)
                done = UPAIR + g
                dve.wait_ge(silu_done, done + 1)
                nc.vector.tensor_tensor(tmp[:, 0:2, :], tmp[:, 0:2, :], svb[:, 2 * g:2 * g + 2, :], ALU.mult) \
                    .then_inc(mul_done, 1)
                dve.wait_ge(acth_done, done + 1)
                nc.vector.tensor_tensor(act_lo[:, 2 * g:2 * g + 2, :], tmp[:, 0:2, :],
                                        act_hi[:, 2 * g:2 * g + 2, :].bitcast(F32), ALU.subtract).then_inc(actl_done, 1)
            down(Q_OUT1, KS // 2, 4, (1, 1), 1.0)
            vectors(5, (1, 2))
            rms(5, Q_F[3] + 1)
            make_x(5)
            ffn(3)
            down(Q_F[3] + 2 * GU, GU, 5, (1, 2), 0.5)

        @block.tensor
        def _(pe):
            mm = nc.tensor.matmul

            def three(out, w, cols, xs, start, stop):
                mm(out, w[0][:, cols], xs[0], start=start, stop=False)
                mm(out, w[0][:, cols], xs[1], start=False, stop=False)
                return mm(out, w[1][:, cols], xs[0], start=False, stop=stop)

            def slot(q0):
                return w_hi[q0 % 2], w_lo[q0 % 2]

            def mod_rows(b):
                if b < 2:
                    pe.wait_ge(mraw_in[b], 16)
                else:
                    pe.wait_ge(mfirst_in[b - 2], 16)
                w = mraw[b] if b < 2 else mfirst[:, b - 2]
                for k in range(KD):
                    last = mm(ps[0:2, ROW_BANK[b // 2], MB * (b % 2):MB * (b % 2) + MB], cT[:, k, :], w[:, k, :],
                              start=(k == 0), stop=(k == KD - 1))
                last.then_inc(mod_pe, 1)

            def row_transposes(a):
                pe.wait_ge(row_done, a + 1)
                for c in range(4 * a, min(4 * a + 4, 2 * MOD_SUM)):
                    last = nc.tensor.transpose(ps[:, 2, 2 * c:2 * c + 2], mod_row[:, P * c:P * c + P], ident[0:2, 0:2])
                if a == MOD_FIRST // 2 - 1:
                    last.then_inc(rowT_pe, 1)

            def mod_psum(b0, ii, bank, col, alone):
                pe.wait_ge(macc_done, b0 + ii - MOD_SUM + 1)
                for a in range(2):
                    for cond in range(2):
                        last = mm(ps[:, bank, bass.ds(col + 2 * a + cond, 1)], macc[:, b0 % 2, cond, P * a:P * a + P],
                                  ones[:, 0:1], start=alone, stop=True, skip_group_check=not alone)
                last.then_inc(msum_done, 1)

            def feature_major(q0, bank, order, parts="hi lo"):
                hi, lo = slot(q0)
                for a, k in order:
                    out, cols = ps[:, bank + a, 0:T], slice(256 * k + P * a, 256 * k + P * a + P)
                    if "hi" in parts:
                        mm(out, hi[:, cols], x_hi[:, k, :], start=(k == 0), stop=False)
                        mm(out, lo[:, cols], x_hi[:, k, :], start=False, stop=False)
                    if "lo" in parts:
                        last = mm(out, hi[:, cols], x_lo[:, k, :], start=False, stop=(k == KD - 1))
                return last if "lo" in parts else None

            def token_major(q0, banks, order, parts="hi lo"):
                hi, lo = slot(q0)
                for t, k in order:
                    tok, cols = slice(P * t, P * t + P), slice(256 * k, 256 * k + 256)
                    out = ps[:, banks[t], 0:256]
                    if "hi" in parts:
                        mm(out, x_hi[:, k, tok], hi[:, cols], start=(k == 0), stop=False)
                        mm(out, x_hi[:, k, tok], lo[:, cols], start=False, stop=False)
                    if "lo" in parts:
                        last = mm(out, x_lo[:, k, tok], hi[:, cols], start=False, stop=(k == KD - 1))
                return last if "lo" in parts else None

            def project(make, q0, i, bank):
                pe.wait_ge(lo_done, q0 + 2 * i + 1)
                tiles = 2 if make is feature_major else TT
                make(q0, bank, [(a, k) for a in range(tiles) for k in range(KD)]).then_inc(pe_done, 1)

            def project_first(make, q, banks, n):
                tiles = range(2 if make is feature_major else TT)
                shared = 3
                pe.wait_ge(lo_done, q + 2)
                for k in range(shared):
                    if k == 0:
                        pe.wait_ge(xh_done, KD * n + 1)
                        for a in range(2):
                            make(q + a, banks[a], [(t, k) for t in tiles], "hi")
                    pe.wait_ge(x_done, KD * n + k + 1)
                    for a in range(2):
                        make(q + a, banks[a], [(t, k) for t in tiles], "hi lo" if k else "lo")
                for k in range(shared, KD):
                    pe.wait_ge(x_done, KD * n + k + 1)
                    last = make(q, banks[0], [(t, k) for t in tiles])
                last.then_inc(pe_done, 1)
                make(q + 1, banks[1], [(t, k) for t in tiles for k in range(shared, KD)]).then_inc(pe_done, 1)

            def norm(n):
                norm_sums(n)
                norm_spread(n)

            def norm_sums(n):
                for k in (4, 5, None, 6, 7):
                    if k is None:
                        pe.wait_ge(acc_done, 3 * n + 3)
                    else:
                        pe.wait_ge(sq_done, KD * n + k + 1)
                    for t in range(TT):
                        part = sqsum[:, P * t:P * t + P] if k is None else sq[:, k % 4, P * t:P * t + P]
                        last = mm(ps[:, 4, t:t + 1], part, ones[:, 0:1], start=(k == 4 and t == 0), stop=(k == 7),
                                  skip_group_check=True)
                last.then_inc(stat_done, 1)

            def norm_spread(n):
                pe.wait_ge(diag_done, n + 1)
                mm(ps[:, 5, 0:T], ones[:, :], sqsum[:, :], start=True, stop=True).then_inc(rb_done, 1)

            def ffn(f, n):
                q = Q_F[f]

                def pair(g0, ii, b):
                    done = PAIRS[f] + g0 + ii
                    if g0 == 0:
                        project_first(feature_major, q, (0, 2), n)
                        return
                    pe.wait_ge(silu_done, done)
                    project(feature_major, q + 2 * g0, ii, 0)
                    pe.wait_ge(mul_done, done)
                    project(feature_major, q + 2 * g0 + 1, ii, 2)
                    if b is not None:
                        pe.wait_ge(mod_done, outs_until(b - 1) + ii)
                        mod_psum(b, ii, 6 + b % 2, 0, True)
                loop_pairs(f, pe, pair)

            def down(q0, n, idx, hi, lo, ready, block=0, blocks=0):
                def panel(j0, i, beside=False, first=False, final=False):
                    pe.wait_ge(lo_done, q0 + j0 + 2 * i + 1)
                    if final:
                        ready(-1)
                    for k, m in enumerate(ORDER):
                        if first:
                            ready(k)
                        for c in range(2):
                            kk = slice(2 * j0 + c, 2 * j0 + c + 1) if isinstance(i, int) else bass.ds(2 * j0 + c + 4 * i, 1)
                            last = three(ps[:, m, 0:T], slot(q0 + j0), slice(1024 * c + P * m, 1024 * c + P * m + P),
                                         (hi[:, kk, :], lo[:, kk, :]), first and c == 0, final and c == 1)
                        if final:
                            last.then_inc(out_done, 1)
                        if k == 3 and beside:
                            mod_psum(block + j0 - 2, 2 * i, ORDER[-1], SPARE + 4 * (j0 - 2) + 8 * i, False)
                    if not final:
                        last.then_inc(pe_done, 1)
                    else:
                        pe.wait_ge(out_done, KD * idx + KD)
                        pe.sem_inc(pe_done, 1)

                panel(0, 0, first=True)
                panel(1, 0)
                steps_beside_blocks(pe, 2, min(blocks, n - 3), n - 1, panel)
                panel(n - 1, 0, beside=blocks == n - 2, final=True)

            def ready_ffn(f):
                def waits(k):
                    if k == 0:
                        pe.wait_ge(actl_done, PAIRS[f] + GU - 1)
                    elif k == 2 and f < 3:
                        pe.wait_ge(mod_done, outs_until(MOD_AT[f] + MOD_GU))
                    elif k == 4:
                        pe.wait_ge(mul_done, PAIRS[f] + GU)
                    elif k == -1:
                        pe.wait_ge(actl_done, PAIRS[f] + GU)
                return waits

            pe.wait_ge(const_in, 16)
            pe.wait_ge(c_in, 32)
            nc.tensor.transpose(ps[:, 0, 0:16], vec[0:16, 0, :], ident[0:16, 0:16]).then_inc(c_pe, 1)
            pe.wait_ge(c_done, 1)
            mod_rows(0)
            mod_rows(1)
            pe.wait_ge(vec_in, 16 * 4)
            for r, n in ((1, 72), (2, 72), (3, 48), (4, KS)):
                last = nc.tensor.transpose(ps[:, 1, 128 * (r - 1):128 * (r - 1) + n], vec[0:n, r, :], ident[0:n, 0:n])
            last.then_inc(vecT_pe, 1)
            pe.wait_ge(x_in, 32)
            for k, m in enumerate(ORDER):
                if k >= 4:
                    pe.wait_ge(h_done, k - 3)
                for t in range(TT):
                    last = nc.tensor.transpose(ps[:, 2 + k % 4, P * t:P * t + P], x_tok[:, t, P * m:P * m + P], ident[:, :])
                last.then_inc(xT_pe, 1)
            mod_rows(2)
            pe.wait_ge(ones_set, 2)
            pe.wait_ge(h_done, KD)
            norm_sums(0)
            mod_rows(3)
            norm_spread(0)
            pe.wait_ge(vecT_done, 1)
            mod_rows(4)
            mod_rows(5)
            for a in range(3):
                row_transposes(a)
            mod_rows(6)
            mod_psum(MOD_SUM, 0, 2, 4 * MOD_SUM, True)
            row_transposes(3)
            ffn(0, 0)
            down(Q_F[0] + 2 * GU, GU, 0, act_hi, act_lo, ready_ffn(0), MOD_AT[0] + MOD_GU, MOD_DN[0])
            norm(1)

            project_first(token_major, Q_IN0, QBANK, 1)
            for g in range(2, 9):
                pe.wait_ge(qkv_dve, g - 1)
                if g == 6:
                    pe.wait_ge(qkv_act, 1)
                project(token_major, Q_IN0 + g, 0, QBANK[g % 2])
                for b in range(MOD_IN - 1):
                    if MOD_PSUM[b] == g:
                        mod_psum(MOD_M + b, 0, 4, 4 * b, True)
            pe.wait_ge(gained, 4)
            groups = (sum([[(q_na, n, None), (k_na, n, kc_na[:, P * n:P * n + P])] for n in range(4)], [])
                      + [(qk_g, n, None) for n in range(4)] + [(qk_g, 4, kc_g[:, :])])

            def scores(b):
                hh, kind = divmod(b, 3)
                if hh < NH:
                    base, qT, kT = HD * (hh % 2), qT_na[:, hh // 2, :], kT_na[:, hh // 2, :]
                else:
                    g = hh - NH
                    base, qT, kT = HD * (g // 4), qT_g[:, g % 4, :], kT_g[:, :]
                rows = slice(base, base + HD)
                if b >= 3:
                    pe.wait_ge(exp_done, b - 2)
                if kind == 0:
                    mm(ps[:, b % 3, 0:P], qT[rows, 0:P], kT[rows, 0:P], start=True, stop=True).then_inc(s_pe, 1)
                else:
                    na = hh < NH
                    last = mm(ps[:, b % 3, 0:T], qT[rows, P * kind:P * kind + P], kT[rows, P:P + T], start=True, stop=not na)
                    if na:
                        last = mm(ps[:, b % 3, 0:NLAT], perm[:, :], bias[:, kind - 1, hh, :], start=False, stop=True)
                    last.then_inc(s_pe, 1)

            for g, (src, n, cache) in enumerate(groups):
                bank = TR_BANK[g % 5]
                if g == 1:
                    pe.wait_ge(tab_in, 16 * 11)
                    pe.wait_ge(qkv_act, 2)
                elif g == 4:
                    pe.wait_ge(qkv_act, 3)
                    pe.wait_ge(tr_act, 2)
                    pe.wait_ge(bias_done, 2)
                    for b in range(3):
                        scores(b)
                    mod_psum(MOD_M + MOD_IN - 1, 0, 4, 4 * (MOD_IN - 1), True)
                    pe.wait_ge(mod_done, outs_until(MOD_M + MOD_IN))
                elif g == 8:
                    pe.wait_ge(rope_done, 1)
                if g >= 5:
                    pe.wait_ge(tr_act, g - 4)
                for t in range(TT):
                    last = nc.tensor.transpose(ps[:, bank, P * t:P * t + P],
                                               src[:, t, 2 * n:2 * n + 2, :].rearrange("p h d -> p (h d)"), ident[:, :])
                if cache is not None:
                    last = nc.tensor.transpose(ps[:, bank, T:T + P], cache, ident[:, :])
                last.then_inc(tr_pe, 1)
            pe.wait_ge(tr_act, 11)
            pe.wait_ge(tr_dve, 2)

            def p_transposes(b):
                pe.wait_ge(prob_done, b + 1)
                if b >= 3:
                    pe.wait_ge(pT_done, b - 2)
                for k in range(1 if b % 3 == 0 else 3):
                    last = nc.tensor.transpose(ps[:, 3 + b % 3, P * k:P * k + P], prob[:, b % 4, P * k:P * k + P], ident[:, :])
                last.then_inc(pT_pe, 1)

            def values(hh):
                pe.wait_ge(pT_done, 3 * hh + 3)
                pair, half = divmod(hh, 2)
                if hh >= 4 and half == 0:
                    pe.wait_ge(ol_done, pair - 1)
                out = ps[HD * half:HD * half + HD, 6 + pair % 2, :]
                if hh < NH:
                    v, cache, cols = v_na, vc_na, slice(HD * hh, HD * hh + HD)
                else:
                    kv = (hh - NH) // 4
                    v, cache, cols = vg_, vc_g, slice(HD * kv, HD * kv + HD)
                mm(out[:, 0:P], v[:, 0, cols], pT_ctx[:, hh % 2, :], start=True, stop=True)
                mm(out[:, P:T], v[:, 1, cols], pT_lat[:, hh % 2, 0, :], start=True, stop=False)
                mm(out[:, P:T], v[:, 2, cols], pT_lat[:, hh % 2, 1, :], start=False, stop=False)
                mm(out[:, P:T], cache[:, cols], pT_lat[:, hh % 2, 2, :], start=False, stop=True).then_inc(o_pe, 1)

            for b in range(3, 48 + 5):
                if b < 48:
                    scores(b)
                if b < 51:
                    p_transposes(b - 3)
                if b >= 7 and b % 3 == 1:
                    values((b - 7) // 3)

            def ready_attn(k):
                if k == 0:
                    pe.wait_ge(pT_done, 48)
                elif k == 2:
                    pe.wait_ge(ol_done, 8)

            down(Q_OUT0, KD // 2, 1, x_hi, x_lo, ready_attn, MOD_M + MOD_IN, MOD_OUT)
            norm(2)
            ffn(1, 2)
            down(Q_F[1] + 2 * GU, GU, 2, act_hi, act_lo, ready_ffn(1), MOD_AT[1] + MOD_GU, MOD_DN[1])
            norm(3)
            ffn(2, 3)
            down(Q_F[2] + 2 * GU, GU, 3, act_hi, act_lo, ready_ffn(2), MOD_AT[2] + MOD_GU, MOD_DN[2])
            norm(4)
            project_first(token_major, Q_V, QBANK, 4)
            pe.wait_ge(ws_in, 32)
            for a in range(2):
                for n in range(4):
                    last = nc.tensor.transpose(ps[:, 4 + a, P * n:P * n + P], ws_row[:, 4 * a + n, :], ident[:, :])
                last.then_inc(ws_pe, 1)
            for g in range(2, 8):
                pe.wait_ge(gelu_v, g - 1)
                project(token_major, Q_V + g, 0, QBANK[g % 2])
                if g < 2 + MOD_SG:
                    if g == 2:
                        pe.wait_ge(wsT_done, 1)
                    mod_psum(MOD_V + g - 2, 0, 4, 4 * (g - 2), True)
            pe.wait_ge(gelu_v, 7)
            project(feature_major, Q_U, 0, 0)
            pe.wait_ge(gelu_v, 8)
            pe.wait_ge(wsn_done, 1)
            for d in range(KS):
                if d == 2:
                    pe.wait_ge(mod_done, outs_until(DEPTH * NMB))
                if d == 6:
                    pe.wait_ge(silu_done, UPAIR + 1)
                if d >= 8:
                    pe.wait_ge(sv_done, d - 7)
                for t in range(TT):
                    last = mm(ps[:, (d + 2) % 8, P * t:P * t + P], v_tok[:, t, P * d:P * d + P], wsn[:, t, d // 2, :],
                              start=True, stop=True)
                last.then_inc(sv_pe, 1)
            for g in range(1, 8):
                if g == 1:
                    pe.wait_ge(sv_done, 10)
                else:
                    if g == 2:
                        pe.wait_ge(sv_done, KS)
                    pe.wait_ge(silu_done, UPAIR + g - 1)
                project(feature_major, Q_U + g, 0, 2 * (g % 2))

            def ready_sgu(k):
                if k == 0:
                    pe.wait_ge(actl_done, UPAIR + 7)
                elif k == 4:
                    pe.wait_ge(silu_done, UPAIR + 8)
                elif k == -1:
                    pe.wait_ge(actl_done, UPAIR + 8)

            down(Q_OUT1, KS // 2, 4, act_hi, act_lo, ready_sgu)
            norm(5)
            ffn(3, 5)
            down(Q_F[3] + 2 * GU, GU, 5, act_hi, act_lo, ready_ffn(3))
            for k, m in enumerate(ORDER):
                pe.wait_ge(h_done, KD * 6 + k + 1)
                for t in range(TT):
                    last = nc.tensor.transpose(ps[:, m, P * t:P * t + P], h[:, m, P * t:P * t + P], ident[:, :])
                last.then_inc(yT_pe, 1)


PAIRS = (0, GU, 2 * GU, 3 * GU + 8)
UPAIR = 3 * GU
QKV_ORDER = (0, 1, 2, 3, 8, 6, 7, 4, 5)
QK_STEPS = 7
MOD_STEPS = (3, 4, 6, 7)
MOD_PSUM = (5, 6, 8, 8)
QBANK = ((0, 1, 2), (3, 6, 7))
TR_BANK = (5, 3, 6, 7, 4)
TR_DVE = (9, 11)
ROW_BANK = (6, 7, 0, 1)

_NAMES = ['x_prompt', 'x_sample', 'cache_na_k', 'cache_na_v', 'cache_gqa_k', 'cache_gqa_v', 'c', 'c_ctx', 'norm_g', 'mod_w',
          'mod_b', 'ffn1_w_gu', 'ffn1_w_down', 'ffn2_w_gu', 'ffn2_w_down', 'attn_w_in', 'attn_w_out', 'na_q_g', 'na_k_g',
          'na_rpb', 'gqa_q_g', 'gqa_k_g', 'sgu_w_in', 'sgu_v_g', 'sgu_w_s', 'sgu_b_s', 'sgu_w_out']
_OUTS = [(1, NCTX, D), (1, NLAT, D), (1, 1, NCTX, NH, HD), (1, 1, NCTX, NH, HD), (1, 1, NCTX, 2, HD), (1, 1, NCTX, 2, HD)]


def shape_constants():
    t = np.arange(NLAT)
    half = HD // 2
    freqs = 10000.0 ** (-np.arange(0, half, 2, dtype=np.float64) / half)
    rope = np.zeros((2, NLAT, HD), np.float32)
    for a, pos in enumerate((t // GRID, t % GRID)):
        ang = pos[:, None] * freqs[None, :]
        for b in range(2):
            at = slice(a * half + b * 16, a * half + b * 16 + 16)
            rope[0, :, at] = np.cos(ang)
            rope[1, :, at] = np.sin(ang) * (1 if b else -1)
    j = np.arange(P)
    qcol = (GRID - 1 - j % GRID)[:, None]
    start = np.clip(qcol - 8, 0, GRID - 16)
    kcol = np.arange(GRID)[None, :]
    mask = np.where((kcol >= start) & (kcol < start + 16), 0.0, -1e30).astype(np.float32)
    consts = np.zeros((2, P, P), np.float32)
    consts[0, j, j] = 1.0
    consts[1, j, GRID * (j // GRID) + GRID - 1 - j % GRID] = 1.0
    return rope, mask, consts


def kernel(**inputs):
    import concourse.bacc as bacc
    from concourse.bass_utils import run_bass_kernel_spmd as run

    nc = bacc.Bacc("TRN2", target_bir_lowering=False, num_devices=1)
    arrays = {n: np.ascontiguousarray(inputs[n]) for n in _NAMES}
    for n, a in zip(("rope_table", "window_mask", "consts"), shape_constants()):
        arrays[n] = a
    ins = [nc.dram_tensor(n, a.shape, F32, kind="ExternalInput").ap() for n, a in arrays.items()]
    outs = [nc.dram_tensor(f"out_{i}", s, F32, kind="ExternalOutput").ap() for i, s in enumerate(_OUTS)]
    toep = nc.dram_tensor("toep_scratch", (NH * NDR, TOEP), F32, kind="Internal").ap()
    build(nc, ins, outs, toep)
    r = run(nc, [arrays], core_ids=[0])
    return tuple(r.results[0][f"out_{i}"] for i in range(len(_OUTS)))
```
